# Optimizing a Trainium2 kernel written in Bass

```python
import jax
import jax.numpy as jnp
from jax import lax
import numpy as np

D_MODEL = 2048
BATCH = 1
SEQ = 256
DEPTH = 2

GRID_W = 64
CTX_LEN = 256
N_GROUPS = 4
GROUP_W = D_MODEL // N_GROUPS
HEAD_DIM = 128
EPS = 1e-6

GLA_HEADS = GROUP_W // HEAD_DIM
GLA_DV = HEAD_DIM
GLA_DK = HEAD_DIM // 2
GLA_RANK = 16
GLA_TAU = 16.0
GLA_CHUNK = 32

GDN_HEADS = GROUP_W // HEAD_DIM
GDN_DK = HEAD_DIM
GDN_DV = HEAD_DIM
GDN_CONV = 5
GDN_CHUNK = 64

SC_WIDTH = GROUP_W
SC_CONV = 3

SWA_HEADS = GROUP_W // HEAD_DIM
SWA_KV_HEADS = 2
SWA_WINDOW = 128
SWA_BLOCK = 128
ROPE_BASE = 10000.0

IN_SPLITS = (
    ("gla_q", GLA_HEADS * GLA_DK), ("gla_k", GLA_HEADS * GLA_DK), ("gla_v", GLA_HEADS * GLA_DV),
    ("gla_lr_f", GLA_RANK), ("gla_lr_b", GLA_RANK), ("gla_gate", GROUP_W),
    ("gdn_q", GDN_HEADS * GDN_DK), ("gdn_k", GDN_HEADS * GDN_DK), ("gdn_v", GDN_HEADS * GDN_DV),
    ("gdn_a_f", GDN_HEADS), ("gdn_a_b", GDN_HEADS), ("gdn_b_f", GDN_HEADS), ("gdn_b_b", GDN_HEADS),
    ("gdn_gate", GROUP_W),
    ("sc_b", SC_WIDTH), ("sc_c", SC_WIDTH), ("sc_h", SC_WIDTH), ("sc_gate", GROUP_W),
    ("swa_q", SWA_HEADS * HEAD_DIM), ("swa_k", SWA_KV_HEADS * HEAD_DIM), ("swa_v", SWA_KV_HEADS * HEAD_DIM),
    ("swa_gate", GROUP_W),
)
IN_WIDTH = sum(size for _, size in IN_SPLITS)

kernel_name = "hybrid_parallel_group_flow_block"

def split_cols(u):
    out, off = {}, 0
    for name, size in IN_SPLITS:
        out[name] = u[..., off:off + size]
        off += size
    return out

def rmsnorm(x, g):
    xf = x.astype(jnp.float32)
    y = xf * lax.rsqrt(jnp.mean(xf * xf, axis=-1, keepdims=True) + EPS)
    return (y * g.astype(jnp.float32)).astype(x.dtype)

def l2norm(x):
    xf = x.astype(jnp.float32)
    return (xf * lax.rsqrt(jnp.sum(xf * xf, axis=-1, keepdims=True) + EPS)).astype(x.dtype)

def to_heads(t, n):
    b, l, _ = t.shape
    return t.reshape(b, l, n, -1).transpose(0, 2, 1, 3)

def from_heads(t):
    b, h, l, d = t.shape
    return t.transpose(0, 2, 1, 3).reshape(b, l, h * d)

def flip_seq(t):
    return jnp.flip(t, axis=2)

def dwconv(x, w):
    width = w.shape[0]
    return lax.conv_general_dilated(
        x, w[:, None, :].astype(x.dtype), window_strides=(1,),
        padding=[(width // 2, width // 2)], dimension_numbers=("NWC", "WIO", "NWC"),
        feature_group_count=x.shape[-1])

def axial_rope_tables(seq_len):
    rows = seq_len // GRID_W
    row = jnp.repeat(jnp.arange(rows, dtype=jnp.float32), GRID_W)
    col = jnp.tile(jnp.arange(GRID_W, dtype=jnp.float32), rows)
    axis_dim = HEAD_DIM // 2
    inv_freq = ROPE_BASE ** (-jnp.arange(0, axis_dim, 2, dtype=jnp.float32) / axis_dim)
    ang_r = row[:, None] * inv_freq
    ang_c = col[:, None] * inv_freq
    return (jnp.cos(ang_r), jnp.sin(ang_r), jnp.cos(ang_c), jnp.sin(ang_c))

def rotate_half(x, cos, sin):
    x1, x2 = jnp.split(x, 2, axis=-1)
    cos = cos[None, :, None, :].astype(x.dtype)
    sin = sin[None, :, None, :].astype(x.dtype)
    return jnp.concatenate([x1 * cos - x2 * sin, x2 * cos + x1 * sin], axis=-1)

def rope2d(x, tabs):
    cos_r, sin_r, cos_c, sin_c = tabs
    half = HEAD_DIM // 2
    return jnp.concatenate([rotate_half(x[..., :half], cos_r, sin_r),
                            rotate_half(x[..., half:], cos_c, sin_c)], axis=-1)

def gla_scan(q, k, v, log_a, s0):
    out_dtype = v.dtype
    q, k, v, log_a = (t.astype(jnp.float32) for t in (q, k, v, log_a))
    b, h, l, dk = q.shape
    dv = v.shape[-1]
    n = l // GLA_CHUNK
    q, k, log_a = (t.reshape(b, h, n, GLA_CHUNK, dk) for t in (q, k, log_a))
    v = v.reshape(b, h, n, GLA_CHUNK, dv)
    cum = jnp.cumsum(log_a, axis=3)
    incl = jnp.tril(jnp.ones((GLA_CHUNK, GLA_CHUNK), bool))[:, :, None]
    pair = jnp.exp(jnp.where(incl, cum[..., :, None, :] - cum[..., None, :, :], -jnp.inf))
    attn = jnp.einsum("bhnid,bhnjd,bhnijd->bhnij", q, k, pair)
    o_intra = jnp.einsum("bhnij,bhnjv->bhniv", attn, v)
    q_in = q * jnp.exp(cum)
    k_out = k * jnp.exp(cum[..., -1:, :] - cum)
    chunk_decay = jnp.exp(cum[..., -1, :])

    def step(state, inp):
        q_n, k_n, v_n, d_n = inp
        o = jnp.einsum("bhcd,bhdv->bhcv", q_n, state)
        state = state * d_n[..., None] + jnp.einsum("bhcd,bhcv->bhdv", k_n, v_n)
        return state, o

    xs = tuple(jnp.moveaxis(t, 2, 0) for t in (q_in, k_out, v, chunk_decay))
    state, o_inter = lax.scan(step, s0, xs)
    o = jnp.moveaxis(o_inter, 0, 2) + o_intra
    return o.reshape(b, h, l, dv).astype(out_dtype), state

def gla_mixer(s, sc, w_decay, b_decay, norm_w, with_ctx):
    def prep(seg):
        q = to_heads(seg["gla_q"], GLA_HEADS) * (GLA_DK ** -0.5)
        k = to_heads(seg["gla_k"], GLA_HEADS)
        v = to_heads(seg["gla_v"], GLA_HEADS)

        def log_decay(lr, d):
            z = (lr @ w_decay[d] + b_decay[d]).astype(jnp.float32)
            return to_heads(jax.nn.log_sigmoid(z) / GLA_TAU, GLA_HEADS)
        return q, k, v, log_decay(seg["gla_lr_f"], 0), log_decay(seg["gla_lr_b"], 1)

    q, k, v, la_f, la_b = prep(s)
    qc, kc, vc, lc_f, lc_b = prep(sc)
    s0 = jnp.zeros((q.shape[0], GLA_HEADS, GLA_DK, GLA_DV), jnp.float32)
    oc_f, st_f = gla_scan(qc, kc, vc, lc_f, s0)
    oc_b, st_b = gla_scan(flip_seq(qc), flip_seq(kc), flip_seq(vc), flip_seq(lc_b), s0)
    o_f, _ = gla_scan(q, k, v, la_f, st_f)
    o_b, _ = gla_scan(flip_seq(q), flip_seq(k), flip_seq(v), flip_seq(la_b), st_b)

    def finish(o, seg):
        return from_heads(rmsnorm(o, norm_w)) * jax.nn.silu(seg["gla_gate"])
    y = finish(o_f + flip_seq(o_b), s)
    yc = finish(oc_f + flip_seq(oc_b), sc) if with_ctx else None
    return y, yc

def gdn_scan(q, k, v, g, beta, s0):
    out_dtype = v.dtype
    q, k, v, g, beta = (t.astype(jnp.float32) for t in (q, k, v, g, beta))
    b, h, l, dk = q.shape
    dv = v.shape[-1]
    n = l // GDN_CHUNK
    q, k = (t.reshape(b, h, n, GDN_CHUNK, dk) for t in (q, k))
    v = v.reshape(b, h, n, GDN_CHUNK, dv)
    g, beta = (t.reshape(b, h, n, GDN_CHUNK) for t in (g, beta))
    cum = jnp.cumsum(g, axis=-1)
    incl = jnp.tril(jnp.ones((GDN_CHUNK, GDN_CHUNK), bool))
    strict = jnp.tril(jnp.ones((GDN_CHUNK, GDN_CHUNK), bool), -1)
    decay = jnp.exp(jnp.where(incl, cum[..., :, None] - cum[..., None, :], -jnp.inf))
    k_beta = k * beta[..., None]
    lower = jnp.where(strict, jnp.einsum("bhnid,bhnjd->bhnij", k_beta, k) * decay, 0.0)
    a_mat = lower + jnp.eye(GDN_CHUNK, dtype=jnp.float32)
    u = lax.linalg.triangular_solve(a_mat, v * beta[..., None], left_side=True, lower=True)
    w = lax.linalg.triangular_solve(a_mat, k_beta * jnp.exp(cum)[..., None], left_side=True, lower=True)
    attn = jnp.einsum("bhnid,bhnjd->bhnij", q, k) * decay
    q_in = q * jnp.exp(cum)[..., None]
    k_out = k * jnp.exp(cum[..., -1:] - cum)[..., None]
    chunk_decay = jnp.exp(cum[..., -1])

    def step(state, inp):
        u_n, w_n, q_n, k_n, a_n, d_n = inp
        v_new = u_n - jnp.einsum("bhcd,bhdv->bhcv", w_n, state)
        o = jnp.einsum("bhcd,bhdv->bhcv", q_n, state) + jnp.einsum("bhij,bhjv->bhiv", a_n, v_new)
        state = state * d_n[..., None, None] + jnp.einsum("bhcd,bhcv->bhdv", k_n, v_new)
        return state, o

    xs = tuple(jnp.moveaxis(t, 2, 0) for t in (u, w, q_in, k_out, attn, chunk_decay))
    state, o = lax.scan(step, s0, xs)
    o = jnp.moveaxis(o, 0, 2).reshape(b, h, l, dv)
    return o.astype(out_dtype), state

def gdn_mixer(s, sc, conv_w, a_log, dt_bias, norm_w, with_ctx):
    qd = GDN_HEADS * GDN_DK

    def prep(seg):
        qkv = jnp.concatenate([seg["gdn_q"], seg["gdn_k"], seg["gdn_v"]], axis=-1)
        qkv = jax.nn.silu(dwconv(qkv, conv_w))
        q = l2norm(to_heads(qkv[..., :qd], GDN_HEADS)) * (GDN_DK ** -0.5)
        k = l2norm(to_heads(qkv[..., qd:2 * qd], GDN_HEADS))
        v = to_heads(qkv[..., 2 * qd:], GDN_HEADS)

        def gates(a_in, b_in, d):
            a32 = a_in.astype(jnp.float32)
            g = -jnp.exp(a_log[d].astype(jnp.float32)) * jax.nn.softplus(a32 + dt_bias[d].astype(jnp.float32))
            return g.transpose(0, 2, 1), jax.nn.sigmoid(b_in.astype(jnp.float32)).transpose(0, 2, 1)
        g_f, b_f = gates(seg["gdn_a_f"], seg["gdn_b_f"], 0)
        g_b, b_b = gates(seg["gdn_a_b"], seg["gdn_b_b"], 1)
        return q, k, v, g_f, b_f, g_b, b_b

    q, k, v, g_f, b_f, g_b, b_b = prep(s)
    qc, kc, vc, gc_f, bc_f, gc_b, bc_b = prep(sc)
    s0 = jnp.zeros((q.shape[0], GDN_HEADS, GDN_DK, GDN_DV), jnp.float32)
    oc_f, st_f = gdn_scan(qc, kc, vc, gc_f, bc_f, s0)
    oc_b, st_b = gdn_scan(flip_seq(qc), flip_seq(kc), flip_seq(vc), flip_seq(gc_b), flip_seq(bc_b), s0)
    o_f, _ = gdn_scan(q, k, v, g_f, b_f, st_f)
    o_b, _ = gdn_scan(flip_seq(q), flip_seq(k), flip_seq(v), flip_seq(g_b), flip_seq(b_b), st_b)

    def finish(o, seg):
        return from_heads(rmsnorm(o, norm_w)) * jax.nn.silu(seg["gdn_gate"])
    y = finish(o_f + flip_seq(o_b), s)
    yc = finish(oc_f + flip_seq(oc_b), sc) if with_ctx else None
    return y, yc

def shortconv_branch(seg, conv_w):
    return seg["sc_b"] * dwconv(seg["sc_c"] * seg["sc_h"], conv_w) * jax.nn.silu(seg["sc_gate"])

def swa_latent(q, k, v, kc, vc, sink):
    b, l, hq, d = q.shape
    hkv = k.shape[2]
    grp = hq // hkv
    blk = SWA_BLOCK
    nb = l // blk
    lc = kc.shape[1]
    qb = q.reshape(b, nb, blk, hkv, grp, d)

    def band(t):
        tp = jnp.pad(t, ((0, 0), (blk, blk), (0, 0), (0, 0))).reshape(b, nb + 2, blk, hkv, d)
        return jnp.concatenate([tp[:, :-2], tp[:, 1:-1], tp[:, 2:]], axis=2)
    kb, vb = band(k), band(v)
    qpos = jnp.arange(l).reshape(nb, blk)
    kpos = qpos[:, :1] - blk + jnp.arange(3 * blk)[None, :]
    valid = ((jnp.abs(qpos[:, :, None] - kpos[:, None, :]) <= SWA_WINDOW)
             & (kpos[:, None, :] >= 0) & (kpos[:, None, :] < l))
    scale = HEAD_DIM ** -0.5
    s_loc = jnp.einsum("bnqhgd,bnkhd->bnhgqk", qb, kb).astype(jnp.float32) * scale
    s_loc = jnp.where(valid[None, :, None, None], s_loc, -jnp.inf)
    s_ctx = jnp.einsum("bnqhgd,bchd->bnhgqc", qb, kc).astype(jnp.float32) * scale
    s_sink = jnp.broadcast_to(sink.astype(jnp.float32).reshape(hkv, grp)[None, None, :, :, None, None],
                              s_loc.shape[:-1] + (1,))
    p = jax.nn.softmax(jnp.concatenate([s_loc, s_ctx, s_sink], axis=-1), axis=-1).astype(v.dtype)
    o = (jnp.einsum("bnhgqk,bnkhd->bnqhgd", p[..., :3 * blk], vb)
         + jnp.einsum("bnhgqc,bchd->bnqhgd", p[..., 3 * blk:3 * blk + lc], vc))
    return o.reshape(b, l, hq * d)

def ctx_attention(qc, kc, vc, sink):
    b, lc, hq, d = qc.shape
    hkv = kc.shape[2]
    grp = hq // hkv
    qg = qc.reshape(b, lc, hkv, grp, d)
    s = jnp.einsum("bqhgd,bkhd->bhgqk", qg, kc).astype(jnp.float32) * (HEAD_DIM ** -0.5)
    s_sink = jnp.broadcast_to(sink.astype(jnp.float32).reshape(hkv, grp)[None, :, :, None, None],
                              s.shape[:-1] + (1,))
    p = jax.nn.softmax(jnp.concatenate([s, s_sink], axis=-1), axis=-1)[..., :lc].astype(vc.dtype)
    return jnp.einsum("bhgqk,bkhd->bqhgd", p, vc).reshape(b, lc, hq * d)

def swa_mixer(s, sc, sink, rope, with_ctx):
    def qkv(seg):
        b, l, _ = seg["swa_q"].shape
        return (seg["swa_q"].reshape(b, l, SWA_HEADS, HEAD_DIM),
                seg["swa_k"].reshape(b, l, SWA_KV_HEADS, HEAD_DIM),
                seg["swa_v"].reshape(b, l, SWA_KV_HEADS, HEAD_DIM))
    q, k, v = qkv(s)
    qc, kc, vc = qkv(sc)
    q, k = rope2d(q, rope), rope2d(k, rope)
    y = swa_latent(q, k, v, kc, vc, sink) * jax.nn.silu(s["swa_gate"])
    yc = ctx_attention(qc, kc, vc, sink) * jax.nn.silu(sc["swa_gate"]) if with_ctx else None
    return y, yc

def setup_inputs(seed: int = 0) -> dict:
    key = jax.random.key(seed)
    ks = jax.random.split(key, 24)
    D = D_MODEL

    def nrm(k, shape, scale):
        return jax.random.normal(k, shape, jnp.float32) * scale

    dt = jnp.exp(jax.random.uniform(ks[14], (DEPTH, 2, GDN_HEADS), jnp.float32,
                                    np.log(1e-3), np.log(1e-1)))
    return {
        "x": nrm(ks[0], (BATCH, SEQ, D), 1.0),
        "c": nrm(ks[1], (BATCH, D), 1.0),
        "ctx": nrm(ks[2], (BATCH, CTX_LEN, D), 1.0),
        "c_ctx": nrm(ks[3], (D,), 1.0),
        "ada_w": nrm(ks[4], (DEPTH, D, 3 * D), 0.5 * D ** -0.5),
        "ada_b": nrm(ks[5], (DEPTH, 3 * D), 0.02),
        "norm_pre": 1.0 + nrm(ks[6], (DEPTH, D), 0.05),
        "norm_post": 1.0 + nrm(ks[7], (DEPTH, D), 0.05),
        "w_in": nrm(ks[8], (DEPTH, D, IN_WIDTH), D ** -0.5),
        "w_out": nrm(ks[9], (DEPTH, D, D), D ** -0.5),
        "gla_w_decay": nrm(ks[10], (DEPTH, 2, GLA_RANK, GLA_HEADS * GLA_DK), GLA_RANK ** -0.5),
        "gla_b_decay": 1.0 + nrm(ks[11], (DEPTH, 2, GLA_HEADS * GLA_DK), 0.5),
        "gla_norm": 1.0 + nrm(ks[12], (DEPTH, GLA_DV), 0.05),
        "gdn_conv": nrm(ks[13], (DEPTH, GDN_CONV, 3 * GDN_HEADS * GDN_DK), GDN_CONV ** -0.5),
        "gdn_a_log": jnp.log(jax.random.uniform(ks[15], (DEPTH, 2, GDN_HEADS), jnp.float32, 1.0, 16.0)),
        "gdn_dt_bias": dt + jnp.log(-jnp.expm1(-dt)),
        "gdn_norm": 1.0 + nrm(ks[16], (DEPTH, GDN_DV), 0.05),
        "sc_conv": nrm(ks[17], (DEPTH, SC_CONV, SC_WIDTH), SC_CONV ** -0.5),
        "swa_sink": nrm(ks[18], (DEPTH, SWA_HEADS), 0.5),
    }

def reference(x, c, ctx, c_ctx, ada_w, ada_b, norm_pre, norm_post, w_in, w_out,
              gla_w_decay, gla_b_decay, gla_norm, gdn_conv, gdn_a_log, gdn_dt_bias, gdn_norm,
              sc_conv, swa_sink):
    rope = axial_rope_tables(x.shape[1])
    h, hc = x, ctx
    for layer in range(DEPTH):
        with_ctx = layer < DEPTH - 1
        shift, scale, gate = jnp.split(jax.nn.silu(c) @ ada_w[layer] + ada_b[layer], 3, axis=-1)
        shift_c, scale_c, gate_c = jnp.split(jax.nn.silu(c_ctx) @ ada_w[layer] + ada_b[layer], 3, axis=-1)
        n = rmsnorm(h, norm_pre[layer]) * (1.0 + scale[:, None]) + shift[:, None]
        nc = rmsnorm(hc, norm_pre[layer]) * (1.0 + scale_c) + shift_c
        s = split_cols(n @ w_in[layer])
        sc = split_cols(nc @ w_in[layer])

        ya, yca = gla_mixer(s, sc, gla_w_decay[layer], gla_b_decay[layer], gla_norm[layer], with_ctx)
        yb, ycb = gdn_mixer(s, sc, gdn_conv[layer], gdn_a_log[layer], gdn_dt_bias[layer], gdn_norm[layer], with_ctx)
        yc_ = shortconv_branch(s, sc_conv[layer])
        yd, ycd = swa_mixer(s, sc, swa_sink[layer], rope, with_ctx)

        y = jnp.concatenate([ya, yb, yc_, yd], axis=-1) @ w_out[layer]
        h = h + gate[:, None] * rmsnorm(y, norm_post[layer])
        if with_ctx:
            ycc = shortconv_branch(sc, sc_conv[layer])
            yctx = jnp.concatenate([yca, ycb, ycc, ycd], axis=-1) @ w_out[layer]
            hc = hc + gate_c * rmsnorm(yctx, norm_post[layer])
    return h


_drawn_inputs = setup_inputs


def setup_inputs(seed=0):
    import zlib

    import numpy as np

    out = dict(_drawn_inputs(seed))
    spreads = {}
    factors = {'gla_norm': 5.155, 'gdn_a_log': 2.839, 'gdn_norm': 4.845, 'swa_sink': 8.0}
    for name, (base, spread) in spreads.items():
        noise = np.random.default_rng([zlib.crc32(name.encode()), seed]).standard_normal(out[name].shape)
        drawn = base * np.exp(spread * noise) if base else spread * noise
        out[name] = jnp.asarray(drawn.astype(out[name].dtype))
    for name, factor in factors.items():
        out[name] = (out[name] * factor).astype(out[name].dtype)
    return out
```

```python
import numpy as np
import concourse.bass as bass
from concourse import mybir
from contextlib import ExitStack

D = 2048
SEQ = 256
CTX = 256
TOK = SEQ + CTX
DEPTH = 2
KT = D // 128
HD = 128
CH = 128
NC = TOK // CH
EPS = 1e-6
GRID_W = 64
ROPE_BASE = 10000.0
NEG = -1e30

GLA_QKV, GLA_LR, GLA_GATE = 0, 1024, 1056
GDN_QKV, GDN_AB, GDN_GATE = 1568, 3104, 3120
SC_ALL = 3632
SWA_QKV, SWA_GATE = 5680, 6704
IN_WIDTH = 7216
NLR, NAB = 32, 16

T_A, T_B = 0, 12
Y_GLA, Y_SWA, Y_GDN, Y_SC = 20, 24, 28, 32
NTILES = 36
Y_ORDER = [Y_GLA + i for i in range(4)] + [Y_GDN + i for i in range(4)] + \
          [Y_SC + i for i in range(4)] + [Y_SWA + i for i in range(4)]
RING = 4

C_IDENT, C_ONES, C_PERM = 0, 128, 256
C_CUMF, C_CUMB, C_TAILF, C_TAILB = 384, 512, 640, 768
C_LO = 896
C_UP = C_LO + 7 * 128
C_COS = C_UP + 7 * 128
C_SIN = C_COS + SEQ
C_MASK = C_SIN + SEQ
C_SEG = C_MASK + 2 * SEQ
C_EPS = C_SEG + TOK
C_ZERO = C_EPS + 1
C_ONE = C_EPS + 2
CW = C_EPS + 3

P_ADAB, P_NPRE, P_NPOST = 0, 48, 64
P_GLAB, P_GLAN = 80, 84
P_CONV, P_GDNN = 85, 145
P_SCW, P_ALOG, P_DT, P_SINK = 146, 158, 166, 174
PL = 178
P_C = DEPTH * PL
PW = P_C + 2 * KT


def constants():
    c = np.zeros((128, CW), np.float32)
    p = np.arange(128)[:, None]
    f = np.arange(128)[None, :]
    c[:, C_IDENT:C_IDENT + 128] = p == f
    c[:, C_ONES:C_ONES + 128] = 1.0
    swap = (f // 64) * 64 + (f % 64 + 32) % 64
    c[:, C_PERM:C_PERM + 128] = p == swap
    c[:, C_CUMF:C_CUMF + 128] = p <= f
    c[:, C_CUMB:C_CUMB + 128] = p >= f
    c[:, C_TAILF:C_TAILF + 128] = p > f
    c[:, C_TAILB:C_TAILB + 128] = p < f
    for lv in range(7):
        lo = (p >> (lv + 1) == f >> (lv + 1)) & ((p >> lv & 1) == 1) & ((f >> lv & 1) == 0)
        c[:, C_LO + 128 * lv:C_LO + 128 * lv + 128] = lo
        c[:, C_UP + 128 * lv:C_UP + 128 * lv + 128] = lo.T
    t = np.arange(SEQ)
    inv = ROPE_BASE ** (-np.arange(0, 64, 2, dtype=np.float64) / 64)
    for half, pos in ((0, t // GRID_W), (1, t % GRID_W)):
        ang = inv[:, None] * pos[None, :]
        for q, sign in ((0, -1.0), (1, 1.0)):
            r = half * 64 + q * 32
            c[r:r + 32, C_COS:C_COS + SEQ] = np.cos(ang)
            c[r:r + 32, C_SIN:C_SIN + SEQ] = sign * np.sin(ang)
    for b in range(2):
        far = np.abs(128 * b + p - t[None, :]) > 128
        c[:, C_MASK + b * SEQ:C_MASK + (b + 1) * SEQ] = np.where(far, NEG, 0.0)
    c[:, C_SEG:C_SEG + TOK] = (np.arange(TOK) % CH != 0)
    c[:, C_EPS] = EPS
    c[:, C_ONE] = 1.0
    return c


def parameters(i):
    def chan(a):
        return np.ascontiguousarray(np.asarray(a, np.float32).reshape(-1, 128).T)

    def rep(a):
        a = np.asarray(a, np.float32).reshape(1, -1)
        return np.repeat(a, 128, axis=0)
    cols = []
    for l in range(DEPTH):
        cols += [chan(i["ada_b"][l]), chan(i["norm_pre"][l]), chan(i["norm_post"][l]),
                 chan(i["gla_b_decay"][l]), chan(i["gla_norm"][l]),
                 np.asarray(i["gdn_conv"][l]).reshape(5, 12, 128).transpose(2, 1, 0).reshape(128, 60),
                 chan(i["gdn_norm"][l]),
                 np.asarray(i["sc_conv"][l]).reshape(3, 4, 128).transpose(2, 1, 0).reshape(128, 12),
                 rep(i["gdn_a_log"][l]), rep(i["gdn_dt_bias"][l]), rep(i["swa_sink"][l])]
    cc = np.stack([np.asarray(i["c_ctx"]).reshape(KT, 128), np.asarray(i["c"]).reshape(KT, 128)], 0)
    cols.append(cc.transpose(2, 1, 0).reshape(128, 2 * KT))
    return np.ascontiguousarray(np.concatenate(cols, axis=1))


class Order:

    def __init__(self, eng, sem):
        self.eng, self.sem, self.base, self.k, self.n, self.i = eng, sem, 0, 0, 0, 0

    def round(self, i, n):
        self.i, self.n, self.k = i, n, 0

    def done(self, ins):
        ins.then_inc(self.sem, 1)
        self.k += 1
        return self.k

    def wait(self, k=None):
        self.eng.wait_ge(self.sem, self.i * self.n + (self.base + (self.k if k is None else k)))

    def straight(self):
        self.base += self.k
        self.i = self.n = self.k = 0

    def close(self, rounds):
        assert self.k == self.n, f"{self.k} steps in a round, {self.n} declared"
        self.base += rounds * self.n
        self.i = self.n = self.k = 0


def build(nc, x_d, ctx_d, ada_d, win_d, wout_d, wdec_d, par_d, con_d, out_d):
    f32 = mybir.dt.float32
    ALU = mybir.AluOpType
    ACT = mybir.ActivationFunctionType
    AX = mybir.AxisListType.X
    es = ExitStack()
    with es:
        def sb(name, shape):
            return es.enter_context(nc.sbuf_tensor(name, shape, f32))

        sems = {}

        def sem(name):
            if name not in sems:
                sems[name] = es.enter_context(nc.semaphore(name))
            return sems[name]

        con = sb("con", [128, CW])
        par = sb("par", [128, PW])
        N = sb("N", [128, KT, TOK])
        act = sb("act", [128, NTILES, TOK])
        ring = sb("ring", [128, RING, KT, 128])
        wdec = sb("wdec", [NLR, 2, 256])
        wab = act[:, Y_SC, 0:KT * NAB].rearrange("p (k n) -> p k n", n=NAB)
        wlr = act[:, Y_SC + 1, 0:KT * NLR].rearrange("p (k n) -> p k n", n=NLR)
        lrT = act[0:NLR, Y_SC + 3, :]
        wdp = act[0:NLR, Y_SC + 2, 0:256].rearrange("r (d n) -> r d n", d=2)
        SC = sb("SC", [128, 24, TOK])
        ab = act[:, Y_SC + 2, 256:256 + NC * NAB].rearrange("p (c k) -> p c k", k=NAB)
        st = SC[:, 6, 0:256].rearrange("p (d v) -> p d v", d=2)
        vn = SC[:, 6, 256:512].rearrange("p (d v) -> p d v", d=2)
        rr = SC[:, 7, 0:256].rearrange("p (d v) -> p d v", d=2)
        cs = sb("cs", [128, KT, 2])
        cst = sb("cst", [128, KT, 2])
        ada = sb("ada", [128, DEPTH, 48, 2])
        modA = sb("modA", [128, DEPTH, KT, 2])
        modG = sb("modG", [128, DEPTH, KT, 2])
        gz = sb("gz", [128, NC, 2, 4])
        gt = sb("gt", [128, NC, 2, 4])
        expA = sb("expA", [128, 2, 4])
        g = sb("g", [128, 4, 2, NC])
        beta = sb("beta", [128, 4, 2, NC])
        eg = sb("eg", [128, 2, 3, 4, NC])
        rn = sb("rn", [128, 2, NC])
        rq = sb("rq", [128, NC])
        ks = sb("ks", [128, 4, 2, NC])
        tot = sb("tot", [128, 2, NC])
        gs = sb("gs", [128, 3, 2, NC])
        gd = sb("gd", [128, 2, NC])
        sm = sb("sm", [128, 6, 8])
        ps = [es.enter_context(nc.psum_tensor(f"bank{i}", [128, 512], f32)) for i in range(8)]
        h_d = nc.dram_tensor("h_spill", (128, KT * TOK), f32, kind="Internal").ap()

        ident = con[:, C_IDENT:C_IDENT + 128]
        ones = con[:, C_ONES:C_ONES + 128]
        one1 = con[:, C_ONE:C_ONE + 1]
        eps = con[:, C_EPS:C_EPS + 1]
        CUM = (C_CUMF, C_CUMB)
        TAIL = (C_TAILF, C_TAILB)

        def cm(at):
            return con[:, at:at + 128]

        def over(a, n=NC):
            return a.unsqueeze(1).to_broadcast([128, n, a.shape[1]])

        def along(a, m=128):
            return a.unsqueeze(2).to_broadcast([128, a.shape[1], m])

        def chunks(a):
            return a.rearrange("p (c t) -> p c t", t=128)

        def P(l, at, n=1):
            return par[:, l * PL + at:l * PL + at + n]

        def bank_wait(pe, n0, i, tb, tt):
            pe.wait_ge(sem(f"bank{(n0 + tt) % 2}_free"), i * (tb // 2) + (n0 + tt) // 2)

        def out_wait(eng, n0, i, tb, tt):
            eng.wait_ge(sem(f"bank{(n0 + tt) % 2}_full"), i * (tb // 2) + ((n0 + tt) // 2 + 1))

        segs = {}
        seq = []
        wt0, n0 = 0, 16
        for l in range(DEPTH):
            for name, dram, col, tiles in (
                    [("ada0", ada_d[0], 0, 48), ] if l == 0 else []) + [
                    ("gdn", win_d[l], GDN_QKV, 12), ("gdng", win_d[l], GDN_GATE, 4),
                    ("small", None, 0, 2),
                    ("p2", None, 0, 16), ("p3", win_d[l], SWA_QKV, 8), ("p4", win_d[l], SC_ALL, 16),
                    ("out", wout_d[l], 0, 16)] + ([("ada1", ada_d[1], 0, 48)] if l == 0 else []):
                segs[(l, name)] = (wt0, n0)
                if name == "p2":
                    seq += [(win_d[l], GLA_QKV, 8), (win_d[l], GLA_GATE, 4), (win_d[l], SWA_GATE, 4)]
                elif name != "small":
                    seq.append((dram, col, tiles))
                if name != "small":
                    wt0 += tiles
                n0 += tiles
        segs["end"] = (wt0, n0)

        block = es.enter_context(nc.Block())

        @block.sync
        def _(sp):
            sp.dma_start(con[:, :], con_d).then_inc(sem("con_in"), 16)
            sp.dma_start(par[:, :], par_d).then_inc(sem("par_in"), 16)
            xin = act[:, 0:16, :].rearrange("p a t -> p (a t)").rearrange("p (b d) -> p b d", b=4)
            sp.dma_start(xin[:, 0:2, :], ctx_d.rearrange("(b p) d -> p b d", p=128)).then_inc(sem("x_in"), 16)
            sp.dma_start(xin[:, 2:4, :], x_d.rearrange("(b p) d -> p b d", p=128)).then_inc(sem("x_in"), 16)
            sp.wait_ge(sem("wdec_zero"), 1)

            def weights(dram, col, tiles, base):
                with sp.Fori(0, tiles // RING) as i:
                    for s in range(RING):
                        sp.wait_ge(sem(f"slot{s}_free"), i + (base // RING + 1))
                        src = dram[:, bass.ds(i * (RING * 128) + (col + s * 128), 128)]
                        sp.dma_start(ring[:, s, :, :], src.rearrange("(k p) n -> p k n", p=128))\
                            .then_inc(sem(f"slot{s}_full"), 16)

            base = 0
            it = iter(seq)

            def nxt(count):
                nonlocal base
                for _ in range(count):
                    dram, col, tiles = next(it)
                    weights(dram, col, tiles, base)
                    base += tiles

            for l in range(DEPTH):
                sp.wait_ge(sem("yo_used"), l)
                sp.dma_start(wab, win_d[l][:, GDN_AB:GDN_AB + NAB].rearrange("(k p) n -> p k n", p=128))\
                    .then_inc(sem("small_in"), 16)
                sp.dma_start(wlr, win_d[l][:, GLA_LR:GLA_LR + NLR].rearrange("(k p) n -> p k n", p=128))\
                    .then_inc(sem("small_in"), 16)
                if l:
                    sp.wait_ge(sem("gla_stat"), 2 * l)
                for d in range(2):
                    sp.dma_start(wdec[16 * d:16 * d + 16, d, :], wdec_d[l, d]).then_inc(sem("wdec_in"), 16)
                if l == 0:
                    nxt(1)
                sp.wait_ge(sem("h_ready"), l + 1)
                sp.dma_start(h_d, N[:, :, :].rearrange("p k t -> p (k t)")).then_inc(sem("h_saved"), 16)
                nxt(2 + 3 + 1 + 1)
                sp.wait_ge(sem("norm_used"), l + 1)
                sp.wait_ge(sem("h_saved"), 16 * (l + 1))
                sp.dma_start(N[:, :, :].rearrange("p k t -> p (k t)"), h_d).then_inc(sem("h_back"), 16)
                nxt(2 if l == 0 else 1)
            for b in range(2):
                sp.wait_ge(sem("out_staged"), 4 * b + 4)
                sp.dma_start(out_d[b * 128:(b + 1) * 128, :],
                             act[:, 4 * b:4 * b + 4, :].rearrange("p a t -> p (a t)")).then_inc(sem("out_sent"), 16)
            sp.wait_ge(sem("out_sent"), 32)

        @block.tensor
        def _(pe):
            def mm(out, a, b, start=True, stop=True):
                return nc.tensor.matmul(out, a, b, start=start, stop=stop, skip_group_check=True)

            def tp(out, a):
                return nc.tensor.transpose(out, a, ident[0:a.shape[0], 0:a.shape[0]])

            class Fill:

                def __init__(self, l, name, tb, i, lo, rhs=None, off=0):
                    self.wt0, self.n0 = segs[(l, name)]
                    self.n0 += off
                    self.wt0 += off
                    self.tb, self.i, self.lo, self.at = tb, i, lo, 0
                    self.rhs = rhs or (lambda k: N[:, k, lo:])

                def __call__(self, steps):
                    for _ in range(steps):
                        if self.at == self.tb * KT:
                            return
                        tt, k = divmod(self.at, KT)
                        s = tt % RING
                        if k == 0:
                            pe.wait_ge(sem(f"slot{s}_full"),
                                       self.i * (16 * self.tb // RING) + 16 * ((self.wt0 + tt) // RING + 1))
                            bank_wait(pe, self.n0, self.i, self.tb, tt)
                        r = self.rhs(k)
                        b = (self.n0 + tt) % 2
                        last = mm(ps[b][:, 0:r.shape[-1]], ring[:, s, k, :], r, k == 0, k == KT - 1)
                        if k == KT - 1:
                            last.then_inc(sem(f"bank{b}_full"), 1)
                            pe.wait_ge(sem(f"bank{b}_full"),
                                       self.i * (self.tb // 2) + ((self.n0 + tt) // 2 + 1))
                            pe.sem_inc(sem(f"slot{s}_free"), 1)
                        self.at += 1

                def rest(self):
                    self(self.tb * KT - self.at)

            def project(l, name, tiles, tb=RING, lo=0, rhs=None, off=0):
                with pe.Fori(0, tiles // tb) as i:
                    Fill(l, name, tb, i, lo, rhs, off).rest()

            for s in range(RING):
                pe.sem_inc(sem(f"slot{s}_free"), 1)
            pe.wait_ge(sem("con_in"), 16)
            pe.wait_ge(sem("x_in"), 32)
            xin = act[:, 0:16, :].rearrange("p a t -> p (a t)").rearrange("p (b d) -> p b d", b=4)
            for k in range(KT):
                bank_wait(pe, 0, 0, KT, k)
                for b in range(4):
                    last = tp(ps[k % 2][:, b * 128:(b + 1) * 128], xin[:, b, k * 128:(k + 1) * 128])
                last.then_inc(sem(f"bank{k % 2}_full"), 1)
            pe.wait_ge(sem("cs_ready"), 1)
            project(0, "ada0", 48, rhs=lambda k: cs[:, k, :])

            def channel_sum(t, width0):
                pe.wait_ge(sem("sumsq_ready"), t + 1)
                mm(ps[2][:, width0:], ones, SC[:, 0, width0:]).then_inc(sem("chansum_done"), 1)

            def gdn(i, t, fill):
                pe.wait_ge(sem("gdn_rg"), t + 1)
                for d in range(2):
                    last = mm(ps[5 + d][:, :], cm(TAIL[d]), SC[:, 18 + d, :])
                last.then_inc(sem("gdn_D"), 1)
                fill(6)
                pe.wait_ge(sem("gdn_x"), t + 1)
                for j in range(3):
                    for c in range(NC):
                        last = tp(ps[2 + j][:, c * 128:(c + 1) * 128], SC[:, j, c * 128:(c + 1) * 128])
                last.then_inc(sem("gdn_tok"), 1)
                pe.wait_ge(sem("gdn_sq"), t + 1)
                for j in range(2):
                    for c in range(NC):
                        last = mm(ps[7][:, j * NC + c:j * NC + c + 1], SC[:, 8 + j, c * 128:(c + 1) * 128], one1)
                last.then_inc(sem("gdn_ss"), 1)
                fill(6)
                pe.wait_ge(sem("gdn_kn"), t + 1)
                pe.wait_ge(sem("gdn_E"), t + 1)
                for src, b in ((7, 5), (8, 2), (9, 3), (6, 6)):
                    for c in range(NC):
                        last = tp(ps[b][:, c * 128:(c + 1) * 128], SC[:, src, c * 128:(c + 1) * 128])
                    last.then_inc(sem("gdn_T1"), 1)
                fill(4)
                pe.wait_ge(sem("gdn_T1c"), 4 * t + 4)
                for a, b, bank in ((14, 15, 5), (14, 16, 4), (14, 17, 7)):
                    for c in range(NC):
                        s = slice(c * 128, (c + 1) * 128)
                        last = mm(ps[bank][:, s], SC[:, a, s], SC[:, b, s])
                    last.then_inc(sem("gdn_G"), 1)
                pe.wait_ge(sem("gdn_sc"), t + 1)
                for d, bank in ((0, 6), (1, 2)):
                    for c in range(NC):
                        last = tp(ps[bank][:, c * 128:(c + 1) * 128], SC[:, d, c * 128:(c + 1) * 128])
                    last.then_inc(sem("gdn_T2"), 1)
                fill(2)
                pe.wait_ge(sem("gdn_U"), 2 * t + 2)
                for d, bank in ((0, 3), (1, 4)):
                    for c in range(NC):
                        s = slice(c * 128, (c + 1) * 128)
                        last = tp(ps[bank][:, s], SC[:, 22 + d, s])
                    last.then_inc(sem("gdn_P"), 1)
                fill(2)
                pe.wait_ge(sem("gdn_T2c"), 2 * t + 2)
                for lv in range(1, 7):
                    for d in range(2):
                        pe.wait_ge(sem("gdn_T"), 12 * t + 2 * (lv - 1) + d + 1)
                        if lv == 1 and d == 1:
                            pe.wait_ge(sem("gdn_T"), 12 * t + 2)
                        for c in range(NC):
                            s = slice(c * 128, (c + 1) * 128)
                            last = mm(ps[2 + d][:, s], SC[:, 22 + d, s], SC[:, 6 + d, s])
                        last.then_inc(sem("gdn_P"), 1)
                    fill(3)
                    for d in range(2):
                        pe.wait_ge(sem("gdn_Pm"), 12 * t + 2 * (lv - 1) + d + 1)
                        if lv == 1:
                            pe.wait_ge(sem("gdn_M0"), 2 * t + d + 1)
                        else:
                            pe.wait_ge(sem("gdn_M"), 10 * t + 2 * (lv - 2) + d + 1)
                        if lv < 6:
                            for c in range(NC):
                                s = slice(c * 128, (c + 1) * 128)
                                last = mm(ps[4 + d][:, s], SC[:, 8 + d, s], SC[:, 16 + d, s])
                            last.then_inc(sem("gdn_Y"), 1)
                        for c in range(NC):
                            s = slice(c * 128, (c + 1) * 128)
                            last = mm(ps[6 + d][:, s], SC[:, 16 + d, s], SC[:, 8 + d, s])
                        last.then_inc(sem("gdn_YT"), 1)
                    fill(3)
                pe.wait_ge(sem("gdn_Mlast"), t + 1)
                pe.wait_ge(sem("gdn_AT"), t + 1)
                first = True
                for s in range(NC):
                    cc = (s, (1, 0, 3, 2)[s])
                    if s > 0:
                        pe.wait_ge(sem("gdn_S"), 3 * t + s)
                        for d in range(2):
                            c = slice(cc[d] * 128, cc[d] * 128 + 128)
                            last = mm(ps[2][:, d * 128:d * 128 + 128], SC[:, 14, c], st[:, d, :])
                        last.then_inc(sem("gdn_KS"), 1)
                        pe.wait_ge(sem("gdn_r"), 3 * t + s)
                    for d in range(2):
                        c = slice(cc[d] * 128, cc[d] * 128 + 128)
                        last = mm(ps[3][:, d * 128:d * 128 + 128], SC[:, 8 + d, c],
                                  rr[:, d, :] if s else SC[:, 12 + d, c])
                    last.then_inc(sem("gdn_vn"), 1)
                    if s > 0:
                        for d in range(2):
                            c = slice(cc[d] * 128, cc[d] * 128 + 128)
                            mm(ps[5][:, c], st[:, d, :], SC[:, 18 + d, c], start=first, stop=True)
                            first = False
                    fill(1)
                    pe.wait_ge(sem("gdn_vnc"), 4 * t + s + 1)
                    if s < NC - 1:
                        for d in range(2):
                            c = slice(cc[d] * 128, cc[d] * 128 + 128)
                            last = mm(ps[4][:, d * 128:d * 128 + 128], SC[:, 10 + d, c], vn[:, d, :])
                        last.then_inc(sem("gdn_dS"), 1)
                    for d in range(2):
                        c = slice(cc[d] * 128, cc[d] * 128 + 128)
                        last = mm(ps[5][:, c], vn[:, d, :], SC[:, 20 + d, c], start=first, stop=True)
                        first = False
                    if s == NC - 1:
                        last.then_inc(sem("gdn_o"), 1)
                    fill(2)
                pe.wait_ge(sem("gdn_osq"), t + 1)
                mm(ps[6][:, :], ones, SC[:, 1, :]).then_inc(sem("gdn_oss"), 1)
                fill.rest()

            def gla(i, t, l, fill):
                pe.wait_ge(sem("gla_stat"), t + 1)
                pe.wait_ge(sem("lr_copied"), l + 1)
                for d in range(2):
                    last = mm(ps[2 + d][:, :], wdp[:, d, :], lrT)
                last.then_inc(sem("gla_z"), 1)
                for a in range(2):
                    for c in range(NC):
                        s = slice(c * 128, (c + 1) * 128)
                        last = tp(ps[4 + a][:, s], SC[:, 16 + a, s])
                last.then_inc(sem("gla_vt"), 1)
                fill(40)
                pe.wait_ge(sem("gla_kd"), t + 1)
                pe.wait_ge(sem("gla_zc"), t + 1)
                for d in range(2):
                    for c in range(NC):
                        s = slice(c * 128, (c + 1) * 128)
                        last = tp(ps[2 + d][:, s], SC[:, 12 + d, s])
                last.then_inc(sem("gla_kt"), 1)
                pe.wait_ge(sem("gla_qd"), t + 1)
                for a in range(2):
                    for d in range(2):
                        bank = (6, 7, 2, 3)[2 * a + d]
                        if a == 1 and d == 0:
                            fill(10)
                            pe.wait_ge(sem("gla_ktc"), t + 1)
                        for c in range(NC):
                            s = slice(c * 128, (c + 1) * 128)
                            last = mm(ps[bank][:, s], SC[64 * a:64 * a + 64, 12 + d, s],
                                      SC[64 * a:64 * a + 64, 10 + d, s])
                        last.then_inc(sem("gla_att"), 1)
                pe.wait_ge(sem("gla_vtc"), t + 1)
                for d in range(2):
                    for a in range(2):
                        for c in range(NC):
                            s = slice(c * 128, (c + 1) * 128)
                            last = mm(ps[4 + d][64 * a:64 * a + 64, s],
                                      SC[:, 14 + d, c * 128 + 64 * a:c * 128 + 64 * a + 64], SC[:, 18 + a, s])
                last.then_inc(sem("gla_dS"), 1)
                fill(30)
                pe.wait_ge(sem("gla_S"), t + 1)
                pe.wait_ge(sem("gla_AT"), t + 1)
                for a in range(2):
                    first = True
                    for c in range(NC):
                        s = slice(c * 128, (c + 1) * 128)
                        for d in range(2):
                            last = mm(ps[6 + a][:, s], SC[:, 18 + a, s], SC[:, 20 + 2 * a + d, s], start=first)
                            first = False
                            step = (c, (1, 0, 3, 2)[c])[d]
                            if step:
                                last = mm(ps[6 + a][:, s],
                                          SC[64 * a:64 * a + 64, d, (step - 1) * 128:step * 128],
                                          SC[64 * a:64 * a + 64, 10 + d, s], start=False)
                    last.then_inc(sem("gla_o"), 1)
                fill(16)
                for a in range(2):
                    pe.wait_ge(sem("gla_osq"), 2 * t + a + 1)
                    mm(ps[2 + a][:, :], ones, SC[:, 4 + a, :]).then_inc(sem("gla_oss"), 1)
                fill.rest()

            def swa(i, t, fill, blocks):
                nb = len(blocks)
                pe.wait_ge(sem("swa_stat"), t + 1)
                for j in range(3):
                    last = mm(ps[2 + j // 2][:, (j % 2) * 256:(j % 2) * 256 + 256], cm(C_PERM), SC[:, j, CTX:])
                last.then_inc(sem("swa_rot"), 1)
                for c in range(NC):
                    s = slice(c * 128, (c + 1) * 128)
                    last = tp(ps[4][:, s], SC[:, 3, s])
                last.then_inc(sem("swa_vt"), 1)
                fill(10)
                pe.wait_ge(sem("swa_rope"), t + 1)
                sc0 = swa_base["score"]
                for j, (a, b) in enumerate((a, b) for a in range(2) for b in blocks):
                    n = TOK if b >= 2 else CTX
                    if j >= 2:
                        pe.wait_ge(sem("swa_sc"), t2(t) * 2 * nb + (swa_base["score"] + j - 1))
                    mm(ps[5 + j % 2][:, 0:n], SC[:, a, b * 128:(b + 1) * 128], SC[:, 2, 0:n])\
                        .then_inc(sem("swa_s"), 1)
                fill(40)
                for j, (a, b) in enumerate((a, b) for a in range(2) for b in blocks):
                    n = TOK if b >= 2 else CTX
                    pe.wait_ge(sem("swa_p"), t2(t) * 2 * nb + (swa_base["score"] + j + 1))
                    if j >= 2:
                        pe.wait_ge(sem("swa_pTc"), t2(t) * 2 * nb + (swa_base["score"] + j - 1))
                    for c in range(n // 128):
                        last = tp(ps[2 + j % 2][:, c * 128:(c + 1) * 128], SC[:, 6 + j, c * 128:(c + 1) * 128])
                    last.then_inc(sem("swa_pT"), 1)
                    fill(3)
                    if j > 0:
                        attend(j - 1, t, blocks)
                attend(2 * nb - 1, t, blocks)
                fill.rest()

            def attend(j, t, blocks):
                nb = len(blocks)
                a, b = j // nb, blocks[j % nb]
                n = TOK if b >= 2 else CTX
                pe.wait_ge(sem("swa_pTc"), t2(t) * 2 * nb + (swa_base["score"] + j + 1))
                if j == 0:
                    pe.wait_ge(sem("swa_vtc"), t + 1)
                bank = (4, 7)[a]
                for c in range(n // 128):
                    last = mm(ps[bank][:, b * 128:(b + 1) * 128], SC[:, 5, c * 128:(c + 1) * 128],
                              SC[:, 14 + j, c * 128:(c + 1) * 128],
                              start=(c == 0 and j % nb == 0), stop=True)
                if j % nb == nb - 1:
                    last.then_inc(sem("swa_o"), 1)

            swa_base = {"score": 0}
            loop_i = [0]

            def t2(t):
                return loop_i[0]

            channel_sum(0, 0)
            for l in range(DEPTH):
                lo = 0 if l == 0 else CTX
                pe.wait_ge(sem("norm_ready"), l + 1)
                with pe.Fori(0, 1) as _i:
                    Fill(l, "gdn", 4, 0, lo).rest()
                with pe.Fori(0, 2) as i:
                    Fill(l, "gdn", 4, i, 0, off=4).rest()
                with pe.Fori(0, 1) as _i:
                    Fill(l, "gdng", 4, 0, lo).rest()
                wt, n = segs[(l, "small")]
                pe.wait_ge(sem("small_in"), 32 * (l + 1))
                bank_wait(pe, n, 0, 2, 0)
                for k in range(KT):
                    last = mm(ps[n % 2][0:NLR, :], wlr[:, k, :], N[:, k, :], k == 0, k == KT - 1)
                last.then_inc(sem(f"bank{n % 2}_full"), 1)
                bank_wait(pe, n, 0, 2, 1)
                for b in range(NC):
                    for k in range(KT):
                        last = mm(ps[1][:, b * NAB:(b + 1) * NAB], N[:, k, b * 128:(b + 1) * 128], wab[:, k, :],
                                  k == 0, k == KT - 1)
                last.then_inc(sem("bank1_full"), 1)
                pe.wait_ge(sem("bank1_full"), (n + 1) // 2 + 1)
                pe.sem_inc(sem("small_done"), 1)
                pe.wait_ge(sem("gdn_g"), l + 1)
                for d in range(2):
                    for kind, lhs in enumerate((cm(CUM[d]), cm(TAIL[d]), ones)):
                        last = mm(ps[3][:, (3 * d + kind) * 16:(3 * d + kind + 1) * 16], lhs, g[:, :, d, :])
                last.then_inc(sem("gdn_cums"), 1)
                with pe.Fori(0, 4) as i:
                    gdn(i, i + 4 * l, Fill(l, "p2", 4, i, 0))
                pe.wait_ge(sem("gdn_y"), 4 * l + 4)
                with pe.Fori(0, 2) as i:
                    gla(i, i + 2 * l, l, Fill(l, "p3", 4, i, 0))
                    pe.wait_ge(sem("gla_y"), i + 2 * l + 1)
                blocks = list(range(4)) if l == 0 else [2, 3]
                with pe.Fori(0, 2) as i:
                    loop_i[0] = i
                    swa(i, i + 2 * l, Fill(l, "p4", 8, i, lo), blocks)
                    pe.wait_ge(sem("swa_y"), i + 2 * l + 1)
                swa_base["score"] += 4 * len(blocks)
                pe.sem_inc(sem("norm_used"), 1)
                pe.wait_ge(sem("sc_y"), 4 * l + 4)
                project(l, "out", 16, rhs=lambda k: act[:, Y_ORDER[k], lo:])
                channel_sum(2 * l + 1, lo)
                if l == 0:
                    project(0, "ada1", 48, rhs=lambda k: cs[:, k, :])
                    channel_sum(2, 0)
            wt, n = segs["end"]
            pe.wait_ge(sem("h_ready"), DEPTH + 1)
            for b in range(2):
                for q in range(4):
                    j = 4 * b + q
                    bank_wait(pe, n, 0, 8, j)
                    for c in range(4):
                        last = tp(ps[(n + j) % 2][:, c * 128:(c + 1) * 128],
                                  N[:, 4 * q + c, CTX + b * 128:CTX + (b + 1) * 128])
                    last.then_inc(sem(f"bank{(n + j) % 2}_full"), 1)

        @block.scalar
        def _(sc_eng):
            A = sc_eng

            def act_(out, in_, f, **kw):
                return nc.scalar.activation(out, in_, f, **kw)

            def evac(l, name, tb, i, tt, dst, off=0):
                n = segs[(l, name)][1] + off
                b = (n + tt) % 2
                out_wait(A, n, i, tb, tt)
                act_(dst, ps[b][:, 0:dst.shape[-1]], ACT.Copy).then_inc(sem(f"bank{b}_free"), 1)

            def evac_loop(l, name, rounds, dst, off=0):
                with A.Fori(0, rounds) as i:
                    for tt in range(RING):
                        evac(l, name, RING, i, tt, dst(i, tt), off)

            A.wait_ge(sem("con_in"), 16)
            A.wait_ge(sem("par_in"), 16)
            act_(cst[:, :, :], par[:, P_C:P_C + 2 * KT].rearrange("p (k s) -> p k s", s=2), ACT.Exp, scale=-1.0)\
                .then_inc(sem("c_exp"), 1)
            for k in range(KT):
                out_wait(A, 0, 0, KT, k)
                act_(N[:, k, :], ps[k % 2][:, :], ACT.Copy).then_inc(sem(f"bank{k % 2}_free"), 1)
            evac_loop(0, "ada0", 12, lambda i, tt: ada[:, 0, i * 4 + tt, :])
            A.wait_ge(sem("bank0_free"), (segs[(0, "ada0")][1] + 48) // 2)
            A.wait_ge(sem("bank1_free"), (segs[(0, "ada0")][1] + 48) // 2)
            A.sem_inc(sem("ada_out"), 1)

            def rstd(t, bank, n, lo):
                A.wait_ge(sem("chansum_done"), t + 1)
                act_(SC[:, 2, lo:], ps[bank][:, lo:], ACT.Ln, scale=1.0 / n, bias=eps).then_inc(sem("rs_ln"), 1)
                A.wait_ge(sem("rs_ln"), t + 1)
                act_(SC[:, 3, lo:], SC[:, 2, lo:], ACT.Exp, scale=-0.5).then_inc(sem("rstd_ready"), 1)

            def gdn(i, t, l, lo, take):
                A.wait_ge(sem("gdn_cv"), t + 1)
                act_(SC[:, 3:6, :], SC[:, 0:3, :], ACT.Exp, scale=-1.0).then_inc(sem("gdn_ex"), 1)
                A.wait_ge(sem("gdn_D"), t + 1)
                for d in range(2):
                    last = act_(SC[:, 20 + d, :], ps[5 + d][:, :], ACT.Exp)
                last.then_inc(sem("gdn_E"), 1)
                A.wait_ge(sem("gdn_x"), t + 1)
                act_(SC[:, 8:10, :], SC[:, 0:2, :], ACT.Square).then_inc(sem("gdn_sq"), 1)
                A.wait_ge(sem("gdn_tok"), t + 1)
                for j in range(3):
                    last = act_(SC[:, 3 + j, :], ps[2 + j][:, :], ACT.Copy)
                last.then_inc(sem("gdn_tokc"), 1)
                A.wait_ge(sem("gdn_ss"), t + 1)
                act_(rn[:, :, :], ps[7][:, 0:2 * NC].rearrange("p (a c) -> p a c", a=2), ACT.Ln, bias=eps)\
                    .then_inc(sem("gdn_rl"), 1)
                A.wait_ge(sem("gdn_rl"), t + 1)
                act_(rn[:, :, :], rn[:, :, :], ACT.Exp, scale=-0.5).then_inc(sem("gdn_rn"), 1)
                for j, (b, dst) in enumerate(((5, 14), (2, 16), (3, 17), (6, 15))):
                    A.wait_ge(sem("gdn_T1"), 4 * t + j + 1)
                    act_(SC[:, dst, :], ps[b][:, :], ACT.Copy).then_inc(sem("gdn_T1c"), 1)
                take(0)
                for d, b in ((0, 6), (1, 2)):
                    A.wait_ge(sem("gdn_T2"), 2 * t + d + 1)
                    act_(SC[:, 18 + d, :], ps[b][:, :], ACT.Copy).then_inc(sem("gdn_T2c"), 1)
                A.wait_ge(sem("gdn_G"), 3 * t + 1)
                act_(SC[:, 15, lo:], act[:, i + Y_GDN, lo:],
                     ACT.Exp, scale=-1.0).then_inc(sem("gdn_ge"), 1)
                A.wait_ge(sem("gdn_P"), 14 * t + 2 + 6)
                take(1)
                A.wait_ge(sem("gdn_P"), 14 * t + 2 + 12)
                take(2)
                for s in range(NC):
                    A.wait_ge(sem("gdn_vn"), 4 * t + s + 1)
                    if s:
                        A.wait_ge(sem("gdn_dS"), 3 * t + s)
                    act_(vn[:, :, :], ps[3][:, 0:256].rearrange("p (d v) -> p d v", d=2), ACT.Copy,
                         scale=1.0 if s == 0 else -1.0).then_inc(sem("gdn_vnc"), 1)
                A.wait_ge(sem("gdn_o"), t + 1)
                act_(SC[:, 0, lo:], ps[5][:, lo:], ACT.Copy)
                act_(SC[:, 1, :], ps[5][:, :], ACT.Square).then_inc(sem("gdn_osq"), 1)
                A.wait_ge(sem("gdn_oss"), t + 1)
                act_(SC[:, 2, lo:], ps[6][:, lo:], ACT.Ln, scale=1.0 / HD, bias=eps).then_inc(sem("gdn_oln"), 1)
                A.wait_ge(sem("gdn_oln"), t + 1)
                act_(SC[:, 3, lo:], SC[:, 2, lo:], ACT.Exp, scale=-0.5).then_inc(sem("gdn_orn"), 1)
                take(3)
                A.wait_ge(sem("gdn_y"), t + 1)

            def gla(i, t, l, lo, take):
                A.wait_ge(sem("gla_z"), t + 1)
                for d in range(2):
                    last = act_(SC[:, d, :], ps[2 + d][:, :], ACT.Identity,
                                bias=par[:, bass.ds(i + (l * PL + P_GLAB + 2 * d), 1)])
                last.then_inc(sem("gla_zc"), 1)
                A.wait_ge(sem("gla_vt"), t + 1)
                for a in range(2):
                    last = act_(SC[:, 18 + a, :], ps[4 + a][:, :], ACT.Copy)
                last.then_inc(sem("gla_vtc"), 1)
                A.wait_ge(sem("gla_abs"), t + 1)
                act_(SC[:, 2:4, :], SC[:, 2:4, :], ACT.Exp, scale=-1.0).then_inc(sem("gla_e"), 1)
                A.wait_ge(sem("gla_e"), t + 1)
                act_(SC[:, 2:4, :], SC[:, 2:4, :], ACT.Ln, bias=one1).then_inc(sem("gla_l"), 1)
                for a in range(2):
                    last = act_(SC[:, 16 + a, lo:], act[:, i * 2 + (Y_GLA + a), lo:], ACT.Exp, scale=-1.0)
                last.then_inc(sem("gla_ge"), 1)
                A.wait_ge(sem("gla_cen"), t + 1)
                act_(SC[:, 8:10, :], SC[:, 2:4, :], ACT.Exp, scale=-1.0 / 16).then_inc(sem("gla_ek"), 1)
                act_(SC[:, 6:8, :], SC[:, 2:4, :], ACT.Exp, scale=1.0 / 16).then_inc(sem("gla_eq"), 1)
                for d in range(2):
                    mid, last_ = (CH // 2 - 1, CH - 1) if d == 0 else (CH // 2, 0)
                    act_(gs[:, 0, d, :], SC[:, 4 + d, mid::CH], ACT.Exp, scale=1.0 / 16)
                    act_(gs[:, 1, d, :], SC[:, 4 + d, last_::CH], ACT.Exp, scale=1.0 / 16)
                act_(gs[:, 2, :, :], gd[:, :, :], ACT.Exp, scale=1.0 / 16).then_inc(sem("gla_gs"), 1)
                take(0)
                take(1)
                A.wait_ge(sem("gla_kt"), t + 1)
                for d in range(2):
                    last = act_(SC[:, 14 + d, :], ps[2 + d][:, :], ACT.Copy)
                last.then_inc(sem("gla_ktc"), 1)
                take(2)
                A.wait_ge(sem("gla_AT"), t + 1)
                for a in range(2):
                    A.wait_ge(sem("gla_o"), 2 * t + a + 1)
                    act_(SC[:, 6 + a, lo:], ps[6 + a][:, lo:], ACT.Copy)
                    act_(SC[:, 4 + a, :], ps[6 + a][:, :], ACT.Square).then_inc(sem("gla_osq"), 1)
                for a in range(2):
                    A.wait_ge(sem("gla_oss"), 2 * t + a + 1)
                    act_(SC[:, 8 + a, lo:], ps[2 + a][:, lo:], ACT.Ln, scale=1.0 / HD, bias=eps)\
                        .then_inc(sem("gla_oln"), 1)
                    A.wait_ge(sem("gla_oln"), 2 * t + a + 1)
                    act_(SC[:, 8 + a, lo:], SC[:, 8 + a, lo:], ACT.Exp, scale=-0.5).then_inc(sem("gla_orn"), 1)
                take(3)
                A.wait_ge(sem("gla_y"), t + 1)

            swb = [0]

            def swa(i, t, l, lo, take, blocks):
                nb = len(blocks)
                A.wait_ge(sem("swa_vt"), t + 1)
                act_(SC[:, 5, :], ps[4][:, :], ACT.Copy).then_inc(sem("swa_vtc"), 1)
                A.wait_ge(sem("swa_stat"), t + 1)
                for a in range(2):
                    last = act_(SC[:, 22 + a, lo:], act[:, i * 2 + (Y_SWA + a), lo:], ACT.Exp, scale=-1.0)
                last.then_inc(sem("swa_ge"), 1)
                take(0)
                A.wait_ge(sem("swa_m"), t + 1)
                for j in range(2 * nb):
                    n = TOK if blocks[j % nb] >= 2 else CTX
                    act_(SC[:, 6 + j, 0:n], SC[:, 6 + j, 0:n], ACT.Exp, scale=HD ** -0.5,
                         bias=sm[:, 1, j:j + 1], accum_out=sm[:, 2, j:j + 1])
                for a in range(2):
                    last = act_(sm[:, 3, a * nb:(a + 1) * nb], sm[:, 1, a * nb:(a + 1) * nb], ACT.Exp,
                                bias=par[:, bass.ds(i * 2 + (l * PL + P_SINK + a), 1)])
                last.then_inc(sem("swa_e"), 1)
                take(1)
                take(2)
                for j in range(2 * nb):
                    n = TOK if blocks[j % nb] >= 2 else CTX
                    A.wait_ge(sem("swa_pT"), i * 2 * nb + (swb[0] + j + 1))
                    act_(SC[:, 14 + j, 0:n], ps[2 + j % 2][:, 0:n], ACT.Copy).then_inc(sem("swa_pTc"), 1)
                for tt in range(3, 8):
                    take(tt)
                A.wait_ge(sem("swa_y"), t + 1)

            def take_(l, name, tb, i, dst):
                return lambda tt: evac(l, name, tb, i, tt, dst(tt))

            rstd(0, 2, D, 0)
            for l in range(DEPTH):
                lo = 0 if l == 0 else CTX
                if l:
                    A.wait_ge(sem("yo_used"), l)
                with A.Fori(0, 1) as _i:
                    for tt in range(4):
                        evac(l, "gdn", 4, 0, tt, act[:, tt, lo:])
                evac_loop(l, "gdn", 2, lambda i, tt: act[:, i * 4 + (4 + tt), :], off=4)
                with A.Fori(0, 1) as _i:
                    for tt in range(4):
                        evac(l, "gdng", 4, 0, tt, act[:, Y_GDN + tt, lo:])
                wt, n = segs[(l, "small")]
                assert n % 2 == 0
                out_wait(A, n, 0, 2, 0)
                act_(lrT, ps[0][0:NLR, :], ACT.Copy).then_inc(sem("bank0_free"), 1)
                A.wait_ge(sem("bank0_free"), n // 2 + 1)
                A.sem_inc(sem("lr_copied"), 1)
                out_wait(A, n, 0, 2, 1)
                act_(ab, ps[1][:, 0:NC * NAB].rearrange("p (c k) -> p c k", k=NAB), ACT.Copy)\
                    .then_inc(sem("bank1_free"), 1)
                A.wait_ge(sem("bank1_free"), n // 2 + 1)
                A.sem_inc(sem("ab_copied"), 1)
                if l:
                    A.wait_ge(sem("gdn_g"), l)
                act_(expA[:, :, :], P(l, P_ALOG, 8).rearrange("p (d h) -> p d h", d=2), ACT.Exp)\
                    .then_inc(sem("expA"), 1)
                A.wait_ge(sem("gate_abs"), l + 1)
                act_(gt[:, :, :, :], gt[:, :, :, :], ACT.Exp, scale=-1.0).then_inc(sem("gate_e"), 1)
                A.wait_ge(sem("gate_e"), l + 1)
                act_(gt[:, :, :, :], gt[:, :, :, :], ACT.Ln, bias=one1).then_inc(sem("gate_l"), 1)
                A.wait_ge(sem("gate_bc"), l + 1)
                act_(beta[:, :, :, :], beta[:, :, :, :], ACT.Exp, scale=-1.0).then_inc(sem("beta_e"), 1)
                A.wait_ge(sem("gdn_cums"), l + 1)
                act_(eg[:, :, :, :, :].rearrange("p a b c d -> p (a b c d)"), ps[3][:, 0:96], ACT.Exp)\
                    .then_inc(sem("gdn_eg"), 1)
                with A.Fori(0, 4) as i:
                    gdn(i, i + 4 * l, l, lo, take_(l, "p2", 4, i, lambda tt: act[:, i * 4 + (T_B + tt), :]))
                with A.Fori(0, 2) as i:
                    gla(i, i + 2 * l, l, lo, take_(l, "p3", 4, i, lambda tt: act[:, i * 4 + (T_A + tt), :]))
                blocks = list(range(4)) if l == 0 else [2, 3]
                with A.Fori(0, 2) as i:
                    swa(i, i + 2 * l, l, lo, take_(l, "p4", 8, i, lambda tt: act[
                        :, (i * 8 + (8 + tt)) if tt < 4 else (i * 20 + (8 + tt)), lo:]), blocks)
                swb[0] += 4 * len(blocks)
                with A.Fori(0, 4) as i:
                    act_(SC[:, 3, lo:], act[:, i + Y_SC, lo:], ACT.Exp, scale=-1.0).then_inc(sem("sc_ge"), 1)
                    A.wait_ge(sem("sc_y"), i + 4 * l + 1)
                n = segs[(l, "out")][1]
                with A.Fori(0, 4) as i:
                    for tt in range(4):
                        b = (n + tt) % 2
                        out_wait(A, n, i, 4, tt)
                        act_(act[:, i * 4 + tt, lo:], ps[b][:, 0:TOK - lo], ACT.Copy)
                        if tt >= 2:
                            A.wait_ge(sem("yo_add"), i * 4 + (16 * l + tt - 1))
                        else:
                            A.wait_ge(sem("yo_round"), i + (4 * l + 1))
                        act_(SC[:, 4 + tt % 2, lo:], ps[b][:, 0:TOK - lo], ACT.Square)\
                            .then_inc(sem(f"bank{b}_free"), 1)
                rstd(2 * l + 1, 2, D, lo)
                if l == 0:
                    evac_loop(0, "ada1", 12, lambda i, tt: ada[:, 1, i * 4 + tt, :])
                    A.wait_ge(sem("bank0_free"), (segs[(0, "ada1")][1] + 48) // 2)
                    A.wait_ge(sem("bank1_free"), (segs[(0, "ada1")][1] + 48) // 2)
                    A.sem_inc(sem("ada_out"), 1)
                    A.wait_ge(sem("rstd_used"), 1)
                    rstd(2, 2, D, 0)
            wt, n = segs["end"]
            A.wait_ge(sem("yo_used"), DEPTH)
            for j in range(8):
                out_wait(A, n, 0, 8, j)
                act_(act[:, j, :], ps[(n + j) % 2][:, :], ACT.Copy).then_inc(sem(f"bank{(n + j) % 2}_free"), 1)
                A.wait_ge(sem(f"bank{(n + j) % 2}_free"), (n + j) // 2 + 1)
                A.sem_inc(sem("out_staged"), 1)

        @block.vector
        def _(dve):
            V = nc.vector
            o = Order(dve, sem("dve_order"))

            def link(ins):
                o.done(ins)
                o.wait()

            dve.wait_ge(sem("con_in"), 16)
            dve.wait_ge(sem("par_in"), 16)
            dve.wait_ge(sem("c_exp"), 1)
            link(V.tensor_scalar(cst[:, :, :], cst[:, :, :], 1.0, None, ALU.add))
            link(V.reciprocal(cst[:, :, :], cst[:, :, :]))
            V.tensor_tensor(cs[:, :, :], cst[:, :, :], par[:, P_C:P_C + 2 * KT].rearrange("p (k s) -> p k s", s=2),
                            ALU.mult).then_inc(sem("cs_ready"), 1)

            def modulation(l):
                dve.wait_ge(sem("ada_out"), l + 1)
                link(V.tensor_tensor(ada[:, l, :, :], ada[:, l, :, :], along(P(l, P_ADAB, 48), 2), ALU.add))
                V.scalar_tensor_tensor(modA[:, l, :, :], ada[:, l, 16:32, :], 1.0, along(P(l, P_NPRE, 16), 2),
                                       ALU.add, ALU.mult)
                link(V.tensor_tensor(modG[:, l, :, :], ada[:, l, 32:48, :], along(P(l, P_NPOST, 16), 2), ALU.mult))

            def prenorm(l, t):
                dve.wait_ge(sem("rstd_ready"), t + 1)
                dve.wait_ge(sem("h_saved"), 16 * (l + 1))
                ws = []
                for k in range(KT + 1):
                    if k < KT:
                        ws.append(o.done(V.tensor_tensor(N[:, k, :], N[:, k, :], SC[:, 3, :], ALU.mult)))
                    if k:
                        o.wait(ws[k - 1])
                        for hf in range(2):
                            s = slice(hf * 256, hf * 256 + 256)
                            last = V.tensor_scalar(N[:, k - 1, s], N[:, k - 1, s], modA[:, l, k - 1, hf:hf + 1],
                                                   ada[:, l, k - 1, hf:hf + 1], ALU.mult, ALU.add)
                last.then_inc(sem("norm_ready"), 1)

            def sigmoid_tail(a):
                link(V.tensor_scalar(a, a, 1.0, None, ALU.add))
                link(V.reciprocal(a, a))

            def two(a):
                return a.rearrange("p (s t) -> p s t", s=2)

            def conv_tap(dst, src, wcol, sh):
                d, s = two(dst), two(src)
                a, b = max(0, -sh), SEQ - max(0, sh)
                return V.scalar_tensor_tensor(d[:, :, a:b], s[:, :, a + sh:b + sh], wcol, d[:, :, a:b],
                                              ALU.mult, ALU.add)

            def gates(l):
                dve.wait_ge(sem("ab_copied"), l + 1)
                z = o.done(V.tensor_tensor(gz[:, :, :, :].rearrange("p c d h -> p c (d h)"), ab[:, :, 0:8],
                                           over(P(l, P_DT, 8)), ALU.add))
                V.tensor_copy(beta[:, :, :, :].rearrange("p h d c -> p c d h"),
                              ab[:, :, 8:16].rearrange("p c (d h) -> p c d h", d=2)).then_inc(sem("gate_bc"), 1)
                o.wait(z)
                V.scalar_tensor_tensor(gt[:, :, :, :], gz[:, :, :, :], -1.0, gz[:, :, :, :], ALU.mult, ALU.max)\
                    .then_inc(sem("gate_abs"), 1)
                dve.wait_ge(sem("gate_l"), l + 1)
                link(V.scalar_tensor_tensor(gz[:, :, :, :], gz[:, :, :, :], 0.0, gt[:, :, :, :], ALU.max, ALU.add))
                dve.wait_ge(sem("expA"), l + 1)
                for d in range(2):
                    last = V.scalar_tensor_tensor(g[:, :, d, :].rearrange("p h c -> p c h"), gz[:, :, d, :], -1.0,
                                                  over(expA[:, d, :]), ALU.mult, ALU.mult)
                last.then_inc(sem("gdn_g"), 1)
                dve.wait_ge(sem("beta_e"), l + 1)
                sigmoid_tail(beta[:, :, :, :])
                dve.sem_inc(sem("beta_ready"), 1)

            def gdn(i, t, l, lo):
                def tile(j):
                    return act[:, i + (T_A + 4 * j), :]

                def wcol(j, tap):
                    return par[:, bass.ds(i * 5 + (l * PL + P_CONV + 20 * j + tap), 1)]
                at = {}
                for j in range(3):
                    at[j] = o.done(V.tensor_scalar(SC[:, j, :], tile(j), wcol(j, 2), None, ALU.mult))
                for tap in (0, 1, 3, 4):
                    for j in range(3):
                        o.wait(at[j])
                        at[j] = o.done(conv_tap(SC[:, j, :], tile(j), wcol(j, tap), tap - 2))
                o.wait()
                dve.sem_inc(sem("gdn_cv"), 1)
                dve.wait_ge(sem("gdn_ex"), t + 1)
                sigmoid_tail(SC[:, 3:6, :])
                V.tensor_tensor(SC[:, 0:3, :], SC[:, 0:3, :], SC[:, 3:6, :], ALU.mult).then_inc(sem("gdn_x"), 1)
                dve.wait_ge(sem("gdn_tokc"), t + 1)
                dve.wait_ge(sem("gdn_ks"), t + 1)
                V.tensor_tensor(chunks(SC[:, 7, :]), chunks(SC[:, 4, :]), along(rn[:, 1, :]), ALU.mult)
                for d in range(2):
                    V.tensor_tensor(chunks(SC[:, 8 + d, :]), chunks(SC[:, 4, :]), along(ks[:, 0, d, :]), ALU.mult)
                V.tensor_tensor(chunks(SC[:, 6, :]), chunks(SC[:, 3, :]), along(rq[:, :]), ALU.mult)\
                    .then_inc(sem("gdn_kn"), 1)
                dve.wait_ge(sem("gdn_Em"), t + 1)
                dve.wait_ge(sem("gdn_G"), 3 * t + 1)
                at_ins = []
                for d in range(2):
                    last = V.tensor_tensor(SC[:, 20 + d, :], ps[5][:, :], SC[:, 20 + d, :], ALU.mult)
                last.then_inc(sem("gdn_AT"), 1)
                for d, bank in ((0, 4), (1, 7)):
                    dve.wait_ge(sem("gdn_G"), 3 * t + 2 + d)
                    V.tensor_tensor(SC[:, 22 + d, :], ps[bank][:, :], SC[:, 22 + d, :], ALU.mult)\
                        .then_inc(sem("gdn_U"), 1)
                MK = (C_LO, C_UP)
                for d, bank in ((0, 3), (1, 4)):
                    dve.wait_ge(sem("gdn_P"), 14 * t + d + 1)
                    o.done(V.tensor_tensor(chunks(SC[:, 16 + d, :]), chunks(ps[bank][:, :]), over(cm(MK[d])),
                                           ALU.mult))
                    o.wait()
                    V.tensor_tensor(chunks(SC[:, 6 + d, :]), over(ident), chunks(SC[:, 16 + d, :]), ALU.subtract)\
                        .then_inc(sem("gdn_T"), 1)
                for lv in range(1, 7):
                    for d in range(2):
                        dve.wait_ge(sem("gdn_P"), 14 * t + 2 * lv + d + 1)
                        V.tensor_tensor(chunks(SC[:, 16 + d, :]), chunks(ps[2 + d][:, :]),
                                        over(cm(MK[d] + 128 * lv)), ALU.mult).then_inc(sem("gdn_Pm"), 1)
                    for d in range(2):
                        if lv < 6:
                            dve.wait_ge(sem("gdn_Y"), 10 * t + 2 * (lv - 1) + d + 1)
                            dve.wait_ge(sem("gdn_T"), 12 * t + 2 * (lv - 1) + d + 1)
                            V.tensor_tensor(SC[:, 6 + d, :], SC[:, 6 + d, :], ps[4 + d][:, :], ALU.subtract)\
                                .then_inc(sem("gdn_T"), 1)
                        dve.wait_ge(sem("gdn_YT"), 12 * t + 2 * (lv - 1) + d + 1)
                        if lv == 1:
                            dve.wait_ge(sem("gdn_M0"), 2 * t + d + 1)
                        else:
                            dve.wait_ge(sem("gdn_M"), 10 * t + 2 * (lv - 2) + d + 1)
                        last = V.tensor_tensor(SC[:, 8 + d, :], SC[:, 8 + d, :], ps[6 + d][:, :], ALU.subtract)
                        if lv < 6:
                            last.then_inc(sem("gdn_M"), 1)
                last.then_inc(sem("gdn_Mlast"), 1)
                at[0] = 0
                for s in range(NC):
                    cc = (s, (1, 0, 3, 2)[s])
                    if s:
                        dve.wait_ge(sem("gdn_KS"), 3 * t + s)
                        for d in range(2):
                            last = V.scalar_tensor_tensor(rr[:, d, :], ps[2][:, d * 128:d * 128 + 128],
                                                          ks[:, 3, d, cc[d]:cc[d] + 1],
                                                          SC[:, 12 + d, cc[d] * 128:cc[d] * 128 + 128],
                                                          ALU.mult, ALU.subtract)
                        last.then_inc(sem("gdn_r"), 1)
                    if s < NC - 1:
                        dve.wait_ge(sem("gdn_dS"), 3 * t + s + 1)
                        if s == 0:
                            V.tensor_copy(st[:, :, :], ps[4][:, 0:256].rearrange("p (d v) -> p d v", d=2))\
                                .then_inc(sem("gdn_S"), 1)
                        else:
                            dve.wait_ge(sem("gdn_S"), 3 * t + s)
                            for d in range(2):
                                last = V.scalar_tensor_tensor(st[:, d, :], st[:, d, :],
                                                              tot[:, d, cc[d]:cc[d] + 1],
                                                              ps[4][:, d * 128:d * 128 + 128], ALU.mult, ALU.add)
                            last.then_inc(sem("gdn_S"), 1)
                dve.wait_ge(sem("gdn_ge"), t + 1)
                sigmoid_tail(SC[:, 15, lo:])
                link(V.tensor_tensor(SC[:, 15, lo:], SC[:, 15, lo:], act[:, i + Y_GDN, lo:], ALU.mult))
                dve.wait_ge(sem("gdn_orn"), t + 1)
                link(V.scalar_tensor_tensor(SC[:, 0, lo:], SC[:, 0, lo:], P(l, P_GDNN), SC[:, 3, lo:],
                                            ALU.mult, ALU.mult))
                V.tensor_tensor(act[:, i + Y_GDN, lo:], SC[:, 0, lo:], SC[:, 15, lo:], ALU.mult)\
                    .then_inc(sem("gdn_y"), 1)
                dve.wait_ge(sem("gdn_y"), t + 1)

            def gla(i, t, l, lo):
                dve.wait_ge(sem("gla_zc"), t + 1)
                V.scalar_tensor_tensor(SC[:, 2:4, :], SC[:, 0:2, :], -1.0, SC[:, 0:2, :], ALU.mult, ALU.max)\
                    .then_inc(sem("gla_abs"), 1)
                dve.wait_ge(sem("gla_l"), t + 1)
                link(V.scalar_tensor_tensor(SC[:, 0:2, :], SC[:, 0:2, :], 0.0, SC[:, 2:4, :], ALU.min, ALU.subtract))
                V.tensor_tensor_scan(SC[:, 4, :], con[:, C_SEG:C_SEG + TOK], SC[:, 0, :], 0.0, ALU.mult, ALU.add)
                link(V.tensor_tensor_scan(SC[:, 5, ::-1], con[:, C_SEG:C_SEG + TOK], SC[:, 1, ::-1], 0.0,
                                          ALU.mult, ALU.add))
                for d in range(2):
                    mid, last_ = (CH // 2 - 1, CH - 1) if d == 0 else (CH // 2, 0)
                    V.tensor_tensor(gd[:, d, :], SC[:, 4 + d, last_::CH], SC[:, 4 + d, mid::CH], ALU.subtract)
                    last = V.tensor_tensor(chunks(SC[:, 2 + d, :]), chunks(SC[:, 4 + d, :]),
                                           along(SC[:, 4 + d, mid::CH]), ALU.subtract)
                link(last)
                V.tensor_scalar(SC[:, 2:4, :], SC[:, 2:4, :], 640.0, -640.0, ALU.min, ALU.max)\
                    .then_inc(sem("gla_cen"), 1)
                dve.wait_ge(sem("gla_eq"), t + 1)
                for d in range(2):
                    last = V.scalar_tensor_tensor(SC[:, 10 + d, :], act[:, i + T_B, :], 64 ** -0.5, SC[:, 6 + d, :],
                                                  ALU.mult, ALU.mult)
                last.then_inc(sem("gla_qd"), 1)
                for a in range(2):
                    for d in range(2):
                        bank = (6, 7, 2, 3)[2 * a + d]
                        dve.wait_ge(sem("gla_att"), 4 * t + 2 * a + d + 1)
                        last = V.tensor_tensor(chunks(SC[:, 20 + 2 * a + d, :]), chunks(ps[bank][:, :]),
                                               over(cm(CUM[d])), ALU.mult)
                last.then_inc(sem("gla_AT"), 1)
                dve.wait_ge(sem("gla_dS"), t + 1)
                dve.wait_ge(sem("gla_gs"), t + 1)
                dve.wait_ge(sem("gla_kd"), t + 1)
                for d in range(2):
                    last = V.tensor_tensor(chunks(SC[:, 2 + d, :]), chunks(ps[4 + d][:, :]),
                                           along(gs[:, 2, d, :]), ALU.mult)
                link(last)
                for s in range(1, NC):
                    for d in range(2):
                        prev = (s - 1, (1, 0, 3, 2)[s - 1])[d]
                        own = SC[:, 2 + d, prev * 128:prev * 128 + 128]
                        to = SC[:, 8 + d, (s - 1) * 128:s * 128]
                        if s == 1:
                            last = V.tensor_copy(to, own)
                        else:
                            last = V.scalar_tensor_tensor(to, SC[:, 8 + d, (s - 2) * 128:(s - 1) * 128],
                                                          gs[:, 1, d, prev:prev + 1], own, ALU.mult, ALU.add)
                    link(last)
                for s in range(1, NC):
                    for d in range(2):
                        c = (s, (1, 0, 3, 2)[s])[d]
                        last = V.tensor_scalar(SC[:, d, (s - 1) * 128:s * 128], SC[:, 8 + d, (s - 1) * 128:s * 128],
                                               gs[:, 0, d, c:c + 1], None, ALU.mult)
                last.then_inc(sem("gla_S"), 1)
                dve.wait_ge(sem("gla_ge"), t + 1)
                sigmoid_tail(SC[:, 16:18, lo:])
                link(V.tensor_tensor(SC[:, 16:18, lo:], SC[:, 16:18, lo:],
                                     act[:, bass.ds(i * 2 + Y_GLA, 2), lo:], ALU.mult))
                for a in range(2):
                    dve.wait_ge(sem("gla_orn"), 2 * t + a + 1)
                    link(V.scalar_tensor_tensor(SC[:, 6 + a, lo:], SC[:, 6 + a, lo:], P(l, P_GLAN),
                                                SC[:, 8 + a, lo:], ALU.mult, ALU.mult))
                V.tensor_tensor(act[:, bass.ds(i * 2 + Y_GLA, 2), lo:], SC[:, 6:8, lo:], SC[:, 16:18, lo:],
                                ALU.mult).then_inc(sem("gla_y"), 1)
                dve.wait_ge(sem("gla_y"), t + 1)

            swb = [0]

            def swa(i, t, l, lo, blocks):
                nb = len(blocks)
                dve.wait_ge(sem("swa_stat"), t + 1)
                dve.wait_ge(sem("swa_rot"), t + 1)
                sin2 = con[:, C_SIN:C_SIN + SEQ]
                V.tensor_tensor(SC[:, 20:22, 0:SEQ], ps[2][:, :].rearrange("p (a t) -> p a t", a=2),
                                over(sin2, 2), ALU.mult)
                V.tensor_tensor(SC[:, 4, 0:SEQ], ps[3][:, 0:SEQ], sin2, ALU.mult)
                link(V.tensor_tensor(SC[:, 0:3, CTX:], SC[:, 0:3, CTX:], over(con[:, C_COS:C_COS + SEQ], 3), ALU.mult))
                V.tensor_tensor(SC[:, 0:2, CTX:], SC[:, 0:2, CTX:], SC[:, 20:22, 0:SEQ], ALU.add)
                V.tensor_tensor(SC[:, 2, CTX:], SC[:, 2, CTX:], SC[:, 4, 0:SEQ], ALU.add)\
                    .then_inc(sem("swa_rope"), 1)
                for j in range(2 * nb):
                    b = blocks[j % nb]
                    n = TOK if b >= 2 else CTX
                    dve.wait_ge(sem("swa_s"), i * 2 * nb + (swb[0] + j + 1))
                    last = V.tensor_copy(SC[:, 6 + j, 0:CTX], ps[5 + j % 2][:, 0:CTX])
                    if b >= 2:
                        mk = C_MASK + (b - 2) * SEQ
                        last = V.tensor_tensor(SC[:, 6 + j, CTX:], ps[5 + j % 2][:, CTX:], con[:, mk:mk + SEQ],
                                               ALU.add)
                    last.then_inc(sem("swa_sc"), 1)
                dve.wait_ge(sem("swa_sc"), i * 2 * nb + (swb[0] + 2 * nb))
                for j in range(2 * nb):
                    n = TOK if blocks[j % nb] >= 2 else CTX
                    last = V.tensor_reduce(sm[:, 0, j:j + 1], SC[:, 6 + j, 0:n], AX, ALU.max)
                link(last)
                for a in range(2):
                    last = V.tensor_scalar(sm[:, 1, a * nb:(a + 1) * nb], sm[:, 0, a * nb:(a + 1) * nb], HD ** -0.5,
                                           par[:, bass.ds(i * 2 + (l * PL + P_SINK + a), 1)], ALU.mult, ALU.max)
                link(last)
                V.tensor_scalar(sm[:, 1, 0:2 * nb], sm[:, 1, 0:2 * nb], -1.0, None, ALU.mult)\
                    .then_inc(sem("swa_m"), 1)
                dve.wait_ge(sem("swa_e"), t + 1)
                link(V.tensor_tensor(sm[:, 4, 0:2 * nb], sm[:, 2, 0:2 * nb], sm[:, 3, 0:2 * nb], ALU.add))
                link(V.reciprocal(sm[:, 5, 0:2 * nb], sm[:, 4, 0:2 * nb]))
                for j in range(2 * nb):
                    n = TOK if blocks[j % nb] >= 2 else CTX
                    V.tensor_scalar(SC[:, 6 + j, 0:n], SC[:, 6 + j, 0:n], sm[:, 5, j:j + 1], None, ALU.mult)\
                        .then_inc(sem("swa_p"), 1)
                dve.wait_ge(sem("swa_ge"), t + 1)
                sigmoid_tail(SC[:, 22:24, lo:])
                link(V.tensor_tensor(SC[:, 22:24, lo:], SC[:, 22:24, lo:],
                                     act[:, bass.ds(i * 2 + Y_SWA, 2), lo:], ALU.mult))
                for a in range(2):
                    dve.wait_ge(sem("swa_o"), 2 * t + a + 1)
                    last = V.tensor_tensor(act[:, i * 2 + (Y_SWA + a), lo:], ps[(4, 7)[a]][:, lo:],
                                           SC[:, 22 + a, lo:], ALU.mult)
                last.then_inc(sem("swa_y"), 1)
                dve.wait_ge(sem("swa_y"), t + 1)

            def shortconv(i, t, l, lo):
                def wcol(tap):
                    return par[:, bass.ds(i * 3 + (l * PL + P_SCW + tap), 1)]
                s0 = lo // 256

                def tap(dst, src, wc, sh):
                    d, s = two(dst)[:, s0:, :], two(src)[:, s0:, :]
                    a, b = max(0, -sh), SEQ - max(0, sh)
                    return V.scalar_tensor_tensor(d[:, :, a:b], s[:, :, a + sh:b + sh], wc, d[:, :, a:b],
                                                  ALU.mult, ALU.add)
                link(V.tensor_tensor(SC[:, 0, lo:], act[:, i + 12, lo:], act[:, i + 16, lo:], ALU.mult))
                link(V.tensor_scalar(SC[:, 1, lo:], SC[:, 0, lo:], wcol(1), None, ALU.mult))
                link(tap(SC[:, 1, :], SC[:, 0, :], wcol(0), -1))
                link(tap(SC[:, 1, :], SC[:, 0, :], wcol(2), 1))
                dve.wait_ge(sem("sc_ge"), t + 1)
                sigmoid_tail(SC[:, 3, lo:])
                link(V.tensor_tensor(SC[:, 3, lo:], SC[:, 3, lo:], act[:, i + Y_SC, lo:], ALU.mult))
                link(V.tensor_tensor(SC[:, 1, lo:], SC[:, 1, lo:], act[:, i + 8, lo:], ALU.mult))
                V.tensor_tensor(act[:, i + Y_SC, lo:], SC[:, 1, lo:], SC[:, 3, lo:], ALU.mult)\
                    .then_inc(sem("sc_y"), 1)
                dve.wait_ge(sem("sc_y"), t + 1)

            modulation(0)
            prenorm(0, 0)
            for l in range(DEPTH):
                lo = 0 if l == 0 else CTX
                gates(l)
                o.straight()
                full = segs[(l, "small")][1] // 2
                dve.wait_ge(sem("bank0_free"), full)
                dve.wait_ge(sem("bank1_free"), full)
                dve.wait_ge(sem("gdn_eg"), l + 1)
                with dve.Fori(0, 4) as i:
                    o.round(i, GDN_DVE)
                    gdn(i, i + 4 * l, l, lo)
                o.close(4)
                full = (segs[(l, "p3")][1]) // 2
                dve.wait_ge(sem("bank0_free"), full)
                dve.wait_ge(sem("bank1_free"), full)
                with dve.Fori(0, 2) as i:
                    o.round(i, GLA_DVE)
                    gla(i, i + 2 * l, l, lo)
                o.close(2)
                blocks = list(range(4)) if l == 0 else [2, 3]
                with dve.Fori(0, 2) as i:
                    o.round(i, SWA_DVE)
                    swa(i, i + 2 * l, l, lo, blocks)
                o.close(2)
                swb[0] += 4 * len(blocks)
                full = (segs[(l, "out")][1]) // 2
                dve.wait_ge(sem("bank0_free"), full)
                dve.wait_ge(sem("bank1_free"), full)
                with dve.Fori(0, 4) as i:
                    o.round(i, SC_DVE)
                    shortconv(i, i + 4 * l, l, lo)
                o.close(4)
                dve.wait_ge(sem("rstd_ready"), 2 * l + 2)
                n = segs[(l, "out")][1] + 16
                dve.wait_ge(sem("bank0_free"), n // 2)
                dve.wait_ge(sem("bank1_free"), n // 2)
                with dve.Fori(0, KT) as k:
                    for hf in range(l, 2):
                        s = slice(hf * 256, hf * 256 + 256)
                        last = V.scalar_tensor_tensor(act[:, k, s], act[:, k, s],
                                                      modG[:, l, k, hf:hf + 1], SC[:, 3, s], ALU.mult, ALU.mult)
                    last.then_inc(sem("yo_scaled"), 1)
                dve.wait_ge(sem("yo_scaled"), KT * (l + 1))
                dve.sem_inc(sem("rstd_used"), 1)
                if l == 0:
                    modulation(1)
                    prenorm(1, 2)

        @block.gpsimd
        def _(pool):
            G = nc.gpsimd
            o = Order(pool, sem("pool_order"))

            def link(ins):
                o.done(ins)
                o.wait()
            G.memset(wdec[:, :, :], 0.0).then_inc(sem("wdec_zero"), 1)
            pool.wait_ge(sem("con_in"), 16)

            def square_sum(lo):
                for k in range(KT):
                    if k == 0:
                        link(G.tensor_tensor(SC[:, 0, lo:], N[:, 0, lo:], N[:, 0, lo:], ALU.mult))
                    else:
                        link(G.tensor_tensor(SC[:, 1, lo:], N[:, k, lo:], N[:, k, lo:], ALU.mult))
                        link(G.tensor_tensor(SC[:, 0, lo:], SC[:, 0, lo:], SC[:, 1, lo:], ALU.add))
                pool.sem_inc(sem("sumsq_ready"), 1)

            pool.wait_ge(sem("bank0_free"), 8)
            pool.wait_ge(sem("bank1_free"), 8)
            pool.sem_inc(sem("h_ready"), 1)
            square_sum(0)

            def gdn(i, t, l):
                rg = SC[:, 18:20, :].rearrange("p d (c t) -> p d c t", t=128)
                for d in range(2):
                    last = G.tensor_tensor(rg[:, d], over(cm(CUM[d])), along(g[:, i, d, :]), ALU.mult)
                last.then_inc(sem("gdn_rg"), 1)
                pool.wait_ge(sem("gdn_E"), t + 1)
                strict = (C_TAILB, C_TAILF)
                for d in range(2):
                    G.tensor_tensor(chunks(SC[:, 22 + d, :]), chunks(SC[:, 20 + d, :]), over(cm(strict[d])), ALU.mult)
                for d in range(2):
                    last = G.tensor_tensor(chunks(SC[:, 20 + d, :]), chunks(SC[:, 20 + d, :]), over(cm(CUM[d])),
                                           ALU.mult)
                last.then_inc(sem("gdn_Em"), 1)
                pool.wait_ge(sem("gdn_rn"), t + 1)
                G.tensor_tensor(ks[:, 0, :, :], beta[:, i, :, :], over(rn[:, 1, :], 2), ALU.mult)
                G.tensor_copy(tot[:, :, :], eg[:, :, 2, i, :])
                link(G.tensor_scalar(rq[:, :], rn[:, 0, :], HD ** -0.5, None, ALU.mult))
                G.tensor_tensor(ks[:, 1, :, :], eg[:, :, 0, i, :], over(rq[:, :], 2), ALU.mult)
                G.tensor_tensor(ks[:, 2, :, :], eg[:, :, 1, i, :], over(rn[:, 1, :], 2), ALU.mult)
                G.tensor_tensor(ks[:, 3, :, :], beta[:, i, :, :], eg[:, :, 0, i, :], ALU.mult)\
                    .then_inc(sem("gdn_ks"), 1)
                pool.wait_ge(sem("gdn_ks"), t + 1)
                pool.wait_ge(sem("gdn_tokc"), t + 1)
                pool.wait_ge(sem("gdn_ss"), t + 1)
                for d in range(2):
                    last = G.tensor_tensor(chunks(SC[:, d, :]), chunks(SC[:, 3, :]), along(ks[:, 1, d, :]), ALU.mult)
                last.then_inc(sem("gdn_sc"), 1)
                for d in range(2):
                    G.tensor_tensor(chunks(SC[:, 12 + d, :]), chunks(SC[:, 5, :]), along(beta[:, i, d, :]), ALU.mult)
                    last = G.tensor_tensor(chunks(SC[:, 10 + d, :]), chunks(SC[:, 4, :]), along(ks[:, 2, d, :]),
                                           ALU.mult)
                level0 = (C_UP, C_LO)
                pool.wait_ge(sem("gdn_T1"), 4 * t + 4)
                for d in range(2):
                    pool.wait_ge(sem("gdn_U"), 2 * t + d + 1)
                    link(G.tensor_tensor(chunks(SC[:, 8 + d, :]), chunks(SC[:, 22 + d, :]), over(cm(level0[d])),
                                         ALU.mult))
                    G.tensor_tensor(chunks(SC[:, 8 + d, :]), over(ident), chunks(SC[:, 8 + d, :]), ALU.subtract)\
                        .then_inc(sem("gdn_M0"), 1)
                pool.wait_ge(sem("gdn_y"), t + 1)

            for l in range(DEPTH):
                lo = 0 if l == 0 else CTX
                pool.wait_ge(sem("beta_ready"), l + 1)
                pool.wait_ge(sem("gdn_eg"), l + 1)
                o.straight()
                with pool.Fori(0, 4) as i:
                    o.round(i, GDN_POOL)
                    gdn(i, i + 4 * l, l)
                o.close(4)
                n = segs[(l, "p3")][1]
                pool.wait_ge(sem("bank0_free"), n // 2)
                pool.wait_ge(sem("bank1_free"), n // 2)
                pool.wait_ge(sem("wdec_in"), 32 * (l + 1))
                with pool.Fori(0, 2) as i:
                    t = i + 2 * l
                    G.tensor_copy(wdp, wdec[:, :, bass.ds(i * 128, 128)])
                    G.tensor_copy(SC[:, 16:18, :], act[:, bass.ds(i * 2 + (T_B + 4), 2), :]).then_inc(sem("gla_stat"), 1)
                    pool.wait_ge(sem("gla_ek"), t + 1)
                    for d in range(2):
                        last = G.tensor_tensor(SC[:, 12 + d, :], act[:, i + (T_B + 2), :], SC[:, 8 + d, :], ALU.mult)
                    last.then_inc(sem("gla_kd"), 1)
                    pool.wait_ge(sem("gla_y"), t + 1)
                n = segs[(l, "p4")][1]
                pool.wait_ge(sem("bank0_free"), n // 2)
                pool.wait_ge(sem("bank1_free"), n // 2)
                with pool.Fori(0, 2) as i:
                    t = i + 2 * l
                    G.tensor_copy(SC[:, 0:2, :], act[:, bass.ds(i * 2, 2), :])
                    G.tensor_copy(SC[:, 2, :], act[:, i + 4, :])
                    G.tensor_copy(SC[:, 3, :], act[:, i + 6, :]).then_inc(sem("swa_stat"), 1)
                    pool.wait_ge(sem("swa_y"), t + 1)
                pool.wait_ge(sem("sc_y"), 4 * l + 4)
                link(G.memset(SC[:, 0, lo:], 0.0))
                if l == 0:
                    pool.sem_inc(sem("yo_round"), 1)
                n = segs[(l, "out")][1]
                o.straight()
                with pool.Fori(0, 4) as i:
                    for tt in range(4):
                        b = (n + tt) % 2
                        pool.wait_ge(sem(f"bank{b}_free"), i * 2 + ((n + tt) // 2 + 1))
                        G.tensor_tensor(SC[:, 0, lo:], SC[:, 0, lo:], SC[:, 4 + tt % 2, lo:], ALU.add)\
                            .then_inc(sem("yo_add"), 1)
                        pool.wait_ge(sem("yo_add"), i * 4 + (16 * l + tt + 1))
                    pool.sem_inc(sem("yo_round"), 1)
                pool.sem_inc(sem("sumsq_ready"), 1)
                pool.wait_ge(sem("h_back"), 16 * (l + 1))
                with pool.Fori(0, KT) as k:
                    pool.wait_ge(sem("yo_scaled"), k + (KT * l + 1))
                    G.tensor_tensor(N[:, k, lo:], N[:, k, lo:], act[:, k, lo:], ALU.add).then_inc(sem("h_add"), 1)
                pool.wait_ge(sem("h_add"), KT * (l + 1))
                pool.sem_inc(sem("yo_used"), 1)
                pool.sem_inc(sem("h_ready"), 1)
                if l == 0:
                    pool.wait_ge(sem("chansum_done"), 2)
                    square_sum(0)


GDN_DVE = 23
GLA_DVE = 12
SWA_DVE = 8
SC_DVE = 8
GDN_POOL = 3


def kernel(**inputs):
    import concourse.bacc as bacc
    from concourse.bass_utils import run_bass_kernel_spmd

    nc = bacc.Bacc("TRN2", target_bir_lowering=False, num_devices=1)
    f32 = mybir.dt.float32
    arrays = {
        "x": np.asarray(inputs["x"]).reshape(SEQ, D),
        "ctx": np.asarray(inputs["ctx"]).reshape(CTX, D),
        "ada_w": np.asarray(inputs["ada_w"]),
        "w_in": np.asarray(inputs["w_in"]),
        "w_out": np.asarray(inputs["w_out"]),
        "w_decay": np.asarray(inputs["gla_w_decay"]),
        "params": parameters(inputs),
        "consts": constants(),
    }
    args = [nc.dram_tensor(n, a.shape, f32, kind="ExternalInput").ap() for n, a in arrays.items()]
    out = nc.dram_tensor("out", (SEQ, D), f32, kind="ExternalOutput").ap()
    build(nc, *args, out)
    r = run_bass_kernel_spmd(nc, [arrays], core_ids=[0])
    return r.results[0]["out"].reshape(1, SEQ, D)
```

```python
import numpy as np
import concourse.bass as bass
from concourse import mybir
from contextlib import ExitStack

D = 2048
SEQ = 256
CTX = 256
TOK = SEQ + CTX
DEPTH = 2
KT = D // 128
HD = 128
CH = 128
NC = TOK // CH
EPS = 1e-6
GRID_W = 64
ROPE_BASE = 10000.0
NEG = -1e30

GLA_QKV, GLA_LR, GLA_GATE = 0, 1024, 1056
GDN_QKV, GDN_AB, GDN_GATE = 1568, 3104, 3120
SC_ALL = 3632
SWA_QKV, SWA_GATE = 5680, 6704
IN_WIDTH = 7216
NLR, NAB = 32, 16

T_A, T_B = 0, 12
Y_GLA, Y_SWA, Y_GDN, Y_SC = 20, 24, 28, 32
NTILES = 36
Y_ORDER = [Y_GLA + i for i in range(4)] + [Y_GDN + i for i in range(4)] + \
          [Y_SC + i for i in range(4)] + [Y_SWA + i for i in range(4)]
RING = 4
WSCALE = 256.0
CLAMP = -40.0

C_IDENT, C_ONES, C_PERM = 0, 128, 256
C_CUMF, C_CUMB, C_TAILF, C_TAILB = 384, 512, 640, 768
C_LO = 896
C_UP = C_LO + 7 * 128
C_COS = C_UP + 7 * 128
C_SIN = C_COS + SEQ
C_MASK = C_SIN + SEQ
C_SEG = C_MASK + 2 * SEQ
C_EPS = C_SEG + TOK
C_ZERO = C_EPS + 1
C_ONE = C_EPS + 2
C_SEL = C_EPS + 3
CW = C_EPS + 5

P_ADAB, P_NPRE, P_NPOST = 0, 48, 64
P_GLAB, P_GLAN = 80, 84
P_CONV, P_GDNN = 85, 145
P_SCW, P_ALOG, P_DT, P_SINK = 146, 158, 166, 174
PL = 178
P_C = DEPTH * PL
PW = P_C + 2 * KT


def constants():
    c = np.zeros((128, CW), np.float32)
    p = np.arange(128)[:, None]
    f = np.arange(128)[None, :]
    c[:, C_IDENT:C_IDENT + 128] = p == f
    c[:, C_ONES:C_ONES + 128] = 1.0
    swap = (f // 64) * 64 + (f % 64 + 32) % 64
    c[:, C_PERM:C_PERM + 128] = p == swap
    c[:, C_CUMF:C_CUMF + 128] = p <= f
    c[:, C_CUMB:C_CUMB + 128] = p >= f
    c[:, C_TAILF:C_TAILF + 128] = p > f
    c[:, C_TAILB:C_TAILB + 128] = p < f
    for lv in range(7):
        lo = (p >> (lv + 1) == f >> (lv + 1)) & ((p >> lv & 1) == 1) & ((f >> lv & 1) == 0)
        c[:, C_LO + 128 * lv:C_LO + 128 * lv + 128] = lo
        c[:, C_UP + 128 * lv:C_UP + 128 * lv + 128] = lo.T
    t = np.arange(SEQ)
    inv = ROPE_BASE ** (-np.arange(0, 64, 2, dtype=np.float64) / 64)
    for half, pos in ((0, t // GRID_W), (1, t % GRID_W)):
        ang = inv[:, None] * pos[None, :]
        for q, sign in ((0, -1.0), (1, 1.0)):
            r = half * 64 + q * 32
            c[r:r + 32, C_COS:C_COS + SEQ] = np.cos(ang)
            c[r:r + 32, C_SIN:C_SIN + SEQ] = sign * np.sin(ang)
    for b in range(2):
        far = np.abs(128 * b + p - t[None, :]) > 128
        c[:, C_MASK + b * SEQ:C_MASK + (b + 1) * SEQ] = np.where(far, NEG, 0.0)
    c[:, C_SEG:C_SEG + TOK] = (np.arange(TOK) % CH != 0)
    c[:, C_EPS] = EPS
    c[:, C_ONE] = 1.0
    c[:, C_SEL:C_SEL + 2] = p % 32 == f[:, 0:2]
    return c


def parameters(i):
    def chan(a):
        return np.ascontiguousarray(np.asarray(a, np.float32).reshape(-1, 128).T)

    def rep(a):
        a = np.asarray(a, np.float32).reshape(1, -1)
        return np.repeat(a, 128, axis=0)
    cols = []
    for l in range(DEPTH):
        cols += [chan(i["ada_b"][l]), chan(i["norm_pre"][l]), chan(i["norm_post"][l]),
                 chan(i["gla_b_decay"][l]), chan(i["gla_norm"][l]),
                 np.asarray(i["gdn_conv"][l]).reshape(5, 12, 128).transpose(2, 1, 0).reshape(128, 60),
                 chan(i["gdn_norm"][l]),
                 np.asarray(i["sc_conv"][l]).reshape(3, 4, 128).transpose(2, 1, 0).reshape(128, 12),
                 rep(i["gdn_a_log"][l]), rep(i["gdn_dt_bias"][l]), rep(i["swa_sink"][l])]
    cc = np.stack([np.asarray(i["c_ctx"]).reshape(KT, 128), np.asarray(i["c"]).reshape(KT, 128)], 0)
    cols.append(cc.transpose(2, 1, 0).reshape(128, 2 * KT))
    return np.ascontiguousarray(np.concatenate(cols, axis=1))


class Order:

    def __init__(self, eng, sem):
        self.eng, self.sem, self.base, self.k, self.n, self.i = eng, sem, 0, 0, 0, 0

    def round(self, i, n):
        self.i, self.n, self.k = i, n, 0

    def done(self, ins):
        ins.then_inc(self.sem, 1)
        self.k += 1
        return self.k

    def wait(self, k=None):
        self.eng.wait_ge(self.sem, self.i * self.n + (self.base + (self.k if k is None else k)))

    def straight(self):
        self.base += self.k
        self.i = self.n = self.k = 0

    def close(self, rounds):
        assert self.k == self.n, f"{self.k} steps in a round, {self.n} declared"
        self.base += rounds * self.n
        self.i = self.n = self.k = 0


def build(nc, x_d, ctx_d, ada_d, win_d, wout_d, wdec_d, par_d, con_d, out_d):
    f32, f16 = mybir.dt.float32, mybir.dt.float16
    ALU = mybir.AluOpType
    ACT = mybir.ActivationFunctionType
    AX = mybir.AxisListType.X
    es = ExitStack()
    with es:
        def sb(name, shape):
            return es.enter_context(nc.sbuf_tensor(name, shape, f32))

        sems = {}

        def sem(name):
            if name not in sems:
                sems[name] = es.enter_context(nc.semaphore(name))
            return sems[name]

        con = sb("con", [128, CW])
        par = sb("par", [128, PW])
        N = sb("N", [128, KT, TOK])
        act = sb("act", [128, NTILES, TOK])
        ring = sb("ring", [128, RING, KT, 128])
        wdec = sb("wdec", [NLR, 2, 256])
        wab = act[:, Y_SC, 0:KT * NAB].rearrange("p (k n) -> p k n", n=NAB)
        wlr = act[:, Y_SC + 1, 0:KT * NLR].rearrange("p (k n) -> p k n", n=NLR)
        lrT = act[0:NLR, Y_SC + 3, :]
        wdp = act[0:NLR, Y_SC + 2, 0:256].rearrange("r (d n) -> r d n", d=2)
        SC = sb("SC", [128, 24, TOK])
        ab = act[:, Y_SC + 2, 256:256 + NC * NAB].rearrange("p (c k) -> p c k", k=NAB)
        wab16 = act[:, Y_SC, 256:512].bitcast(f16).rearrange("p (h k n) -> p h k n", h=2, n=NAB)
        wlr16 = act[:, Y_SWA, :].bitcast(f16).rearrange("p (h k n) -> p h k n", h=2, n=NLR)
        st = SC[:, 6, 0:256].rearrange("p (d v) -> p d v", d=2)
        vn = SC[:, 6, 256:512].rearrange("p (d v) -> p d v", d=2)
        rr = SC[:, 7, 0:256].rearrange("p (d v) -> p d v", d=2)
        cs = sb("cs", [128, KT, 2])
        csp = SC[:, 7, :].rearrange("p (k m) -> p k m", m=32)
        cst = sb("cst", [128, KT, 2])
        ada = sb("ada", [128, DEPTH, 48, 2])
        modA = sb("modA", [128, DEPTH, KT, 2])
        modG = sb("modG", [128, DEPTH, KT, 2])
        gz = sb("gz", [128, NC, 2, 4])
        gt = sb("gt", [128, NC, 2, 4])
        expA = sb("expA", [128, 2, 4])
        g = sb("g", [128, 4, 2, NC])
        beta = sb("beta", [128, 4, 2, NC])
        eg = sb("eg", [128, 2, 3, 4, NC])
        rn = sb("rn", [128, 2, NC])
        rq = sb("rq", [128, NC])
        ks = sb("ks", [128, 4, 2, NC])
        tot = sb("tot", [128, 2, NC])
        gs = sb("gs", [128, 3, 2, NC])
        gd = sb("gd", [128, 2, NC])
        sm = sb("sm", [128, 6, 8])
        ps = [es.enter_context(nc.psum_tensor(f"bank{i}", [128, 512], f32)) for i in range(8)]
        h_d = nc.dram_tensor("h_spill", (128, KT * TOK), f32, kind="Internal").ap()

        ident = con[:, C_IDENT:C_IDENT + 128]
        ones = con[:, C_ONES:C_ONES + 128]
        one1 = con[:, C_ONE:C_ONE + 1]
        eps = con[:, C_EPS:C_EPS + 1]
        CUM = (C_CUMF, C_CUMB)
        TAIL = (C_TAILF, C_TAILB)

        def cm(at):
            return con[:, at:at + 128]

        def over(a, n=NC):
            return a.unsqueeze(1).to_broadcast([128, n, a.shape[1]])

        def along(a, m=128):
            return a.unsqueeze(2).to_broadcast([128, a.shape[1], m])

        def chunks(a):
            return a.rearrange("p (c t) -> p c t", t=128)

        def pair(a):
            return a.bitcast(f16).rearrange("p (h t) -> p h t", h=2)

        def halves(s):
            return ring[:, 2 + s, :, :].rearrange("p k n -> p (k n)").bitcast(f16)\
                .rearrange("p (k h n) -> p k h n", h=2, n=128)

        def P(l, at, n=1):
            return par[:, l * PL + at:l * PL + at + n]

        def bank_wait(pe, n0, i, tb, tt):
            pe.wait_ge(sem(f"bank{(n0 + tt) % 2}_free"), i * (tb // 2) + (n0 + tt) // 2)

        def out_wait(eng, n0, i, tb, tt):
            eng.wait_ge(sem(f"bank{(n0 + tt) % 2}_full"), i * (tb // 2) + ((n0 + tt) // 2 + 1))

        segs = {}
        seq = []
        wt0, n0 = 0, 16
        for l in range(DEPTH):
            for name, dram, col, tiles in (
                    [("ada0", None, 0, 24)] if l == 0 else []) + [
                    ("gdn", win_d[l], GDN_QKV, 12), ("gdng", win_d[l], GDN_GATE, 4),
                    ("small", None, 0, 2),
                    ("p2", None, 0, 16), ("p3", win_d[l], SWA_QKV, 8), ("p4", win_d[l], SC_ALL, 16),
                    ("out", wout_d[l], 0, 16)] + ([("ada1", None, 0, 24)] if l == 0 else []):
                segs[(l, name)] = (wt0, n0)
                if name == "p2":
                    seq += [(win_d[l], GLA_QKV, 8), (win_d[l], GLA_GATE, 4), (win_d[l], SWA_GATE, 4)]
                elif dram is not None:
                    seq.append((dram, col, tiles))
                if name[:3] != "ada" and name != "small":
                    wt0 += tiles
                n0 += tiles
        segs["end"] = (wt0, n0)

        block = es.enter_context(nc.Block())

        @block.sync
        def _(sp):
            sp.dma_start(con[:, :], con_d).then_inc(sem("con_in"), 16)
            sp.dma_start(par[:, :], par_d).then_inc(sem("par_in"), 16)
            xin = act[:, 0:16, :].rearrange("p a t -> p (a t)").rearrange("p (b d) -> p b d", b=4)
            sp.dma_start(xin[:, 0:2, :], ctx_d.rearrange("(b p) d -> p b d", p=128)).then_inc(sem("x_in"), 16)
            sp.dma_start(xin[:, 2:4, :], x_d.rearrange("(b p) d -> p b d", p=128)).then_inc(sem("x_in"), 16)
            sp.wait_ge(sem("wdec_zero"), 1)

            def ada_weights(l):
                if l:
                    sp.wait_ge(sem("layer_multiplied"), l)
                with sp.Fori(0, 12) as i:
                    for s in range(RING):
                        sp.wait_ge(sem(f"slot{s}_free"), i + (12 * l + 1))
                        sp.dma_start(ring[:, s, :, :], ada_d[l][:, bass.ds(i * (RING * 128) + s * 128, 128)]
                                     .rearrange("(k p) n -> p k n", p=128)).then_inc(sem(f"slot{s}_full"), 16)
                for s in range(2):
                    sp.wait_ge(sem(f"slot{s}_free"), 12 * (l + 1) + 1)

            def weights(dram, col, tiles, base):
                with sp.Fori(0, tiles // RING) as i:
                    for tt in range(RING):
                        sp.wait_ge(sem(f"stage{tt % 2}_split"), i * (RING // 2) + ((base + tt) // 2 + 1))
                        src = dram[:, bass.ds(i * (RING * 128) + (col + tt * 128), 128)]
                        sp.dma_start(ring[:, tt % 2, :, :], src.rearrange("(k p) n -> p k n", p=128))\
                            .then_inc(sem(f"stage{tt % 2}_full"), 16)

            base = 0
            it = iter(seq)

            def nxt(count):
                nonlocal base
                for _ in range(count):
                    dram, col, tiles = next(it)
                    weights(dram, col, tiles, base)
                    base += tiles

            for l in range(DEPTH):
                sp.wait_ge(sem("yo_used"), l)
                sp.dma_start(wab, win_d[l][:, GDN_AB:GDN_AB + NAB].rearrange("(k p) n -> p k n", p=128))\
                    .then_inc(sem("small_in"), 16)
                sp.dma_start(wlr, win_d[l][:, GLA_LR:GLA_LR + NLR].rearrange("(k p) n -> p k n", p=128))\
                    .then_inc(sem("small_in"), 16)
                if l:
                    sp.wait_ge(sem("gla_stat"), 2 * l)
                for d in range(2):
                    sp.dma_start(wdec[16 * d:16 * d + 16, d, :], wdec_d[l, d]).then_inc(sem("wdec_in"), 16)
                if l == 0:
                    ada_weights(0)
                sp.wait_ge(sem("h_ready"), l + 1)
                sp.dma_start(h_d, N[:, :, :].rearrange("p k t -> p (k t)")).then_inc(sem("h_saved"), 16)
                nxt(2 + 3 + 1 + 1)
                sp.wait_ge(sem("norm_used"), l + 1)
                sp.wait_ge(sem("h_saved"), 16 * (l + 1))
                sp.dma_start(N[:, :, :].rearrange("p k t -> p (k t)"), h_d).then_inc(sem("h_back"), 16)
                nxt(1)
                if l == 0:
                    ada_weights(1)
            for b in range(2):
                sp.wait_ge(sem("out_staged"), 4 * b + 4)
                sp.dma_start(out_d[b * 128:(b + 1) * 128, :],
                             act[:, 4 * b:4 * b + 4, :].rearrange("p a t -> p (a t)")).then_inc(sem("out_sent"), 16)
            sp.wait_ge(sem("out_sent"), 32)

        @block.tensor
        def _(pe):
            def mm(out, a, b, start=True, stop=True):
                return nc.tensor.matmul(out, a, b, start=start, stop=stop, skip_group_check=True)

            def tp(out, a):
                return nc.tensor.transpose(out, a, ident[0:a.shape[0], 0:a.shape[0]])

            def pairs(out, ah, al, bh, bl, first, last):
                mm(out, ah, bh, first, False)
                mm(out, ah, bl, False, False)
                return mm(out, al, bh, False, last)

            def ada_rows(l):
                n = segs[(0, f"ada{l}")][1]
                with pe.Fori(0, 12) as i:
                    bank_wait(pe, n, i, 2, 0)
                    for s in range(RING):
                        pe.wait_ge(sem(f"slot{s}_full"), i * 16 + 16 * (12 * l + 1))
                        for k in range(KT):
                            j = k % 4
                            last = mm(ps[0][32 * j:32 * j + 32, s * 128:(s + 1) * 128], csp[:, k, :],
                                      ring[:, s, k, :], k < 4, k >= KT - 4)
                        last.then_inc(sem(f"slot{s}_free"), 1)
                    pe.wait_ge(sem("slot3_free"), i + (12 * l + 2))
                    pe.sem_inc(sem("bank0_full"), 1)
                    bank_wait(pe, n, i, 2, 1)
                    pe.wait_ge(sem("bank0_free"), i + (n // 2 + 1))
                    for s in range(RING):
                        last = mm(ps[1][:, 2 * s:2 * s + 2], SC[:, 6, s * 128:(s + 1) * 128],
                                  con[:, C_SEL:C_SEL + 2])
                    last.then_inc(sem("bank1_full"), 1)

            class Fill:

                def __init__(self, l, name, tb, i, lo, rhs=None, off=0):
                    self.wt0, self.n0 = segs[(l, name)]
                    self.n0 += off
                    self.wt0 += off
                    self.tb, self.i, self.lo, self.at = tb, i, lo, 0
                    self.rhs = rhs or (lambda k: pair(N[:, k, :])[:, :, lo:])

                def __call__(self, steps):
                    for _ in range(steps):
                        if self.at == self.tb * KT:
                            return
                        tt, k = divmod(self.at, KT)
                        s = tt % 2
                        if k == 0:
                            pe.wait_ge(sem(f"stage{s}_split"),
                                       self.i * (self.tb // 2) + ((self.wt0 + tt) // 2 + 2))
                            bank_wait(pe, self.n0, self.i, self.tb, tt)
                        w = halves(s)
                        x = self.rhs(k)
                        b = (self.n0 + tt) % 2
                        last = pairs(ps[b][:, 0:x.shape[-1]], w[:, k, 0, :], w[:, k, 1, :], x[:, 0, :], x[:, 1, :],
                                     k == 0, k == KT - 1)
                        if k == KT - 1:
                            last.then_inc(sem(f"bank{b}_full"), 1)
                        self.at += 1

                def rest(self):
                    self(self.tb * KT - self.at)

            def project(l, name, tiles, tb=RING, lo=0, rhs=None, off=0):
                with pe.Fori(0, tiles // tb) as i:
                    Fill(l, name, tb, i, lo, rhs, off).rest()

            for s in range(RING):
                pe.sem_inc(sem(f"slot{s}_free"), 1)
            pe.wait_ge(sem("con_in"), 16)
            pe.wait_ge(sem("x_in"), 32)
            xin = act[:, 0:16, :].rearrange("p a t -> p (a t)").rearrange("p (b d) -> p b d", b=4)
            for k in range(KT):
                bank_wait(pe, 0, 0, KT, k)
                for b in range(4):
                    last = tp(ps[k % 2][:, b * 128:(b + 1) * 128], xin[:, b, k * 128:(k + 1) * 128])
                last.then_inc(sem(f"bank{k % 2}_full"), 1)
            pe.wait_ge(sem("cs_ready"), 1)
            ada_rows(0)

            def channel_sum(t, width0):
                pe.wait_ge(sem("sumsq_ready"), t + 1)
                mm(ps[2][:, width0:], ones, SC[:, 0, width0:]).then_inc(sem("chansum_done"), 1)

            def gdn(i, t, fill):
                pe.wait_ge(sem("gdn_rg"), t + 1)
                for d in range(2):
                    last = mm(ps[5 + d][:, :], cm(TAIL[d]), SC[:, 18 + d, :])
                last.then_inc(sem("gdn_D"), 1)
                fill(6)
                pe.wait_ge(sem("gdn_x"), t + 1)
                for j in range(3):
                    for c in range(NC):
                        last = tp(ps[2 + j][:, c * 128:(c + 1) * 128], SC[:, j, c * 128:(c + 1) * 128])
                last.then_inc(sem("gdn_tok"), 1)
                pe.wait_ge(sem("gdn_sq"), t + 1)
                for j in range(2):
                    for c in range(NC):
                        last = mm(ps[7][:, j * NC + c:j * NC + c + 1], SC[:, 8 + j, c * 128:(c + 1) * 128], one1)
                last.then_inc(sem("gdn_ss"), 1)
                fill(6)
                pe.wait_ge(sem("gdn_kn"), t + 1)
                pe.wait_ge(sem("gdn_E"), t + 1)
                for src, b in ((7, 5), (8, 2), (9, 3), (6, 6)):
                    for c in range(NC):
                        last = tp(ps[b][:, c * 128:(c + 1) * 128], SC[:, src, c * 128:(c + 1) * 128])
                    last.then_inc(sem("gdn_T1"), 1)
                fill(4)
                pe.wait_ge(sem("gdn_T1c"), 4 * t + 4)
                for a, b, bank in ((14, 15, 5), (14, 16, 4), (14, 17, 7)):
                    for c in range(NC):
                        s = slice(c * 128, (c + 1) * 128)
                        last = mm(ps[bank][:, s], SC[:, a, s], SC[:, b, s])
                    last.then_inc(sem("gdn_G"), 1)
                pe.wait_ge(sem("gdn_sc"), t + 1)
                for d, bank in ((0, 6), (1, 2)):
                    for c in range(NC):
                        last = tp(ps[bank][:, c * 128:(c + 1) * 128], SC[:, d, c * 128:(c + 1) * 128])
                    last.then_inc(sem("gdn_T2"), 1)
                fill(2)
                pe.wait_ge(sem("gdn_U"), 2 * t + 2)
                for d, bank in ((0, 3), (1, 4)):
                    for c in range(NC):
                        s = slice(c * 128, (c + 1) * 128)
                        last = tp(ps[bank][:, s], SC[:, 22 + d, s])
                    last.then_inc(sem("gdn_P"), 1)
                fill(2)
                pe.wait_ge(sem("gdn_T2c"), 2 * t + 2)
                for lv in range(1, 7):
                    for d in range(2):
                        pe.wait_ge(sem("gdn_T"), 12 * t + 2 * (lv - 1) + d + 1)
                        if lv == 1 and d == 1:
                            pe.wait_ge(sem("gdn_T"), 12 * t + 2)
                        for c in range(NC):
                            s = slice(c * 128, (c + 1) * 128)
                            last = mm(ps[2 + d][:, s], SC[:, 22 + d, s], SC[:, 6 + d, s])
                        last.then_inc(sem("gdn_P"), 1)
                    fill(3)
                    for d in range(2):
                        pe.wait_ge(sem("gdn_Pm"), 12 * t + 2 * (lv - 1) + d + 1)
                        if lv == 1:
                            pe.wait_ge(sem("gdn_M0"), 2 * t + d + 1)
                        else:
                            pe.wait_ge(sem("gdn_M"), 10 * t + 2 * (lv - 2) + d + 1)
                        if lv < 6:
                            for c in range(NC):
                                s = slice(c * 128, (c + 1) * 128)
                                last = mm(ps[4 + d][:, s], SC[:, 8 + d, s], SC[:, 16 + d, s])
                            last.then_inc(sem("gdn_Y"), 1)
                        for c in range(NC):
                            s = slice(c * 128, (c + 1) * 128)
                            last = mm(ps[6 + d][:, s], SC[:, 16 + d, s], SC[:, 8 + d, s])
                        last.then_inc(sem("gdn_YT"), 1)
                    fill(3)
                pe.wait_ge(sem("gdn_Mlast"), t + 1)
                pe.wait_ge(sem("gdn_AT"), t + 1)
                first = True
                for s in range(NC):
                    cc = (s, (1, 0, 3, 2)[s])
                    if s > 0:
                        pe.wait_ge(sem("gdn_S"), 3 * t + s)
                        for d in range(2):
                            c = slice(cc[d] * 128, cc[d] * 128 + 128)
                            last = mm(ps[2][:, d * 128:d * 128 + 128], SC[:, 14, c], st[:, d, :])
                        last.then_inc(sem("gdn_KS"), 1)
                        pe.wait_ge(sem("gdn_r"), 3 * t + s)
                    for d in range(2):
                        c = slice(cc[d] * 128, cc[d] * 128 + 128)
                        last = mm(ps[3][:, d * 128:d * 128 + 128], SC[:, 8 + d, c],
                                  rr[:, d, :] if s else SC[:, 12 + d, c])
                    last.then_inc(sem("gdn_vn"), 1)
                    if s > 0:
                        for d in range(2):
                            c = slice(cc[d] * 128, cc[d] * 128 + 128)
                            mm(ps[5][:, c], st[:, d, :], SC[:, 18 + d, c], start=first, stop=True)
                            first = False
                    fill(1)
                    pe.wait_ge(sem("gdn_vnc"), 4 * t + s + 1)
                    if s < NC - 1:
                        for d in range(2):
                            c = slice(cc[d] * 128, cc[d] * 128 + 128)
                            last = mm(ps[4][:, d * 128:d * 128 + 128], SC[:, 10 + d, c], vn[:, d, :])
                        last.then_inc(sem("gdn_dS"), 1)
                    for d in range(2):
                        c = slice(cc[d] * 128, cc[d] * 128 + 128)
                        last = mm(ps[5][:, c], vn[:, d, :], SC[:, 20 + d, c], start=first, stop=True)
                        first = False
                    if s == NC - 1:
                        last.then_inc(sem("gdn_o"), 1)
                    fill(2)
                pe.wait_ge(sem("gdn_osq"), t + 1)
                mm(ps[6][:, :], ones, SC[:, 1, :]).then_inc(sem("gdn_oss"), 1)
                fill.rest()

            def gla(i, t, l, fill):
                pe.wait_ge(sem("gla_stat"), t + 1)
                pe.wait_ge(sem("lr_copied"), l + 1)
                for d in range(2):
                    last = mm(ps[2 + d][:, :], wdp[:, d, :], lrT)
                last.then_inc(sem("gla_z"), 1)
                for a in range(2):
                    for c in range(NC):
                        s = slice(c * 128, (c + 1) * 128)
                        last = tp(ps[4 + a][:, s], SC[:, 16 + a, s])
                last.then_inc(sem("gla_vt"), 1)
                fill(40)
                pe.wait_ge(sem("gla_kd"), t + 1)
                pe.wait_ge(sem("gla_zc"), t + 1)
                for d in range(2):
                    for c in range(NC):
                        s = slice(c * 128, (c + 1) * 128)
                        last = tp(ps[2 + d][:, s], SC[:, 12 + d, s])
                last.then_inc(sem("gla_kt"), 1)
                pe.wait_ge(sem("gla_qd"), t + 1)
                for a in range(2):
                    for d in range(2):
                        bank = (6, 7, 2, 3)[2 * a + d]
                        if a == 1 and d == 0:
                            fill(10)
                            pe.wait_ge(sem("gla_ktc"), t + 1)
                        for c in range(NC):
                            s = slice(c * 128, (c + 1) * 128)
                            last = mm(ps[bank][:, s], SC[64 * a:64 * a + 64, 12 + d, s],
                                      SC[64 * a:64 * a + 64, 10 + d, s])
                        last.then_inc(sem("gla_att"), 1)
                pe.wait_ge(sem("gla_vtc"), t + 1)
                for d in range(2):
                    for a in range(2):
                        for c in range(NC):
                            s = slice(c * 128, (c + 1) * 128)
                            last = mm(ps[4 + d][64 * a:64 * a + 64, s],
                                      SC[:, 14 + d, c * 128 + 64 * a:c * 128 + 64 * a + 64], SC[:, 18 + a, s])
                last.then_inc(sem("gla_dS"), 1)
                fill(30)
                pe.wait_ge(sem("gla_S"), t + 1)
                pe.wait_ge(sem("gla_AT"), t + 1)
                for a in range(2):
                    first = True
                    for c in range(NC):
                        s = slice(c * 128, (c + 1) * 128)
                        for d in range(2):
                            last = mm(ps[6 + a][:, s], SC[:, 18 + a, s], SC[:, 20 + 2 * a + d, s], start=first)
                            first = False
                            step = (c, (1, 0, 3, 2)[c])[d]
                            if step:
                                last = mm(ps[6 + a][:, s],
                                          SC[64 * a:64 * a + 64, d, (step - 1) * 128:step * 128],
                                          SC[64 * a:64 * a + 64, 10 + d, s], start=False)
                    last.then_inc(sem("gla_o"), 1)
                fill(16)
                for a in range(2):
                    pe.wait_ge(sem("gla_osq"), 2 * t + a + 1)
                    mm(ps[2 + a][:, :], ones, SC[:, 4 + a, :]).then_inc(sem("gla_oss"), 1)
                fill.rest()

            def swa(i, t, fill, blocks):
                nb = len(blocks)
                pe.wait_ge(sem("swa_stat"), t + 1)
                for j in range(3):
                    last = mm(ps[2 + j // 2][:, (j % 2) * 256:(j % 2) * 256 + 256], cm(C_PERM), SC[:, j, CTX:])
                last.then_inc(sem("swa_rot"), 1)
                for c in range(NC):
                    s = slice(c * 128, (c + 1) * 128)
                    last = tp(ps[4][:, s], SC[:, 3, s])
                last.then_inc(sem("swa_vt"), 1)
                fill(10)
                pe.wait_ge(sem("swa_rope"), t + 1)
                sc0 = swa_base["score"]
                for j, (a, b) in enumerate((a, b) for a in range(2) for b in blocks):
                    n = TOK if b >= 2 else CTX
                    if j >= 2:
                        pe.wait_ge(sem("swa_sc"), t2(t) * 2 * nb + (swa_base["score"] + j - 1))
                    mm(ps[5 + j % 2][:, 0:n], SC[:, a, b * 128:(b + 1) * 128], SC[:, 2, 0:n])\
                        .then_inc(sem("swa_s"), 1)
                fill(40)
                for j, (a, b) in enumerate((a, b) for a in range(2) for b in blocks):
                    n = TOK if b >= 2 else CTX
                    pe.wait_ge(sem("swa_p"), t2(t) * 2 * nb + (swa_base["score"] + j + 1))
                    if j >= 2:
                        pe.wait_ge(sem("swa_pTc"), t2(t) * 2 * nb + (swa_base["score"] + j - 1))
                    for c in range(n // 128):
                        last = tp(ps[2 + j % 2][:, c * 128:(c + 1) * 128], SC[:, 6 + j, c * 128:(c + 1) * 128])
                    last.then_inc(sem("swa_pT"), 1)
                    fill(3)
                    if j > 0:
                        attend(j - 1, t, blocks)
                attend(2 * nb - 1, t, blocks)
                fill.rest()

            def attend(j, t, blocks):
                nb = len(blocks)
                a, b = j // nb, blocks[j % nb]
                n = TOK if b >= 2 else CTX
                pe.wait_ge(sem("swa_pTc"), t2(t) * 2 * nb + (swa_base["score"] + j + 1))
                if j == 0:
                    pe.wait_ge(sem("swa_vtc"), t + 1)
                bank = (4, 7)[a]
                for c in range(n // 128):
                    last = mm(ps[bank][:, b * 128:(b + 1) * 128], SC[:, 5, c * 128:(c + 1) * 128],
                              SC[:, 14 + j, c * 128:(c + 1) * 128],
                              start=(c == 0 and j % nb == 0), stop=True)
                if j % nb == nb - 1:
                    last.then_inc(sem("swa_o"), 1)

            swa_base = {"score": 0}
            loop_i = [0]

            def t2(t):
                return loop_i[0]

            channel_sum(0, 0)
            for l in range(DEPTH):
                lo = 0 if l == 0 else CTX
                pe.wait_ge(sem("norm_ready"), l + 1)
                with pe.Fori(0, 1) as _i:
                    Fill(l, "gdn", 4, 0, lo).rest()
                with pe.Fori(0, 2) as i:
                    Fill(l, "gdn", 4, i, 0, off=4).rest()
                with pe.Fori(0, 1) as _i:
                    Fill(l, "gdng", 4, 0, lo).rest()
                wt, n = segs[(l, "small")]
                pe.wait_ge(sem("small_split"), l + 1)
                bank_wait(pe, n, 0, 2, 0)
                for k in range(KT):
                    x = pair(N[:, k, :])
                    last = pairs(ps[n % 2][0:NLR, :], wlr16[:, 0, k, :], wlr16[:, 1, k, :], x[:, 0, :], x[:, 1, :],
                                 k == 0, k == KT - 1)
                last.then_inc(sem(f"bank{n % 2}_full"), 1)
                bank_wait(pe, n, 0, 2, 1)
                for b in range(NC):
                    for k in range(KT):
                        x = pair(N[:, k, :])[:, :, b * 128:(b + 1) * 128]
                        last = pairs(ps[1][:, b * NAB:(b + 1) * NAB], x[:, 0, :], x[:, 1, :],
                                     wab16[:, 0, k, :], wab16[:, 1, k, :], k == 0, k == KT - 1)
                last.then_inc(sem("bank1_full"), 1)
                pe.wait_ge(sem("gdn_g"), l + 1)
                for d in range(2):
                    for kind, lhs in enumerate((cm(CUM[d]), cm(TAIL[d]), ones)):
                        last = mm(ps[3][:, (3 * d + kind) * 16:(3 * d + kind + 1) * 16], lhs, g[:, :, d, :])
                last.then_inc(sem("gdn_cums"), 1)
                for rounds, first in GDN_LOOPS[l]:
                    with pe.Fori(0, rounds) as i:
                        gdn(i + first, i + (4 * l + first),
                            Fill(l, "p2", 4, i, lo if first else 0, off=4 * first))
                pe.wait_ge(sem("gdn_y"), 4 * l + 4)
                with pe.Fori(0, 2) as i:
                    gla(i, i + 2 * l, l, Fill(l, "p3", 4, i, 0))
                    pe.wait_ge(sem("gla_y"), i + 2 * l + 1)
                blocks = list(range(4)) if l == 0 else [2, 3]
                with pe.Fori(0, 2) as i:
                    loop_i[0] = i
                    swa(i, i + 2 * l, Fill(l, "p4", 8, i, lo), blocks)
                    pe.wait_ge(sem("swa_y"), i + 2 * l + 1)
                swa_base["score"] += 4 * len(blocks)
                pe.wait_ge(sem("bank1_full"), segs[(l, "out")][1] // 2)
                pe.sem_inc(sem("norm_used"), 1)
                pe.wait_ge(sem("sc_y"), 4 * l + 4)
                project(l, "out", 16, rhs=lambda k: pair(act[:, Y_ORDER[k], :])[:, :, lo:])
                pe.wait_ge(sem("bank1_full"), (segs[(l, "out")][1] + 16) // 2)
                pe.sem_inc(sem("layer_multiplied"), 1)
                channel_sum(2 * l + 1, lo)
                if l == 0:
                    pe.wait_ge(sem("cs_ready"), 2)
                    ada_rows(1)
                    channel_sum(2, 0)
            wt, n = segs["end"]
            pe.wait_ge(sem("h_ready"), DEPTH + 1)
            for b in range(2):
                for q in range(4):
                    j = 4 * b + q
                    bank_wait(pe, n, 0, 8, j)
                    for c in range(4):
                        last = tp(ps[(n + j) % 2][:, c * 128:(c + 1) * 128],
                                  N[:, 4 * q + c, CTX + b * 128:CTX + (b + 1) * 128])
                    last.then_inc(sem(f"bank{(n + j) % 2}_full"), 1)

        @block.scalar
        def _(sc_eng):
            A = sc_eng
            oa = Order(A, sem("act_order"))

            def act_(out, in_, f, **kw):
                return nc.scalar.activation(out, in_, f, **kw)

            def evac(l, name, tb, i, tt, dst, off=0):
                n = segs[(l, name)][1] + off
                b = (n + tt) % 2
                out_wait(A, n, i, tb, tt)
                act_(dst, ps[b][:, 0:dst.shape[-1]], ACT.Copy, scale=1.0 / WSCALE)\
                    .then_inc(sem(f"bank{b}_free"), 1)

            def ada_evac(l):
                n = segs[(0, f"ada{l}")][1]
                with A.Fori(0, 12) as i:
                    out_wait(A, n, i, 2, 0)
                    act_(SC[:, 6, :], ps[0][:, :], ACT.Copy).then_inc(sem("bank0_free"), 1)
                    out_wait(A, n, i, 2, 1)
                    act_(ada[:, l, bass.ds(i * 4, 4), :], ps[1][:, 0:8].rearrange("p (k s) -> p k s", s=2), ACT.Copy)\
                        .then_inc(sem("bank1_free"), 1)
                A.wait_ge(sem("bank1_free"), (n + 24) // 2)
                A.sem_inc(sem("ada_out"), 1)

            def link(ins):
                oa.done(ins)
                oa.wait()

            def sigmoid(a):
                link(act_(a, a, ACT.Exp, scale=-1.0))
                link(act_(a, a, ACT.Ln, bias=one1))
                return act_(a, a, ACT.Exp, scale=-1.0)

            nc.scalar.preload_act_table_set("natural_log_exp_and_others")

            def evac_loop(l, name, rounds, dst, off=0):
                with A.Fori(0, rounds) as i:
                    for tt in range(RING):
                        evac(l, name, RING, i, tt, dst(i, tt), off)

            A.wait_ge(sem("con_in"), 16)
            A.wait_ge(sem("par_in"), 16)
            act_(cst[:, :, :], par[:, P_C:P_C + 2 * KT].rearrange("p (k s) -> p k s", s=2), ACT.Exp, scale=-1.0)\
                .then_inc(sem("c_exp"), 1)
            for k in range(KT):
                out_wait(A, 0, 0, KT, k)
                act_(N[:, k, :], ps[k % 2][:, :], ACT.Copy).then_inc(sem(f"bank{k % 2}_free"), 1)
            ada_evac(0)

            def rstd(t, bank, n, lo):
                A.wait_ge(sem("chansum_done"), t + 1)
                link(act_(SC[:, 2, lo:], ps[bank][:, lo:], ACT.Ln, scale=1.0 / n, bias=eps))
                act_(SC[:, 3, lo:], SC[:, 2, lo:], ACT.Exp, scale=-0.5).then_inc(sem("rstd_ready"), 1)

            def gdn(i, t, l, lo, take):
                A.wait_ge(sem("gdn_D"), t + 1)
                for d in range(2):
                    last = act_(SC[:, 20 + d, :], ps[5 + d][:, :], ACT.Exp)
                last.then_inc(sem("gdn_E"), 1)
                A.wait_ge(sem("gdn_x"), t + 1)
                act_(SC[:, 8:10, :], SC[:, 0:2, :], ACT.Square).then_inc(sem("gdn_sq"), 1)
                A.wait_ge(sem("gdn_tok"), t + 1)
                for j in range(3):
                    last = act_(SC[:, 3 + j, :], ps[2 + j][:, :], ACT.Copy)
                last.then_inc(sem("gdn_tokc"), 1)
                A.wait_ge(sem("gdn_ss"), t + 1)
                link(act_(rn[:, :, :], ps[7][:, 0:2 * NC].rearrange("p (a c) -> p a c", a=2), ACT.Ln, bias=eps))
                act_(rn[:, :, :], rn[:, :, :], ACT.Exp, scale=-0.5).then_inc(sem("gdn_rn"), 1)
                for j, (b, dst) in enumerate(((5, 14), (2, 16), (3, 17), (6, 15))):
                    A.wait_ge(sem("gdn_T1"), 4 * t + j + 1)
                    act_(SC[:, dst, :], ps[b][:, :], ACT.Copy).then_inc(sem("gdn_T1c"), 1)
                take(0)
                for d, b in ((0, 6), (1, 2)):
                    A.wait_ge(sem("gdn_T2"), 2 * t + d + 1)
                    act_(SC[:, 18 + d, :], ps[b][:, :], ACT.Copy).then_inc(sem("gdn_T2c"), 1)
                A.wait_ge(sem("gdn_gc"), t + 1)
                sigmoid(SC[:, 2, lo:]).then_inc(sem("gdn_gs"), 1)
                A.wait_ge(sem("gdn_P"), 14 * t + 2 + 6)
                take(1)
                A.wait_ge(sem("gdn_P"), 14 * t + 2 + 12)
                take(2)
                for s in range(NC):
                    A.wait_ge(sem("gdn_vn"), 4 * t + s + 1)
                    if s:
                        A.wait_ge(sem("gdn_dS"), 3 * t + s)
                    act_(vn[:, :, :], ps[3][:, 0:256].rearrange("p (d v) -> p d v", d=2), ACT.Copy,
                         scale=1.0 if s == 0 else -1.0).then_inc(sem("gdn_vnc"), 1)
                A.wait_ge(sem("gdn_o"), t + 1)
                act_(SC[:, 0, lo:], ps[5][:, lo:], ACT.Copy)
                act_(SC[:, 1, :], ps[5][:, :], ACT.Square).then_inc(sem("gdn_osq"), 1)
                A.wait_ge(sem("gdn_oss"), t + 1)
                link(act_(SC[:, 3, lo:], ps[6][:, lo:], ACT.Ln, scale=1.0 / HD, bias=eps))
                act_(SC[:, 3, lo:], SC[:, 3, lo:], ACT.Exp, scale=-0.5).then_inc(sem("gdn_orn"), 1)
                take(3)
                A.wait_ge(sem("gdn_y"), t + 1)

            def gla(i, t, l, lo, take):
                A.wait_ge(sem("gla_z"), t + 1)
                for d in range(2):
                    last = act_(SC[:, d, :], ps[2 + d][:, :], ACT.Identity,
                                bias=par[:, bass.ds(i + (l * PL + P_GLAB + 2 * d), 1)])
                last.then_inc(sem("gla_zc"), 1)
                A.wait_ge(sem("gla_vt"), t + 1)
                for a in range(2):
                    last = act_(SC[:, 18 + a, :], ps[4 + a][:, :], ACT.Copy)
                last.then_inc(sem("gla_vtc"), 1)
                A.wait_ge(sem("gla_abs"), t + 1)
                link(act_(SC[:, 2:4, :], SC[:, 2:4, :], ACT.Exp, scale=-1.0))
                act_(SC[:, 2:4, :], SC[:, 2:4, :], ACT.Ln, bias=one1).then_inc(sem("gla_l"), 1)
                A.wait_ge(sem("gla_cen"), t + 1)
                act_(SC[:, 8:10, :], SC[:, 2:4, :], ACT.Exp, scale=-1.0 / 16).then_inc(sem("gla_ek"), 1)
                act_(SC[:, 6:8, :], SC[:, 2:4, :], ACT.Exp, scale=1.0 / 16).then_inc(sem("gla_eq"), 1)
                for d in range(2):
                    mid, last_ = (CH // 2 - 1, CH - 1) if d == 0 else (CH // 2, 0)
                    act_(gs[:, 0, d, :], SC[:, 4 + d, mid::CH], ACT.Exp, scale=1.0 / 16)
                    act_(gs[:, 1, d, :], SC[:, 4 + d, last_::CH], ACT.Exp, scale=1.0 / 16)
                act_(gs[:, 2, :, :], gd[:, :, :], ACT.Exp, scale=1.0 / 16).then_inc(sem("gla_gs"), 1)
                A.wait_ge(sem("gla_gc"), t + 1)
                sigmoid(SC[:, 16:18, lo:]).then_inc(sem("gla_gsig"), 1)
                take(0)
                take(1)
                A.wait_ge(sem("gla_kt"), t + 1)
                for d in range(2):
                    last = act_(SC[:, 14 + d, :], ps[2 + d][:, :], ACT.Copy)
                last.then_inc(sem("gla_ktc"), 1)
                take(2)
                A.wait_ge(sem("gla_AT"), t + 1)
                for a in range(2):
                    A.wait_ge(sem("gla_o"), 2 * t + a + 1)
                    act_(SC[:, 6 + a, lo:], ps[6 + a][:, lo:], ACT.Copy)
                    act_(SC[:, 4 + a, :], ps[6 + a][:, :], ACT.Square).then_inc(sem("gla_osq"), 1)
                for a in range(2):
                    A.wait_ge(sem("gla_oss"), 2 * t + a + 1)
                    link(act_(SC[:, 8 + a, lo:], ps[2 + a][:, lo:], ACT.Ln, scale=1.0 / HD, bias=eps))
                    act_(SC[:, 8 + a, lo:], SC[:, 8 + a, lo:], ACT.Exp, scale=-0.5).then_inc(sem("gla_orn"), 1)
                take(3)
                A.wait_ge(sem("gla_y"), t + 1)

            swb = [0]

            def swa(i, t, l, lo, take, blocks):
                nb = len(blocks)
                A.wait_ge(sem("swa_vt"), t + 1)
                act_(SC[:, 5, :], ps[4][:, :], ACT.Copy).then_inc(sem("swa_vtc"), 1)
                A.wait_ge(sem("swa_gc"), t + 1)
                sigmoid(SC[:, 22:24, lo:]).then_inc(sem("swa_gs"), 1)
                take(0)
                A.wait_ge(sem("swa_m"), t + 1)
                for j in range(2 * nb):
                    n = TOK if blocks[j % nb] >= 2 else CTX
                    act_(SC[:, 6 + j, 0:n], SC[:, 6 + j, 0:n], ACT.Exp, scale=HD ** -0.5,
                         bias=sm[:, 1, j:j + 1], accum_out=sm[:, 2, j:j + 1])
                for a in range(2):
                    last = act_(sm[:, 3, a * nb:(a + 1) * nb], sm[:, 1, a * nb:(a + 1) * nb], ACT.Exp,
                                bias=par[:, bass.ds(i * 2 + (l * PL + P_SINK + a), 1)])
                last.then_inc(sem("swa_e"), 1)
                take(1)
                take(2)
                for j in range(2 * nb):
                    n = TOK if blocks[j % nb] >= 2 else CTX
                    A.wait_ge(sem("swa_pT"), i * 2 * nb + (swb[0] + j + 1))
                    act_(SC[:, 14 + j, 0:n], ps[2 + j % 2][:, 0:n], ACT.Copy).then_inc(sem("swa_pTc"), 1)
                for tt in range(3, 8):
                    take(tt)
                A.wait_ge(sem("swa_y"), t + 1)

            def take_(l, name, tb, i, dst, off=0):
                return lambda tt: evac(l, name, tb, i, tt, dst(tt), off)

            rstd(0, 2, D, 0)
            for l in range(DEPTH):
                lo = 0 if l == 0 else CTX
                if l:
                    A.wait_ge(sem("yo_used"), l)
                oa.straight()
                with A.Fori(0, 1) as i:
                    oa.round(i, CONV_ACT)
                    for tt in range(4):
                        evac(l, "gdn", 4, 0, tt, act[:, tt, lo:])
                        A.wait_ge(sem("conv_done"), 12 * l + tt + 1)
                        sigmoid(SC[:, 10 + tt % 2, lo:]).then_inc(sem("conv_gs"), 1)
                oa.close(1)
                with A.Fori(0, 2) as i:
                    oa.round(i, CONV_ACT)
                    for tt in range(4):
                        evac(l, "gdn", 4, i, tt, act[:, i * 4 + (4 + tt), :], off=4)
                        t = i * 4 + (12 * l + 4 + tt + 1)
                        A.wait_ge(sem("conv_done"), t)
                        sigmoid(SC[:, 10 + tt % 2, :]).then_inc(sem("conv_gs"), 1)
                oa.close(2)
                with A.Fori(0, 1) as _i:
                    for tt in range(4):
                        evac(l, "gdng", 4, 0, tt, act[:, Y_GDN + tt, lo:])
                wt, n = segs[(l, "small")]
                assert n % 2 == 0
                out_wait(A, n, 0, 2, 0)
                act_(lrT, ps[0][0:NLR, :], ACT.Copy, scale=1.0 / WSCALE).then_inc(sem("bank0_free"), 1)
                A.wait_ge(sem("bank0_free"), n // 2 + 1)
                A.sem_inc(sem("lr_copied"), 1)
                out_wait(A, n, 0, 2, 1)
                act_(ab, ps[1][:, 0:NC * NAB].rearrange("p (c k) -> p c k", k=NAB), ACT.Copy, scale=1.0 / WSCALE)\
                    .then_inc(sem("bank1_free"), 1)
                A.wait_ge(sem("bank1_free"), n // 2 + 1)
                A.sem_inc(sem("ab_copied"), 1)
                if l:
                    A.wait_ge(sem("gdn_g"), l)
                act_(expA[:, :, :], P(l, P_ALOG, 8).rearrange("p (d h) -> p d h", d=2), ACT.Exp)\
                    .then_inc(sem("expA"), 1)
                A.wait_ge(sem("gate_abs"), l + 1)
                link(act_(gt[:, :, :, :], gt[:, :, :, :], ACT.Exp, scale=-1.0))
                act_(gt[:, :, :, :], gt[:, :, :, :], ACT.Ln, bias=one1).then_inc(sem("gate_l"), 1)
                A.wait_ge(sem("gate_bc"), l + 1)
                sigmoid(beta[:, :, :, :]).then_inc(sem("beta_ready"), 1)
                A.wait_ge(sem("gdn_cums"), l + 1)
                act_(eg[:, :, :, :, :].rearrange("p a b c d -> p (a b c d)"), ps[3][:, 0:96], ACT.Exp)\
                    .then_inc(sem("gdn_eg"), 1)
                oa.straight()
                for rounds, first in GDN_LOOPS[l]:
                    with A.Fori(0, rounds) as i:
                        oa.round(i, GDN_ACT)
                        pl = lo if first else 0
                        gdn(i + first, i + (4 * l + first), l, lo, take_(
                            l, "p2", 4, i, lambda tt: act[:, i * 4 + (T_B + 4 * first + tt), pl:], 4 * first))
                    oa.close(rounds)
                with A.Fori(0, 2) as i:
                    oa.round(i, GLA_ACT)
                    gla(i, i + 2 * l, l, lo, take_(l, "p3", 4, i, lambda tt: act[:, i * 4 + (T_A + tt), :]))
                oa.close(2)
                blocks = list(range(4)) if l == 0 else [2, 3]
                with A.Fori(0, 2) as i:
                    oa.round(i, SWA_ACT)
                    swa(i, i + 2 * l, l, lo, take_(l, "p4", 8, i, lambda tt: act[
                        :, (i * 8 + (8 + tt)) if tt < 4 else (i * 20 + (8 + tt)), lo:]), blocks)
                oa.close(2)
                swb[0] += 4 * len(blocks)
                with A.Fori(0, 4) as i:
                    oa.round(i, SC_ACT)
                    A.wait_ge(sem("sc_gc"), i + (4 * l + 1))
                    sigmoid(SC[:, 3, lo:]).then_inc(sem("sc_gs"), 1)
                    A.wait_ge(sem("sc_y"), i + 4 * l + 1)
                oa.close(4)
                n = segs[(l, "out")][1]
                with A.Fori(0, 4) as i:
                    for tt in range(4):
                        b = (n + tt) % 2
                        out_wait(A, n, i, 4, tt)
                        act_(act[:, i * 4 + tt, lo:], ps[b][:, 0:TOK - lo], ACT.Copy, scale=1.0 / WSCALE)
                        if tt >= 2:
                            A.wait_ge(sem("yo_add"), i * 4 + (16 * l + tt - 1))
                        else:
                            A.wait_ge(sem("yo_round"), i + (4 * l + 1))
                        act_(SC[:, 4 + tt % 2, lo:], ps[b][:, 0:TOK - lo], ACT.Square, scale=1.0 / WSCALE)\
                            .then_inc(sem(f"bank{b}_free"), 1)
                rstd(2 * l + 1, 2, D, lo)
                if l == 0:
                    ada_evac(1)
                    A.wait_ge(sem("rstd_used"), 1)
                    rstd(2, 2, D, 0)
            wt, n = segs["end"]
            A.wait_ge(sem("yo_used"), DEPTH)
            for j in range(8):
                out_wait(A, n, 0, 8, j)
                act_(act[:, j, :], ps[(n + j) % 2][:, :], ACT.Copy).then_inc(sem(f"bank{(n + j) % 2}_free"), 1)
                A.wait_ge(sem(f"bank{(n + j) % 2}_free"), (n + j) // 2 + 1)
                A.sem_inc(sem("out_staged"), 1)

        @block.vector
        def _(dve):
            V = nc.vector
            o = Order(dve, sem("dve_order"))

            def link(ins):
                o.done(ins)
                o.wait()

            dve.wait_ge(sem("con_in"), 16)
            dve.wait_ge(sem("par_in"), 16)
            dve.wait_ge(sem("c_exp"), 1)
            link(V.tensor_scalar(cst[:, :, :], cst[:, :, :], 1.0, None, ALU.add))
            link(V.reciprocal(cst[:, :, :], cst[:, :, :]))
            link(V.tensor_tensor(cs[:, :, :], cst[:, :, :], par[:, P_C:P_C + 2 * KT].rearrange(
                "p (k s) -> p k s", s=2), ALU.mult))

            def pad_cs():
                link(V.memset(csp, 0.0))
                V.tensor_copy(csp[:, :, 0:2], cs[:, :, :]).then_inc(sem("cs_ready"), 1)

            for s in range(2):
                dve.sem_inc(sem(f"stage{s}_split"), 1)
            pad_cs()

            def split_tile(s, full, k0=None):
                dve.wait_ge(sem(f"stage{s}_full"), full)
                h = halves(s)
                link(V.tensor_scalar(h[:, :, 0, :], ring[:, s, :, :], WSCALE, None, ALU.mult))
                V.scalar_tensor_tensor(h[:, :, 1, :], ring[:, s, :, :], WSCALE, h[:, :, 0, :],
                                       ALU.mult, ALU.subtract).then_inc(sem(f"stage{s}_split"), 1)

            def splitter(l, name, tb, i, off=0):
                wt, n = segs[(l, name)]

                def split(j):
                    out_wait(dve, n + off, i, tb, j)
                    split_tile(j % 2, i * (8 * tb) + 16 * ((wt + off + j + 2) // 2 + 1))
                return split

            def split_y(dst, src, lo):
                d = pair(dst)
                link(V.tensor_copy(d[:, 0, lo:], src))
                return V.tensor_tensor(d[:, 1, lo:], src, d[:, 0, lo:], ALU.subtract)

            def modulation(l):
                dve.wait_ge(sem("ada_out"), l + 1)
                link(V.tensor_tensor(ada[:, l, :, :], ada[:, l, :, :], along(P(l, P_ADAB, 48), 2), ALU.add))
                V.scalar_tensor_tensor(modA[:, l, :, :], ada[:, l, 16:32, :], 1.0, along(P(l, P_NPRE, 16), 2),
                                       ALU.add, ALU.mult)
                link(V.tensor_tensor(modG[:, l, :, :], ada[:, l, 32:48, :], along(P(l, P_NPOST, 16), 2), ALU.mult))

            def prenorm(l, t):
                dve.wait_ge(sem("rstd_ready"), t + 1)
                dve.wait_ge(sem("h_saved"), 16 * (l + 1))
                at = {}
                for k in range(KT + 3):
                    if k < KT:
                        if k >= 4:
                            o.wait(at[k - 4, 3])
                        at[k, 0] = o.done(V.tensor_tensor(SC[:, 8 + k % 4, :], N[:, k, :], SC[:, 3, :], ALU.mult))
                    q = k - 1
                    if 0 <= q < KT:
                        o.wait(at[q, 0])
                        for hf in range(2):
                            s = slice(hf * 256, hf * 256 + 256)
                            last = V.tensor_scalar(SC[:, 8 + q % 4, s], SC[:, 8 + q % 4, s],
                                                   modA[:, l, q, hf:hf + 1], ada[:, l, q, hf:hf + 1],
                                                   ALU.mult, ALU.add)
                        at[q, 1] = o.done(last)
                    q = k - 2
                    if 0 <= q < KT:
                        o.wait(at[q, 1])
                        at[q, 2] = o.done(V.tensor_copy(pair(N[:, q, :])[:, 0, :], SC[:, 8 + q % 4, :]))
                    q = k - 3
                    if 0 <= q < KT:
                        o.wait(at[q, 2])
                        at[q, 3] = o.done(V.tensor_tensor(pair(N[:, q, :])[:, 1, :], SC[:, 8 + q % 4, :],
                                                          pair(N[:, q, :])[:, 0, :], ALU.subtract))
                o.wait()
                dve.sem_inc(sem("norm_ready"), 1)

            def two(a):
                return a.rearrange("p (s t) -> p s t", s=2)

            def conv_tap(dst, src, wcol, sh):
                d, s = two(dst), two(src)
                a, b = max(0, -sh), SEQ - max(0, sh)
                return V.scalar_tensor_tensor(d[:, :, a:b], s[:, :, a + sh:b + sh], wcol, d[:, :, a:b],
                                              ALU.mult, ALU.add)

            def gates(l):
                dve.wait_ge(sem("ab_copied"), l + 1)
                z = o.done(V.tensor_tensor(gz[:, :, :, :].rearrange("p c d h -> p c (d h)"), ab[:, :, 0:8],
                                           over(P(l, P_DT, 8)), ALU.add))
                V.tensor_copy(beta[:, :, :, :].rearrange("p h d c -> p c d h"),
                              ab[:, :, 8:16].rearrange("p c (d h) -> p c d h", d=2)).then_inc(sem("gate_bc"), 1)
                o.wait(z)
                V.scalar_tensor_tensor(gt[:, :, :, :], gz[:, :, :, :], -1.0, gz[:, :, :, :], ALU.mult, ALU.max)\
                    .then_inc(sem("gate_abs"), 1)
                dve.wait_ge(sem("gate_l"), l + 1)
                link(V.scalar_tensor_tensor(gz[:, :, :, :], gz[:, :, :, :], 0.0, gt[:, :, :, :], ALU.max, ALU.add))
                dve.wait_ge(sem("expA"), l + 1)
                for d in range(2):
                    last = V.scalar_tensor_tensor(g[:, :, d, :].rearrange("p h c -> p c h"), gz[:, :, d, :], -1.0,
                                                  over(expA[:, d, :]), ALU.mult, ALU.mult)
                last.then_inc(sem("gdn_g"), 1)

            def conv_tile(j, tile, l, l0, t, wcol):
                s0, acc, sg = l0 // SEQ, SC[:, 8 + j % 2, :], SC[:, 10 + j % 2, :]

                def tap(tp, sh):
                    d, s = two(acc)[:, s0:, :], two(tile)[:, s0:, :]
                    a, b = max(0, -sh), SEQ - max(0, sh)
                    return V.scalar_tensor_tensor(d[:, :, a:b], s[:, :, a + sh:b + sh], wcol(tp), d[:, :, a:b],
                                                  ALU.mult, ALU.add)
                link(V.tensor_scalar(acc[:, l0:], tile[:, l0:], wcol(2), None, ALU.mult))
                for tp in (0, 1, 3, 4):
                    link(tap(tp, tp - 2))
                V.tensor_scalar(sg[:, l0:], acc[:, l0:], CLAMP, None, ALU.max).then_inc(sem("conv_done"), 1)

            def conv_end(j, tile, l0, t):
                dve.wait_ge(sem("conv_gs"), t)
                return V.tensor_tensor(tile[:, l0:], SC[:, 8 + j % 2, l0:], SC[:, 10 + j % 2, l0:], ALU.mult)

            def gdn_projection(l, lo):
                n = segs[(l, "gdn")][1]
                for rounds, first in ((1, 0), (2, 4)):
                    l0 = lo if first == 0 else 0
                    with dve.Fori(0, rounds) as i:
                        o.round(i, CONV_DVE)
                        split = splitter(l, "gdn", 4, i, first)
                        for j in range(4):
                            tile = act[:, i * 4 + (T_A + first + j), :]
                            t = i * 4 + (12 * l + first + j + 1)
                            split(j)
                            dve.wait_ge(sem(f"bank{(n + j) % 2}_free"), i * 2 + ((n + first + j) // 2 + 1))
                            conv_tile(j, tile, l, l0, t, lambda tp: par[
                                :, bass.ds(i * 20 + (l * PL + P_CONV + 5 * (first + j) + tp), 1)])
                            link(conv_end(j, tile, l0, t))
                    o.close(rounds)
                split = splitter(l, "gdng", 4, 0)
                for j in range(4):
                    split(j)
                dve.wait_ge(sem("small_in"), 32 * (l + 1))
                for w16, w in ((wlr16, wlr), (wab16, wab)):
                    link(V.tensor_scalar(w16[:, 0], w, WSCALE, None, ALU.mult))
                    last = V.scalar_tensor_tensor(w16[:, 1], w, WSCALE, w16[:, 0], ALU.mult, ALU.subtract)
                last.then_inc(sem("small_split"), 1)

            def gdn(i, t, l, lo, split):
                qkv = act[:, T_A:T_A + 12, :].rearrange("p (j h) t -> p j h t", j=3)
                V.tensor_copy(SC[:, 0:3, :], qkv[:, :, i, :]).then_inc(sem("gdn_x"), 1)
                dve.wait_ge(sem("gdn_tokc"), t + 1)
                dve.wait_ge(sem("gdn_ks"), t + 1)
                V.tensor_tensor(chunks(SC[:, 7, :]), chunks(SC[:, 4, :]), along(rn[:, 1, :]), ALU.mult)
                for d in range(2):
                    V.tensor_tensor(chunks(SC[:, 8 + d, :]), chunks(SC[:, 4, :]), along(ks[:, 0, d, :]), ALU.mult)
                V.tensor_tensor(chunks(SC[:, 6, :]), chunks(SC[:, 3, :]), along(rq[:, :]), ALU.mult)\
                    .then_inc(sem("gdn_kn"), 1)
                V.tensor_scalar(SC[:, 2, lo:], act[:, i + Y_GDN, lo:], CLAMP, None, ALU.max)\
                    .then_inc(sem("gdn_gc"), 1)
                split(0)
                dve.wait_ge(sem("gdn_Em"), t + 1)
                dve.wait_ge(sem("gdn_G"), 3 * t + 1)
                for d in range(2):
                    last = V.tensor_tensor(SC[:, 20 + d, :], ps[5][:, :], SC[:, 20 + d, :], ALU.mult)
                last.then_inc(sem("gdn_AT"), 1)
                for d, bank in ((0, 4), (1, 7)):
                    dve.wait_ge(sem("gdn_G"), 3 * t + 2 + d)
                    V.tensor_tensor(SC[:, 22 + d, :], ps[bank][:, :], SC[:, 22 + d, :], ALU.mult)\
                        .then_inc(sem("gdn_U"), 1)
                MK = (C_LO, C_UP)
                for d, bank in ((0, 3), (1, 4)):
                    dve.wait_ge(sem("gdn_P"), 14 * t + d + 1)
                    o.done(V.tensor_tensor(chunks(SC[:, 16 + d, :]), chunks(ps[bank][:, :]), over(cm(MK[d])),
                                           ALU.mult))
                    o.wait()
                    V.tensor_tensor(chunks(SC[:, 6 + d, :]), over(ident), chunks(SC[:, 16 + d, :]), ALU.subtract)\
                        .then_inc(sem("gdn_T"), 1)
                for lv in range(1, 7):
                    for d in range(2):
                        dve.wait_ge(sem("gdn_P"), 14 * t + 2 * lv + d + 1)
                        V.tensor_tensor(chunks(SC[:, 16 + d, :]), chunks(ps[2 + d][:, :]),
                                        over(cm(MK[d] + 128 * lv)), ALU.mult).then_inc(sem("gdn_Pm"), 1)
                    for d in range(2):
                        if lv < 6:
                            dve.wait_ge(sem("gdn_Y"), 10 * t + 2 * (lv - 1) + d + 1)
                            dve.wait_ge(sem("gdn_T"), 12 * t + 2 * (lv - 1) + d + 1)
                            V.tensor_tensor(SC[:, 6 + d, :], SC[:, 6 + d, :], ps[4 + d][:, :], ALU.subtract)\
                                .then_inc(sem("gdn_T"), 1)
                        dve.wait_ge(sem("gdn_YT"), 12 * t + 2 * (lv - 1) + d + 1)
                        if lv == 1:
                            dve.wait_ge(sem("gdn_M0"), 2 * t + d + 1)
                        else:
                            dve.wait_ge(sem("gdn_M"), 10 * t + 2 * (lv - 2) + d + 1)
                        last = V.tensor_tensor(SC[:, 8 + d, :], SC[:, 8 + d, :], ps[6 + d][:, :], ALU.subtract)
                        if lv < 6:
                            last.then_inc(sem("gdn_M"), 1)
                    if lv == 3:
                        split(1)
                last.then_inc(sem("gdn_Mlast"), 1)
                for s in range(NC):
                    cc = (s, (1, 0, 3, 2)[s])
                    if s:
                        dve.wait_ge(sem("gdn_KS"), 3 * t + s)
                        for d in range(2):
                            last = V.scalar_tensor_tensor(rr[:, d, :], ps[2][:, d * 128:d * 128 + 128],
                                                          ks[:, 3, d, cc[d]:cc[d] + 1],
                                                          SC[:, 12 + d, cc[d] * 128:cc[d] * 128 + 128],
                                                          ALU.mult, ALU.subtract)
                        last.then_inc(sem("gdn_r"), 1)
                    if s < NC - 1:
                        dve.wait_ge(sem("gdn_dS"), 3 * t + s + 1)
                        if s == 0:
                            V.tensor_copy(st[:, :, :], ps[4][:, 0:256].rearrange("p (d v) -> p d v", d=2))\
                                .then_inc(sem("gdn_S"), 1)
                        else:
                            dve.wait_ge(sem("gdn_S"), 3 * t + s)
                            for d in range(2):
                                last = V.scalar_tensor_tensor(st[:, d, :], st[:, d, :],
                                                              tot[:, d, cc[d]:cc[d] + 1],
                                                              ps[4][:, d * 128:d * 128 + 128], ALU.mult, ALU.add)
                            last.then_inc(sem("gdn_S"), 1)
                    if s == 1:
                        split(2)
                dve.wait_ge(sem("gdn_orn"), t + 1)
                link(V.scalar_tensor_tensor(SC[:, 0, lo:], SC[:, 0, lo:], P(l, P_GDNN), SC[:, 3, lo:],
                                            ALU.mult, ALU.mult))
                dve.wait_ge(sem("gdn_silu"), t + 1)
                link(V.tensor_tensor(SC[:, 1, lo:], SC[:, 0, lo:], SC[:, 2, lo:], ALU.mult))
                split_y(act[:, i + Y_GDN, :], SC[:, 1, lo:], lo).then_inc(sem("gdn_y"), 1)
                dve.wait_ge(sem("gdn_y"), t + 1)
                split(3)

            def gla(i, t, l, lo, split):
                dve.wait_ge(sem("gla_zc"), t + 1)
                V.scalar_tensor_tensor(SC[:, 2:4, :], SC[:, 0:2, :], -1.0, SC[:, 0:2, :], ALU.mult, ALU.max)\
                    .then_inc(sem("gla_abs"), 1)
                dve.wait_ge(sem("gla_l"), t + 1)
                link(V.scalar_tensor_tensor(SC[:, 0:2, :], SC[:, 0:2, :], 0.0, SC[:, 2:4, :], ALU.min, ALU.subtract))
                V.tensor_tensor_scan(SC[:, 4, :], con[:, C_SEG:C_SEG + TOK], SC[:, 0, :], 0.0, ALU.mult, ALU.add)
                link(V.tensor_tensor_scan(SC[:, 5, ::-1], con[:, C_SEG:C_SEG + TOK], SC[:, 1, ::-1], 0.0,
                                          ALU.mult, ALU.add))
                for d in range(2):
                    mid, last_ = (CH // 2 - 1, CH - 1) if d == 0 else (CH // 2, 0)
                    V.tensor_tensor(gd[:, d, :], SC[:, 4 + d, last_::CH], SC[:, 4 + d, mid::CH], ALU.subtract)
                    last = V.tensor_tensor(chunks(SC[:, 2 + d, :]), chunks(SC[:, 4 + d, :]),
                                           along(SC[:, 4 + d, mid::CH]), ALU.subtract)
                link(last)
                V.tensor_scalar(SC[:, 2:4, :], SC[:, 2:4, :], 640.0, -640.0, ALU.min, ALU.max)\
                    .then_inc(sem("gla_cen"), 1)
                dve.wait_ge(sem("gla_vtc"), t + 1)
                V.tensor_scalar(SC[:, 16:18, lo:], act[:, bass.ds(i * 2 + Y_GLA, 2), lo:], CLAMP, None, ALU.max)\
                    .then_inc(sem("gla_gc"), 1)
                split(0)
                dve.wait_ge(sem("gla_eq"), t + 1)
                for d in range(2):
                    last = V.scalar_tensor_tensor(SC[:, 10 + d, :], act[:, i + T_B, :], 64 ** -0.5, SC[:, 6 + d, :],
                                                  ALU.mult, ALU.mult)
                last.then_inc(sem("gla_qd"), 1)
                split(1)
                for a in range(2):
                    for d in range(2):
                        bank = (6, 7, 2, 3)[2 * a + d]
                        dve.wait_ge(sem("gla_att"), 4 * t + 2 * a + d + 1)
                        last = V.tensor_tensor(chunks(SC[:, 20 + 2 * a + d, :]), chunks(ps[bank][:, :]),
                                               over(cm(CUM[d])), ALU.mult)
                last.then_inc(sem("gla_AT"), 1)
                dve.wait_ge(sem("gla_dS"), t + 1)
                dve.wait_ge(sem("gla_gs"), t + 1)
                dve.wait_ge(sem("gla_kd"), t + 1)
                for d in range(2):
                    last = V.tensor_tensor(chunks(SC[:, 2 + d, :]), chunks(ps[4 + d][:, :]),
                                           along(gs[:, 2, d, :]), ALU.mult)
                link(last)
                for s in range(1, NC):
                    for d in range(2):
                        prev = (s - 1, (1, 0, 3, 2)[s - 1])[d]
                        own = SC[:, 2 + d, prev * 128:prev * 128 + 128]
                        to = SC[:, 8 + d, (s - 1) * 128:s * 128]
                        if s == 1:
                            last = V.tensor_copy(to, own)
                        else:
                            last = V.scalar_tensor_tensor(to, SC[:, 8 + d, (s - 2) * 128:(s - 1) * 128],
                                                          gs[:, 1, d, prev:prev + 1], own, ALU.mult, ALU.add)
                    link(last)
                for s in range(1, NC):
                    for d in range(2):
                        c = (s, (1, 0, 3, 2)[s])[d]
                        last = V.tensor_scalar(SC[:, d, (s - 1) * 128:s * 128], SC[:, 8 + d, (s - 1) * 128:s * 128],
                                               gs[:, 0, d, c:c + 1], None, ALU.mult)
                last.then_inc(sem("gla_S"), 1)
                split(2)
                dve.wait_ge(sem("gla_silu"), t + 1)
                for a in range(2):
                    dve.wait_ge(sem("gla_orn"), 2 * t + a + 1)
                    link(V.scalar_tensor_tensor(SC[:, 6 + a, lo:], SC[:, 6 + a, lo:], P(l, P_GLAN),
                                                SC[:, 8 + a, lo:], ALU.mult, ALU.mult))
                link(V.tensor_tensor(SC[:, 4:6, lo:], SC[:, 6:8, lo:], SC[:, 16:18, lo:], ALU.mult))
                for a in range(2):
                    last = split_y(act[:, i * 2 + (Y_GLA + a), :], SC[:, 4 + a, lo:], lo)
                last.then_inc(sem("gla_y"), 1)
                dve.wait_ge(sem("gla_y"), t + 1)
                split(3)

            swb = [0]

            def swa(i, t, l, lo, blocks, split):
                nb = len(blocks)
                dve.wait_ge(sem("swa_stat"), t + 1)
                dve.wait_ge(sem("swa_rot"), t + 1)
                V.tensor_scalar(SC[:, 22:24, lo:], act[:, bass.ds(i * 2 + Y_SWA, 2), lo:], CLAMP, None, ALU.max)\
                    .then_inc(sem("swa_gc"), 1)
                sin2 = con[:, C_SIN:C_SIN + SEQ]
                V.tensor_tensor(SC[:, 20:22, 0:SEQ], ps[2][:, :].rearrange("p (a t) -> p a t", a=2),
                                over(sin2, 2), ALU.mult)
                V.tensor_tensor(SC[:, 4, 0:SEQ], ps[3][:, 0:SEQ], sin2, ALU.mult)
                link(V.tensor_tensor(SC[:, 0:3, CTX:], SC[:, 0:3, CTX:], over(con[:, C_COS:C_COS + SEQ], 3), ALU.mult))
                V.tensor_tensor(SC[:, 0:2, CTX:], SC[:, 0:2, CTX:], SC[:, 20:22, 0:SEQ], ALU.add)
                V.tensor_tensor(SC[:, 2, CTX:], SC[:, 2, CTX:], SC[:, 4, 0:SEQ], ALU.add)\
                    .then_inc(sem("swa_rope"), 1)
                for j in range(2 * nb):
                    b = blocks[j % nb]
                    n = TOK if b >= 2 else CTX
                    dve.wait_ge(sem("swa_s"), i * 2 * nb + (swb[0] + j + 1))
                    last = V.tensor_copy(SC[:, 6 + j, 0:CTX], ps[5 + j % 2][:, 0:CTX])
                    if b >= 2:
                        mk = C_MASK + (b - 2) * SEQ
                        last = V.tensor_tensor(SC[:, 6 + j, CTX:], ps[5 + j % 2][:, CTX:], con[:, mk:mk + SEQ],
                                               ALU.add)
                    last.then_inc(sem("swa_sc"), 1)
                dve.wait_ge(sem("swa_sc"), i * 2 * nb + (swb[0] + 2 * nb))
                split(0)
                for j in range(2 * nb):
                    n = TOK if blocks[j % nb] >= 2 else CTX
                    last = V.tensor_reduce(sm[:, 0, j:j + 1], SC[:, 6 + j, 0:n], AX, ALU.max)
                link(last)
                for a in range(2):
                    last = V.tensor_scalar(sm[:, 1, a * nb:(a + 1) * nb], sm[:, 0, a * nb:(a + 1) * nb], HD ** -0.5,
                                           par[:, bass.ds(i * 2 + (l * PL + P_SINK + a), 1)], ALU.mult, ALU.max)
                link(last)
                V.tensor_scalar(sm[:, 1, 0:2 * nb], sm[:, 1, 0:2 * nb], -1.0, None, ALU.mult)\
                    .then_inc(sem("swa_m"), 1)
                split(1)
                dve.wait_ge(sem("swa_e"), t + 1)
                link(V.tensor_tensor(sm[:, 4, 0:2 * nb], sm[:, 2, 0:2 * nb], sm[:, 3, 0:2 * nb], ALU.add))
                link(V.reciprocal(sm[:, 5, 0:2 * nb], sm[:, 4, 0:2 * nb]))
                for j in range(2 * nb):
                    n = TOK if blocks[j % nb] >= 2 else CTX
                    V.tensor_scalar(SC[:, 6 + j, 0:n], SC[:, 6 + j, 0:n], sm[:, 5, j:j + 1], None, ALU.mult)\
                        .then_inc(sem("swa_p"), 1)
                split(2)
                split(3)
                dve.wait_ge(sem("swa_silu"), t + 1)
                for a in range(2):
                    dve.wait_ge(sem("swa_o"), 2 * t + a + 1)
                    link(V.tensor_tensor(SC[:, a, lo:], ps[(4, 7)[a]][:, lo:], SC[:, 22 + a, lo:], ALU.mult))
                    last = split_y(act[:, i * 2 + (Y_SWA + a), :], SC[:, a, lo:], lo)
                last.then_inc(sem("swa_y"), 1)
                dve.wait_ge(sem("swa_y"), t + 1)
                for j in range(4, 8):
                    split(j)

            def shortconv(i, t, l, lo):
                def wcol(tap):
                    return par[:, bass.ds(i * 3 + (l * PL + P_SCW + tap), 1)]
                s0 = lo // 256

                def tap(dst, src, wc, sh):
                    d, s = two(dst)[:, s0:, :], two(src)[:, s0:, :]
                    a, b = max(0, -sh), SEQ - max(0, sh)
                    return V.scalar_tensor_tensor(d[:, :, a:b], s[:, :, a + sh:b + sh], wc, d[:, :, a:b],
                                                  ALU.mult, ALU.add)
                V.tensor_scalar(SC[:, 3, lo:], act[:, i + Y_SC, lo:], CLAMP, None, ALU.max).then_inc(sem("sc_gc"), 1)
                link(V.tensor_tensor(SC[:, 0, lo:], act[:, i + 12, lo:], act[:, i + 16, lo:], ALU.mult))
                link(V.tensor_scalar(SC[:, 1, lo:], SC[:, 0, lo:], wcol(1), None, ALU.mult))
                link(tap(SC[:, 1, :], SC[:, 0, :], wcol(0), -1))
                link(tap(SC[:, 1, :], SC[:, 0, :], wcol(2), 1))
                link(V.tensor_tensor(SC[:, 1, lo:], SC[:, 1, lo:], act[:, i + 8, lo:], ALU.mult))
                dve.wait_ge(sem("sc_gs"), t + 1)
                link(V.tensor_tensor(SC[:, 3, lo:], SC[:, 3, lo:], act[:, i + Y_SC, lo:], ALU.mult))
                link(V.tensor_tensor(SC[:, 1, lo:], SC[:, 1, lo:], SC[:, 3, lo:], ALU.mult))
                split_y(act[:, i + Y_SC, :], SC[:, 1, lo:], lo).then_inc(sem("sc_y"), 1)
                dve.wait_ge(sem("sc_y"), t + 1)

            modulation(0)
            prenorm(0, 0)
            for l in range(DEPTH):
                lo = 0 if l == 0 else CTX
                wt = segs[(l, "gdn")][0]
                for s in range(2):
                    dve.wait_ge(sem(f"slot{2 + s}_free"), 12 * (l + 1) + 1)
                    split_tile(s, 16 * (wt // 2 + 1))
                o.straight()
                gdn_projection(l, lo)
                gates(l)
                o.straight()
                full = segs[(l, "small")][1] // 2
                dve.wait_ge(sem("bank0_free"), full)
                dve.wait_ge(sem("bank1_free"), full)
                dve.wait_ge(sem("gdn_eg"), l + 1)
                for rounds, first in GDN_LOOPS[l]:
                    with dve.Fori(0, rounds) as i:
                        o.round(i, GDN_DVE)
                        gdn(i + first, i + (4 * l + first), l, lo, splitter(l, "p2", 4, i, 4 * first))
                    o.close(rounds)
                full = (segs[(l, "p3")][1]) // 2
                dve.wait_ge(sem("bank0_free"), full)
                dve.wait_ge(sem("bank1_free"), full)
                with dve.Fori(0, 2) as i:
                    o.round(i, GLA_DVE)
                    gla(i, i + 2 * l, l, lo, splitter(l, "p3", 4, i))
                o.close(2)
                blocks = list(range(4)) if l == 0 else [2, 3]
                with dve.Fori(0, 2) as i:
                    o.round(i, SWA_DVE)
                    swa(i, i + 2 * l, l, lo, blocks, splitter(l, "p4", 8, i))
                o.close(2)
                swb[0] += 4 * len(blocks)
                full = (segs[(l, "out")][1]) // 2
                dve.wait_ge(sem("bank0_free"), full)
                dve.wait_ge(sem("bank1_free"), full)
                with dve.Fori(0, 4) as i:
                    o.round(i, SC_DVE)
                    shortconv(i, i + 4 * l, l, lo)
                o.close(4)
                with dve.Fori(0, 3) as i:
                    o.round(i, 4)
                    split = splitter(l, "out", 4, i)
                    for j in range(4):
                        split(j)
                o.close(3)
                split = splitter(l, "out", 4, 0, 12)
                for j in range(2):
                    split(j)
                o.straight()
                dve.wait_ge(sem("rstd_ready"), 2 * l + 2)
                n = segs[(l, "out")][1] + 16
                dve.wait_ge(sem("bank0_free"), n // 2)
                dve.wait_ge(sem("bank1_free"), n // 2)
                with dve.Fori(0, KT) as k:
                    for hf in range(l, 2):
                        s = slice(hf * 256, hf * 256 + 256)
                        last = V.scalar_tensor_tensor(act[:, k, s], act[:, k, s],
                                                      modG[:, l, k, hf:hf + 1], SC[:, 3, s], ALU.mult, ALU.mult)
                    last.then_inc(sem("yo_scaled"), 1)
                dve.wait_ge(sem("yo_scaled"), KT * (l + 1))
                dve.sem_inc(sem("rstd_used"), 1)
                if l == 0:
                    pad_cs()
                    modulation(1)
                    prenorm(1, 2)

        @block.gpsimd
        def _(pool):
            G = nc.gpsimd
            o = Order(pool, sem("pool_order"))

            def link(ins):
                o.done(ins)
                o.wait()
            G.memset(wdec[:, :, :], 0.0).then_inc(sem("wdec_zero"), 1)
            pool.wait_ge(sem("con_in"), 16)

            def square_sum(lo):
                for k in range(KT):
                    if k == 0:
                        link(G.tensor_tensor(SC[:, 0, lo:], N[:, 0, lo:], N[:, 0, lo:], ALU.mult))
                    else:
                        link(G.tensor_tensor(SC[:, 1, lo:], N[:, k, lo:], N[:, k, lo:], ALU.mult))
                        link(G.tensor_tensor(SC[:, 0, lo:], SC[:, 0, lo:], SC[:, 1, lo:], ALU.add))
                pool.sem_inc(sem("sumsq_ready"), 1)

            pool.wait_ge(sem("bank0_free"), 8)
            pool.wait_ge(sem("bank1_free"), 8)
            pool.sem_inc(sem("h_ready"), 1)
            square_sum(0)

            def gdn(i, t, l, lo):
                rg = SC[:, 18:20, :].rearrange("p d (c t) -> p d c t", t=128)
                for d in range(2):
                    last = G.tensor_tensor(rg[:, d], over(cm(CUM[d])), along(g[:, i, d, :]), ALU.mult)
                last.then_inc(sem("gdn_rg"), 1)
                pool.wait_ge(sem("gdn_E"), t + 1)
                strict = (C_TAILB, C_TAILF)
                for d in range(2):
                    G.tensor_tensor(chunks(SC[:, 22 + d, :]), chunks(SC[:, 20 + d, :]), over(cm(strict[d])), ALU.mult)
                for d in range(2):
                    last = G.tensor_tensor(chunks(SC[:, 20 + d, :]), chunks(SC[:, 20 + d, :]), over(cm(CUM[d])),
                                           ALU.mult)
                last.then_inc(sem("gdn_Em"), 1)
                pool.wait_ge(sem("gdn_rn"), t + 1)
                G.tensor_tensor(ks[:, 0, :, :], beta[:, i, :, :], over(rn[:, 1, :], 2), ALU.mult)
                G.tensor_copy(tot[:, :, :], eg[:, :, 2, i, :])
                link(G.tensor_scalar(rq[:, :], rn[:, 0, :], HD ** -0.5, None, ALU.mult))
                G.tensor_tensor(ks[:, 1, :, :], eg[:, :, 0, i, :], over(rq[:, :], 2), ALU.mult)
                G.tensor_tensor(ks[:, 2, :, :], eg[:, :, 1, i, :], over(rn[:, 1, :], 2), ALU.mult)
                G.tensor_tensor(ks[:, 3, :, :], beta[:, i, :, :], eg[:, :, 0, i, :], ALU.mult)\
                    .then_inc(sem("gdn_ks"), 1)
                pool.wait_ge(sem("gdn_ks"), t + 1)
                pool.wait_ge(sem("gdn_tokc"), t + 1)
                pool.wait_ge(sem("gdn_ss"), t + 1)
                for d in range(2):
                    last = G.tensor_tensor(chunks(SC[:, d, :]), chunks(SC[:, 3, :]), along(ks[:, 1, d, :]), ALU.mult)
                last.then_inc(sem("gdn_sc"), 1)
                pool.wait_ge(sem("gdn_gs"), t + 1)
                G.tensor_tensor(SC[:, 2, lo:], SC[:, 2, lo:], act[:, i + Y_GDN, lo:], ALU.mult)\
                    .then_inc(sem("gdn_silu"), 1)
                for d in range(2):
                    G.tensor_tensor(chunks(SC[:, 12 + d, :]), chunks(SC[:, 5, :]), along(beta[:, i, d, :]), ALU.mult)
                    last = G.tensor_tensor(chunks(SC[:, 10 + d, :]), chunks(SC[:, 4, :]), along(ks[:, 2, d, :]),
                                           ALU.mult)
                level0 = (C_UP, C_LO)
                pool.wait_ge(sem("gdn_T1"), 4 * t + 4)
                for d in range(2):
                    pool.wait_ge(sem("gdn_U"), 2 * t + d + 1)
                    link(G.tensor_tensor(chunks(SC[:, 8 + d, :]), chunks(SC[:, 22 + d, :]), over(cm(level0[d])),
                                         ALU.mult))
                    G.tensor_tensor(chunks(SC[:, 8 + d, :]), over(ident), chunks(SC[:, 8 + d, :]), ALU.subtract)\
                        .then_inc(sem("gdn_M0"), 1)
                pool.wait_ge(sem("gdn_y"), t + 1)

            for l in range(DEPTH):
                lo = 0 if l == 0 else CTX
                pool.wait_ge(sem("beta_ready"), l + 1)
                pool.wait_ge(sem("gdn_eg"), l + 1)
                o.straight()
                for rounds, first in GDN_LOOPS[l]:
                    with pool.Fori(0, rounds) as i:
                        o.round(i, GDN_POOL)
                        gdn(i + first, i + (4 * l + first), l, lo)
                    o.close(rounds)
                n = segs[(l, "p3")][1]
                pool.wait_ge(sem("bank0_free"), n // 2)
                pool.wait_ge(sem("bank1_free"), n // 2)
                pool.wait_ge(sem("wdec_in"), 32 * (l + 1))
                with pool.Fori(0, 2) as i:
                    t = i + 2 * l
                    G.tensor_copy(wdp, wdec[:, :, bass.ds(i * 128, 128)])
                    G.tensor_copy(SC[:, 16:18, :], act[:, bass.ds(i * 2 + (T_B + 4), 2), :]).then_inc(sem("gla_stat"), 1)
                    pool.wait_ge(sem("gla_ek"), t + 1)
                    for d in range(2):
                        last = G.tensor_tensor(SC[:, 12 + d, :], act[:, i + (T_B + 2), :], SC[:, 8 + d, :], ALU.mult)
                    last.then_inc(sem("gla_kd"), 1)
                    pool.wait_ge(sem("gla_gsig"), t + 1)
                    G.tensor_tensor(SC[:, 16:18, lo:], SC[:, 16:18, lo:], act[:, bass.ds(i * 2 + Y_GLA, 2), lo:],
                                    ALU.mult).then_inc(sem("gla_silu"), 1)
                    pool.wait_ge(sem("gla_y"), t + 1)
                n = segs[(l, "p4")][1]
                pool.wait_ge(sem("bank0_free"), n // 2)
                pool.wait_ge(sem("bank1_free"), n // 2)
                with pool.Fori(0, 2) as i:
                    t = i + 2 * l
                    G.tensor_copy(SC[:, 0:2, :], act[:, bass.ds(i * 2, 2), :])
                    G.tensor_copy(SC[:, 2, :], act[:, i + 4, :])
                    G.tensor_copy(SC[:, 3, :], act[:, i + 6, :]).then_inc(sem("swa_stat"), 1)
                    pool.wait_ge(sem("swa_gs"), t + 1)
                    G.tensor_tensor(SC[:, 22:24, lo:], SC[:, 22:24, lo:], act[:, bass.ds(i * 2 + Y_SWA, 2), lo:],
                                    ALU.mult).then_inc(sem("swa_silu"), 1)
                    pool.wait_ge(sem("swa_y"), t + 1)
                pool.wait_ge(sem("sc_y"), 4 * l + 4)
                link(G.memset(SC[:, 0, lo:], 0.0))
                if l == 0:
                    pool.sem_inc(sem("yo_round"), 1)
                n = segs[(l, "out")][1]
                o.straight()
                with pool.Fori(0, 4) as i:
                    for tt in range(4):
                        b = (n + tt) % 2
                        pool.wait_ge(sem(f"bank{b}_free"), i * 2 + ((n + tt) // 2 + 1))
                        G.tensor_tensor(SC[:, 0, lo:], SC[:, 0, lo:], SC[:, 4 + tt % 2, lo:], ALU.add)\
                            .then_inc(sem("yo_add"), 1)
                        pool.wait_ge(sem("yo_add"), i * 4 + (16 * l + tt + 1))
                    pool.sem_inc(sem("yo_round"), 1)
                pool.sem_inc(sem("sumsq_ready"), 1)
                pool.wait_ge(sem("h_back"), 16 * (l + 1))
                with pool.Fori(0, KT) as k:
                    pool.wait_ge(sem("yo_scaled"), k + (KT * l + 1))
                    G.tensor_tensor(N[:, k, lo:], N[:, k, lo:], act[:, k, lo:], ALU.add).then_inc(sem("h_add"), 1)
                pool.wait_ge(sem("h_add"), KT * (l + 1))
                pool.sem_inc(sem("yo_used"), 1)
                pool.sem_inc(sem("h_ready"), 1)
                if l == 0:
                    pool.wait_ge(sem("chansum_done"), 2)
                    square_sum(0)


GDN_LOOPS = (((4, 0),), ((2, 0), (2, 2)))
CONV_ACT, GDN_ACT, GLA_ACT, SWA_ACT, SC_ACT = 8, 4, 5, 2, 2
CONV_DVE = 28
GDN_DVE = 9
GLA_DVE = 16
SWA_DVE = 17
SC_DVE = 8
GDN_POOL = 3


def kernel(**inputs):
    import concourse.bacc as bacc
    from concourse.bass_utils import run_bass_kernel_spmd

    nc = bacc.Bacc("TRN2", target_bir_lowering=False, num_devices=1)
    f32 = mybir.dt.float32
    arrays = {
        "x": np.asarray(inputs["x"]).reshape(SEQ, D),
        "ctx": np.asarray(inputs["ctx"]).reshape(CTX, D),
        "ada_w": np.asarray(inputs["ada_w"]),
        "w_in": np.asarray(inputs["w_in"]),
        "w_out": np.asarray(inputs["w_out"]),
        "w_decay": np.asarray(inputs["gla_w_decay"]),
        "params": parameters(inputs),
        "consts": constants(),
    }
    args = [nc.dram_tensor(n, a.shape, f32, kind="ExternalInput").ap() for n, a in arrays.items()]
    out = nc.dram_tensor("out", (SEQ, D), f32, kind="ExternalOutput").ap()
    build(nc, *args, out)
    r = run_bass_kernel_spmd(nc, [arrays], core_ids=[0])
    return r.results[0]["out"].reshape(1, SEQ, D)
```

```python
import numpy as np
import concourse.bass as bass
from concourse import mybir
from contextlib import ExitStack

D = 2048
SEQ = 256
CTX = 256
TOK = SEQ + CTX
DEPTH = 2
KT = D // 128
HD = 128
CH = 128
NC = TOK // CH
EPS = 1e-6
GRID_W = 64
ROPE_BASE = 10000.0
NEG = -1e30

GLA_QKV, GLA_LR, GLA_GATE = 0, 1024, 1056
GDN_QKV, GDN_AB, GDN_GATE = 1568, 3104, 3120
SC_ALL = 3632
SWA_QKV, SWA_GATE = 5680, 6704
IN_WIDTH = 7216
NLR, NAB = 32, 16

T_A, T_B = 0, 12
Y_GLA, Y_SWA, Y_GDN, Y_SC = 20, 24, 28, 32
NTILES = 36
Y_ORDER = [Y_GLA + i for i in range(4)] + [Y_GDN + i for i in range(4)] + \
          [Y_SC + i for i in range(4)] + [Y_SWA + i for i in range(4)]
RING = 4
WSCALE = 256.0
CLAMP = -40.0

C_IDENT, C_ONES, C_PERM = 0, 128, 256
C_CUMF, C_CUMB, C_TAILF, C_TAILB = 384, 512, 640, 768
C_LO = 896
C_UP = C_LO + 7 * 128
C_COS = C_UP + 7 * 128
C_SIN = C_COS + SEQ
C_MASK = C_SIN + SEQ
C_SEG = C_MASK + 2 * SEQ
C_EPS = C_SEG + TOK
C_ZERO = C_EPS + 1
C_ONE = C_EPS + 2
C_SEL = C_EPS + 3
CW = C_EPS + 5

P_ADAB, P_NPRE, P_NPOST = 0, 48, 64
P_GLAB, P_GLAN = 80, 84
P_CONV, P_GDNN = 85, 145
P_SCW, P_ALOG, P_DT, P_SINK = 146, 158, 166, 174
PL = 178
P_C = DEPTH * PL
PW = P_C + 2 * KT


def constants():
    c = np.zeros((128, CW), np.float32)
    p = np.arange(128)[:, None]
    f = np.arange(128)[None, :]
    c[:, C_IDENT:C_IDENT + 128] = p == f
    c[:, C_ONES:C_ONES + 128] = 1.0
    swap = (f // 64) * 64 + (f % 64 + 32) % 64
    c[:, C_PERM:C_PERM + 128] = p == swap
    c[:, C_CUMF:C_CUMF + 128] = p <= f
    c[:, C_CUMB:C_CUMB + 128] = p >= f
    c[:, C_TAILF:C_TAILF + 128] = p > f
    c[:, C_TAILB:C_TAILB + 128] = p < f
    for lv in range(7):
        lo = (p >> (lv + 1) == f >> (lv + 1)) & ((p >> lv & 1) == 1) & ((f >> lv & 1) == 0)
        c[:, C_LO + 128 * lv:C_LO + 128 * lv + 128] = lo
        c[:, C_UP + 128 * lv:C_UP + 128 * lv + 128] = lo.T
    t = np.arange(SEQ)
    inv = ROPE_BASE ** (-np.arange(0, 64, 2, dtype=np.float64) / 64)
    for half, pos in ((0, t // GRID_W), (1, t % GRID_W)):
        ang = inv[:, None] * pos[None, :]
        for q, sign in ((0, -1.0), (1, 1.0)):
            r = half * 64 + q * 32
            c[r:r + 32, C_COS:C_COS + SEQ] = np.cos(ang)
            c[r:r + 32, C_SIN:C_SIN + SEQ] = sign * np.sin(ang)
    for b in range(2):
        far = np.abs(128 * b + p - t[None, :]) > 128
        c[:, C_MASK + b * SEQ:C_MASK + (b + 1) * SEQ] = np.where(far, NEG, 0.0)
    c[:, C_SEG:C_SEG + TOK] = (np.arange(TOK) % CH != 0)
    c[:, C_EPS] = EPS
    c[:, C_ONE] = 1.0
    c[:, C_SEL:C_SEL + 2] = p % 32 == f[:, 0:2]
    return c


def parameters(i):
    def chan(a):
        return np.ascontiguousarray(np.asarray(a, np.float32).reshape(-1, 128).T)

    def rep(a):
        a = np.asarray(a, np.float32).reshape(1, -1)
        return np.repeat(a, 128, axis=0)
    cols = []
    for l in range(DEPTH):
        cols += [chan(i["ada_b"][l]), chan(i["norm_pre"][l]), chan(i["norm_post"][l]),
                 chan(i["gla_b_decay"][l]), chan(i["gla_norm"][l]),
                 np.asarray(i["gdn_conv"][l]).reshape(5, 12, 128).transpose(2, 1, 0).reshape(128, 60),
                 chan(i["gdn_norm"][l]),
                 np.asarray(i["sc_conv"][l]).reshape(3, 4, 128).transpose(2, 1, 0).reshape(128, 12),
                 rep(i["gdn_a_log"][l]), rep(i["gdn_dt_bias"][l]), rep(i["swa_sink"][l])]
    cc = np.stack([np.asarray(i["c_ctx"]).reshape(KT, 128), np.asarray(i["c"]).reshape(KT, 128)], 0)
    cols.append(cc.transpose(2, 1, 0).reshape(128, 2 * KT))
    return np.ascontiguousarray(np.concatenate(cols, axis=1))


class Order:

    def __init__(self, eng, sem):
        self.eng, self.sem, self.base, self.k, self.n, self.i = eng, sem, 0, 0, 0, 0

    def round(self, i, n):
        self.i, self.n, self.k = i, n, 0

    def done(self, ins):
        ins.then_inc(self.sem, 1)
        self.k += 1
        return self.k

    def wait(self, k=None):
        self.eng.wait_ge(self.sem, self.i * self.n + (self.base + (self.k if k is None else k)))

    def straight(self):
        self.base += self.k
        self.i = self.n = self.k = 0

    def close(self, rounds):
        assert self.k == self.n, f"{self.k} steps in a round, {self.n} declared"
        self.base += rounds * self.n
        self.i = self.n = self.k = 0


def build(nc, x_d, ctx_d, ada_d, win_d, wout_d, wdec_d, par_d, con_d, out_d):
    f32, f16 = mybir.dt.float32, mybir.dt.float16
    ALU = mybir.AluOpType
    ACT = mybir.ActivationFunctionType
    AX = mybir.AxisListType.X
    es = ExitStack()
    with es:
        def sb(name, shape):
            return es.enter_context(nc.sbuf_tensor(name, shape, f32))

        sems = {}

        def sem(name):
            if name not in sems:
                sems[name] = es.enter_context(nc.semaphore(name))
            return sems[name]

        con = sb("con", [128, CW])
        par = sb("par", [128, PW])
        N = sb("N", [128, KT, TOK])
        act = sb("act", [128, NTILES, TOK])
        ring = sb("ring", [128, RING, KT, 128])
        wdec = sb("wdec", [NLR, 2, 256])
        wab = act[:, Y_SC, 0:KT * NAB].rearrange("p (k n) -> p k n", n=NAB)
        wlr = act[:, Y_SC + 1, 0:KT * NLR].rearrange("p (k n) -> p k n", n=NLR)
        lrT = act[0:NLR, Y_SC + 3, :]
        wdp = act[0:NLR, Y_SC + 2, 0:256].rearrange("r (d n) -> r d n", d=2)
        SC = sb("SC", [128, 24, TOK])
        ab = act[:, Y_SC + 2, 256:256 + NC * NAB].rearrange("p (c k) -> p c k", k=NAB)
        wab16 = act[:, Y_SC, 256:512].bitcast(f16).rearrange("p (h k n) -> p h k n", h=2, n=NAB)
        wlr16 = act[:, Y_SWA, :].bitcast(f16).rearrange("p (h k n) -> p h k n", h=2, n=NLR)
        st = SC[:, 6, 0:256].rearrange("p (d v) -> p d v", d=2)
        vn = SC[:, 6, 256:512].rearrange("p (d v) -> p d v", d=2)
        rr = SC[:, 7, 0:256].rearrange("p (d v) -> p d v", d=2)
        cs = sb("cs", [128, KT, 2])
        csp = SC[:, 7, :].rearrange("p (k m) -> p k m", m=32)
        cst = sb("cst", [128, KT, 2])
        ada = sb("ada", [128, DEPTH, 48, 2])
        modA = sb("modA", [128, DEPTH, KT, 2])
        modG = sb("modG", [128, DEPTH, KT, 2])
        gz = sb("gz", [128, NC, 2, 4])
        gt = sb("gt", [128, NC, 2, 4])
        expA = sb("expA", [128, 2, 4])
        g = sb("g", [128, 5, 2, NC])
        beta = sb("beta", [128, 4, 2, NC])
        eg = sb("eg", [128, 2, 3, 4, NC])
        rn = sb("rn", [128, 2, NC])
        rq = sb("rq", [128, NC])
        ks = sb("ks", [128, 4, 2, NC])
        tot = sb("tot", [128, 2, NC])
        gs = sb("gs", [128, 3, 2, NC])
        gd = sb("gd", [128, 2, NC])
        sm = sb("sm", [128, 6, 8])
        ps = [es.enter_context(nc.psum_tensor(f"bank{i}", [128, 512], f32)) for i in range(8)]
        h_d = nc.dram_tensor("h_spill", (128, KT, TOK), f32, kind="Internal").ap()

        ident = con[:, C_IDENT:C_IDENT + 128]
        ones = con[:, C_ONES:C_ONES + 128]
        one1 = con[:, C_ONE:C_ONE + 1]
        eps = con[:, C_EPS:C_EPS + 1]
        CUM = (C_CUMF, C_CUMB)
        TAIL = (C_TAILF, C_TAILB)

        def cm(at):
            return con[:, at:at + 128]

        def over(a, n=NC):
            return a.unsqueeze(1).to_broadcast([128, n, a.shape[1]])

        def along(a, m=128):
            return a.unsqueeze(2).to_broadcast([128, a.shape[1], m])

        def chunks(a):
            return a.rearrange("p (c t) -> p c t", t=128)

        def pair(a):
            return a.bitcast(f16).rearrange("p (h t) -> p h t", h=2)

        def halves(s):
            return ring[:, 2 + s, :, :].rearrange("p k n -> p (k n)").bitcast(f16)\
                .rearrange("p (k h n) -> p k h n", h=2, n=128)

        def quarter(s):
            return ring[:, s, :, :].rearrange("p k n -> p (k n)").rearrange("p (k n) -> p k n", n=512)

        def P(l, at, n=1):
            return par[:, l * PL + at:l * PL + at + n]

        def bank_wait(pe, n0, i, tb, tt):
            pe.wait_ge(sem(f"bank{(n0 + tt) % 2}_free"), i * (tb // 2) + (n0 + tt) // 2)

        def out_wait(eng, n0, i, tb, tt):
            eng.wait_ge(sem(f"bank{(n0 + tt) % 2}_full"), i * (tb // 2) + ((n0 + tt) // 2 + 1))

        segs = {}
        seq = []
        wt0, n0 = 0, 16
        for l in range(DEPTH):
            for name, dram, col, tiles in (
                    [("ada0", None, 0, 24)] if l == 0 else []) + [
                    ("gdn", win_d[l], GDN_QKV, 12), ("small", None, 0, 2),
                    ("gdng", win_d[l], GDN_GATE, 4),
                    ("p2", None, 0, 16), ("p3", win_d[l], SWA_QKV, 8), ("p4", win_d[l], SC_ALL, 16),
                    ("out", wout_d[l], 0, 16)] + ([("ada1", None, 0, 24)] if l == 0 else []):
                segs[(l, name)] = (wt0, n0)
                if name == "p2":
                    seq += [(win_d[l], GLA_QKV, 8), (win_d[l], GLA_GATE, 4), (win_d[l], SWA_GATE, 4)]
                elif name == "out":
                    seq += [(dram, 0, 4), (dram, 4 * 128, 12)]
                elif dram is not None:
                    seq.append((dram, col, tiles))
                if name[:3] != "ada" and name != "small":
                    wt0 += tiles
                n0 += tiles
        segs["end"] = (wt0, n0)

        block = es.enter_context(nc.Block())

        @block.sync
        def _(sp):
            sp.dma_start(con[:, :], con_d).then_inc(sem("con_in"), 16)
            sp.dma_start(par[:, :], par_d).then_inc(sem("par_in"), 16)
            xin = act[:, 0:16, :].rearrange("p a t -> p (a t)").rearrange("p (b d) -> p b d", b=4)
            sp.dma_start(xin[:, 0:2, :], ctx_d.rearrange("(b p) d -> p b d", p=128)).then_inc(sem("x_in"), 16)
            sp.dma_start(xin[:, 2:4, :], x_d.rearrange("(b p) d -> p b d", p=128)).then_inc(sem("x_in"), 16)
            sp.wait_ge(sem("wdec_zero"), 1)

            def ada_weights(l, rounds, first):
                with sp.Fori(0, rounds) as i:
                    for s in range(RING):
                        sp.wait_ge(sem(f"slot{s}_free"), i + (12 * l + first + 1))
                        src = ada_d[l][s * 512:(s + 1) * 512, bass.ds(i * 512 + first * 512, 512)]
                        sp.dma_start(quarter(s), src.rearrange("(k p) n -> p k n", p=128))\
                            .then_inc(sem(f"slot{s}_full"), 16)

            def weights(dram, col, tiles, base):
                with sp.Fori(0, tiles // RING) as i:
                    for tt in range(RING):
                        sp.wait_ge(sem(f"stage{tt % 2}_split"), i * (RING // 2) + ((base + tt) // 2 + 1))
                        src = dram[:, bass.ds(i * (RING * 128) + (col + tt * 128), 128)]
                        sp.dma_start(ring[:, tt % 2, :, :], src.rearrange("(k p) n -> p k n", p=128))\
                            .then_inc(sem(f"stage{tt % 2}_full"), 16)

            base = 0
            it = iter(seq)

            def nxt(count):
                nonlocal base
                for _ in range(count):
                    dram, col, tiles = next(it)
                    weights(dram, col, tiles, base)
                    base += tiles

            for l in range(DEPTH):
                sp.wait_ge(sem("yo_used"), l)
                sp.dma_start(wab, win_d[l][:, GDN_AB:GDN_AB + NAB].rearrange("(k p) n -> p k n", p=128))\
                    .then_inc(sem("small_in"), 16)
                sp.dma_start(wlr, win_d[l][:, GLA_LR:GLA_LR + NLR].rearrange("(k p) n -> p k n", p=128))\
                    .then_inc(sem("small_in"), 16)
                if l:
                    sp.wait_ge(sem("gla_stat"), 2 * l)
                for d in range(2):
                    sp.dma_start(wdec[16 * d:16 * d + 16, d, :], wdec_d[l, d]).then_inc(sem("wdec_in"), 16)
                if l == 0:
                    ada_weights(0, *ADA_NORM)
                sp.wait_ge(sem("h_ready"), l + 1)
                lo = CTX * l
                sp.dma_start(h_d[:, :, lo:], N[:, :, lo:]).then_inc(sem("h_saved"), 16)
                ada_weights(l, *ADA_GATE)
                for s in range(2):
                    sp.wait_ge(sem(f"slot{s}_free"), 12 * (l + 1) + 1)
                nxt(2 + 3 + 1 + 1)
                nxt(1)
                sp.wait_ge(sem("norm_used"), l + 1)
                sp.wait_ge(sem("h_saved"), 16 * (l + 1))
                sp.dma_start(N[:, :, lo:], h_d[:, :, lo:]).then_inc(sem("h_back"), 16)
                nxt(1)
                if l == 0:
                    sp.wait_ge(sem("layer_multiplied"), 1)
                    ada_weights(1, *ADA_NORM)
            for j in range(8):
                q, b = divmod(j, 2)
                sp.wait_ge(sem("out_staged"), j + 1)
                sp.dma_start(out_d[b * 128:(b + 1) * 128, q * 512:(q + 1) * 512], SC[:, 8 + j, :])\
                    .then_inc(sem("out_sent"), 16)
            sp.wait_ge(sem("out_sent"), 8 * 16)

        @block.tensor
        def _(pe):
            def mm(out, a, b, start=True, stop=True):
                return nc.tensor.matmul(out, a, b, start=start, stop=stop, skip_group_check=True)

            def tp(out, a):
                return nc.tensor.transpose(out, a, ident[0:a.shape[0], 0:a.shape[0]])

            def pairs(out, ah, al, bh, bl, first, last):
                mm(out, ah, bh, first, False)
                mm(out, ah, bl, False, False)
                return mm(out, al, bh, False, last)

            def ada_rows(l, rounds, first):
                n = segs[(0, f"ada{l}")][1] + 2 * first
                with pe.Fori(0, rounds) as i:
                    bank_wait(pe, n, i, 2, 0)
                    for s in range(RING):
                        pe.wait_ge(sem(f"slot{s}_full"), i * 16 + 16 * (12 * l + first + 1))
                        for j in range(4):
                            last = mm(ps[0][32 * j:32 * j + 32, :], csp[:, 4 * s + j, :], quarter(s)[:, j, :],
                                      s == 0, s == RING - 1)
                        last.then_inc(sem(f"slot{s}_free"), 1)
                    pe.wait_ge(sem("slot3_free"), i + (12 * l + first + 2))
                    pe.sem_inc(sem("bank0_full"), 1)
                    bank_wait(pe, n, i, 2, 1)
                    pe.wait_ge(sem("bank0_free"), i + (n // 2 + 1))
                    for s in range(RING):
                        last = mm(ps[1][:, 2 * s:2 * s + 2], SC[:, 6, s * 128:(s + 1) * 128],
                                  con[:, C_SEL:C_SEL + 2])
                    last.then_inc(sem("bank1_full"), 1)

            class Fill:

                def __init__(self, l, name, tb, i, lo, rhs=None, off=0, korder=range(KT)):
                    self.korder = korder
                    self.wt0, self.n0 = segs[(l, name)]
                    self.n0 += off
                    self.wt0 += off
                    self.tb, self.i, self.lo, self.at = tb, i, lo, 0
                    self.rhs = rhs or (lambda k: pair(N[:, k, :])[:, :, lo:])

                def __call__(self, steps):
                    for _ in range(steps):
                        if self.at == self.tb * KT:
                            return
                        tt, k = divmod(self.at, KT)
                        s = (self.wt0 + tt) % 2
                        if k == 0:
                            pe.wait_ge(sem(f"stage{s}_split"),
                                       self.i * (self.tb // 2) + ((self.wt0 + tt) // 2 + 2))
                            bank_wait(pe, self.n0, self.i, self.tb, tt)
                        w = halves(s)
                        x = self.rhs(k)
                        b = (self.n0 + tt) % 2
                        kw = self.korder[k]
                        last = pairs(ps[b][:, 0:x.shape[-1]], w[:, kw, 0, :], w[:, kw, 1, :], x[:, 0, :], x[:, 1, :],
                                     k == 0, k == KT - 1)
                        if k == KT - 1:
                            last.then_inc(sem(f"bank{b}_full"), 1)
                        self.at += 1

                def rest(self):
                    self(self.tb * KT - self.at)

            for s in range(RING):
                pe.sem_inc(sem(f"slot{s}_free"), 1)
            pe.wait_ge(sem("con_in"), 16)
            pe.wait_ge(sem("x_in"), 32)
            xin = act[:, 0:16, :].rearrange("p a t -> p (a t)").rearrange("p (b d) -> p b d", b=4)
            for k in range(KT):
                bank_wait(pe, 0, 0, KT, k)
                for b in range(4):
                    last = tp(ps[k % 2][:, b * 128:(b + 1) * 128], xin[:, b, k * 128:(k + 1) * 128])
                last.then_inc(sem(f"bank{k % 2}_full"), 1)
            pe.wait_ge(sem("cs_ready"), 1)
            ada_rows(0, *ADA_NORM)

            def channel_sum(t, width0):
                pe.wait_ge(sem("sumsq_ready"), t + 1)
                mm(ps[2][:, width0:], ones, SC[:, 0, width0:]).then_inc(sem("chansum_done"), 1)

            def gdn(i, t, l, fill):
                pe.wait_ge(sem("gdn_rg"), t + (l + 1))
                for d in range(2):
                    last = mm(ps[5 + d][:, :], cm(TAIL[d]), SC[:, 16 + d, :])
                last.then_inc(sem("gdn_D"), 1)
                fill(4)
                pe.wait_ge(sem("gdn_x"), t + 1)
                for j in range(3):
                    for c in range(NC):
                        last = tp(ps[2 + j][:, c * 128:(c + 1) * 128], SC[:, j, c * 128:(c + 1) * 128])
                last.then_inc(sem("gdn_tok"), 1)
                fill(10)
                pe.wait_ge(sem("gdn_kn"), t + 1)
                pe.wait_ge(sem("gdn_E"), t + 1)
                for src, b in ((7, 5), (8, 2), (9, 3), (6, 6)):
                    for c in range(NC):
                        last = tp(ps[b][:, c * 128:(c + 1) * 128], SC[:, src, c * 128:(c + 1) * 128])
                    last.then_inc(sem("gdn_T1"), 1)
                fill(4)
                pe.wait_ge(sem("gdn_T1c"), 4 * t + 4)
                for a, b, bank in ((14, 15, 5), (14, 16, 4), (14, 17, 7)):
                    for c in range(NC):
                        s = slice(c * 128, (c + 1) * 128)
                        last = mm(ps[bank][:, s], SC[:, a, s], SC[:, b, s])
                    last.then_inc(sem("gdn_G"), 1)
                pe.wait_ge(sem("gdn_sc"), t + 1)
                for d, bank in ((0, 6), (1, 2)):
                    for c in range(NC):
                        last = tp(ps[bank][:, c * 128:(c + 1) * 128], SC[:, d, c * 128:(c + 1) * 128])
                    last.then_inc(sem("gdn_T2"), 1)
                fill(2)
                pe.wait_ge(sem("gdn_U"), 2 * t + 2)
                for d, bank in ((0, 3), (1, 4)):
                    for c in range(NC):
                        s = slice(c * 128, (c + 1) * 128)
                        last = tp(ps[bank][:, s], SC[:, 22 + d, s])
                    last.then_inc(sem("gdn_P"), 1)
                fill(2)
                pe.wait_ge(sem("gdn_T2c"), 2 * t + 2)
                for lv in range(1, 7):
                    for d in range(2):
                        pe.wait_ge(sem("gdn_T"), 12 * t + 2 * (lv - 1) + d + 1)
                        if lv == 1 and d == 1:
                            pe.wait_ge(sem("gdn_T"), 12 * t + 2)
                        for c in range(NC):
                            s = slice(c * 128, (c + 1) * 128)
                            last = mm(ps[2 + d][:, s], SC[:, 22 + d, s], SC[:, 6 + d, s])
                        last.then_inc(sem("gdn_P"), 1)
                    fill(2)
                    for d in range(2):
                        pe.wait_ge(sem("gdn_Pm"), 12 * t + 2 * (lv - 1) + d + 1)
                        if lv == 1:
                            pe.wait_ge(sem("gdn_M0"), 2 * t + d + 1)
                        else:
                            pe.wait_ge(sem("gdn_M"), 10 * t + 2 * (lv - 2) + d + 1)
                        if lv < 6:
                            for c in range(NC):
                                s = slice(c * 128, (c + 1) * 128)
                                last = mm(ps[4 + d][:, s], SC[:, 8 + d, s], SC[:, 16 + d, s])
                            last.then_inc(sem("gdn_Y"), 1)
                        for c in range(NC):
                            s = slice(c * 128, (c + 1) * 128)
                            last = mm(ps[6 + d][:, s], SC[:, 16 + d, s], SC[:, 8 + d, s])
                        last.then_inc(sem("gdn_YT"), 1)
                    fill(2)
                pe.wait_ge(sem("gdn_Mlast"), t + 1)
                pe.wait_ge(sem("gdn_AT"), t + 1)
                pe.wait_ge(sem("gdn_vk"), t + 1)
                first = True
                for s in range(NC):
                    cc = (s, (1, 0, 3, 2)[s])
                    if s > 0:
                        pe.wait_ge(sem("gdn_S"), 3 * t + s)
                        for d in range(2):
                            c = slice(cc[d] * 128, cc[d] * 128 + 128)
                            last = mm(ps[2][:, d * 128:d * 128 + 128], SC[:, 14, c], st[:, d, :])
                        last.then_inc(sem("gdn_KS"), 1)
                        pe.wait_ge(sem("gdn_r"), 3 * t + s)
                    for d in range(2):
                        c = slice(cc[d] * 128, cc[d] * 128 + 128)
                        last = mm(ps[3][:, d * 128:d * 128 + 128], SC[:, 8 + d, c],
                                  rr[:, d, :] if s else SC[:, 12 + d, c])
                    last.then_inc(sem("gdn_vn"), 1)
                    if s > 0:
                        for d in range(2):
                            c = slice(cc[d] * 128, cc[d] * 128 + 128)
                            mm(ps[5][:, c], st[:, d, :], SC[:, 18 + d, c], start=first, stop=True)
                            first = False
                    fill(2)
                    pe.wait_ge(sem("gdn_vnc"), 4 * t + s + 1)
                    if s < NC - 1:
                        for d in range(2):
                            c = slice(cc[d] * 128, cc[d] * 128 + 128)
                            last = mm(ps[4][:, d * 128:d * 128 + 128], SC[:, 10 + d, c], vn[:, d, :])
                        last.then_inc(sem("gdn_dS"), 1)
                    for d in range(2):
                        c = slice(cc[d] * 128, cc[d] * 128 + 128)
                        last = mm(ps[5][:, c], vn[:, d, :], SC[:, 20 + d, c], start=first, stop=True)
                        first = False
                    if s == NC - 1:
                        last.then_inc(sem("gdn_o"), 1)
                    fill(2)
                pe.wait_ge(sem("gdn_osq"), t + 1)
                mm(ps[6][:, :], ones, SC[:, 1, :]).then_inc(sem("gdn_oss"), 1)
                fill.rest()
                pe.wait_ge(sem("gdn_orn"), t + 1)

            def gla(i, t, l, fill):
                fill(10)
                pe.wait_ge(sem("gla_wd"), t + 1)
                pe.wait_ge(sem("lr_copied"), l + 1)
                for d in range(2):
                    last = mm(ps[2 + d][:, :], wdp[:, d, :], lrT)
                last.then_inc(sem("gla_z"), 1)
                pe.wait_ge(sem("gla_stat"), t + 1)
                for a in range(2):
                    for c in range(NC):
                        s = slice(c * 128, (c + 1) * 128)
                        last = tp(ps[4 + a][:, s], SC[:, 16 + a, s])
                last.then_inc(sem("gla_vt"), 1)
                fill(30)
                pe.wait_ge(sem("gla_kd"), t + 1)
                pe.wait_ge(sem("gla_zc"), t + 1)
                for d in range(2):
                    for c in range(NC):
                        s = slice(c * 128, (c + 1) * 128)
                        last = tp(ps[2 + d][:, s], SC[:, 12 + d, s])
                last.then_inc(sem("gla_kt"), 1)
                pe.wait_ge(sem("gla_qd"), t + 1)
                for a in range(2):
                    for d in range(2):
                        bank = (6, 7, 2, 3)[2 * a + d]
                        if a == 1 and d == 0:
                            fill(8)
                            pe.wait_ge(sem("gla_ktc"), t + 1)
                        for c in range(NC):
                            s = slice(c * 128, (c + 1) * 128)
                            last = mm(ps[bank][:, s], SC[64 * a:64 * a + 64, 12 + d, s],
                                      SC[64 * a:64 * a + 64, 10 + d, s])
                        last.then_inc(sem("gla_att"), 1)
                pe.wait_ge(sem("gla_vtc"), t + 1)
                for d in range(2):
                    for a in range(2):
                        for c in range(NC):
                            s = slice(c * 128, (c + 1) * 128)
                            last = mm(ps[4 + d][64 * a:64 * a + 64, s],
                                      SC[:, 14 + d, c * 128 + 64 * a:c * 128 + 64 * a + 64], SC[:, 18 + a, s])
                last.then_inc(sem("gla_dS"), 1)
                fill(12)
                pe.wait_ge(sem("gla_S"), t + 1)
                pe.wait_ge(sem("gla_AT"), t + 1)
                for a in range(2):
                    first = True
                    for c in range(NC):
                        s = slice(c * 128, (c + 1) * 128)
                        for d in range(2):
                            last = mm(ps[6 + a][:, s], SC[:, 18 + a, s], SC[:, 20 + 2 * a + d, s], start=first)
                            first = False
                            step = (c, (1, 0, 3, 2)[c])[d]
                            if step:
                                last = mm(ps[6 + a][:, s],
                                          SC[64 * a:64 * a + 64, d, (step - 1) * 128:step * 128],
                                          SC[64 * a:64 * a + 64, 10 + d, s], start=False)
                    last.then_inc(sem("gla_o"), 1)
                fill(2)
                for a in range(2):
                    pe.wait_ge(sem("gla_osq"), 2 * t + a + 1)
                    mm(ps[2 + a][:, :], ones, SC[:, 4 + a, :]).then_inc(sem("gla_oss"), 1)
                fill.rest()

            def swa(i, t, l, fill, blocks):
                nb = len(blocks)
                before = i * 2 * nb + swa_blocks(l)
                fill(20)
                pe.wait_ge(sem("swa_stat"), t + 1)
                for j in range(3):
                    last = mm(ps[2 + j // 2][:, (j % 2) * 256:(j % 2) * 256 + 256], cm(C_PERM), SC[:, j, CTX:])
                last.then_inc(sem("swa_rot"), 1)
                for c in range(NC):
                    s = slice(c * 128, (c + 1) * 128)
                    last = tp(ps[4][:, s], SC[:, 3, s])
                last.then_inc(sem("swa_vt"), 1)
                fill(10)
                pe.wait_ge(sem("swa_rope"), t + 1)
                for j, (a, b) in enumerate((a, b) for a in range(2) for b in blocks):
                    n = TOK if b >= 2 else CTX
                    if j >= 2:
                        pe.wait_ge(sem("swa_sc"), before + (j - 1))
                    mm(ps[5 + j % 2][:, 0:n], SC[:, a, b * 128:(b + 1) * 128], SC[:, 2, 0:n])\
                        .then_inc(sem("swa_s"), 1)
                fill(30)
                for j, (a, b) in enumerate((a, b) for a in range(2) for b in blocks):
                    n = TOK if b >= 2 else CTX
                    pe.wait_ge(sem("swa_p"), before + (j + 1))
                    if j >= 2:
                        pe.wait_ge(sem("swa_pTc"), before + (j - 1))
                    for c in range(n // 128):
                        last = tp(ps[2 + j % 2][:, c * 128:(c + 1) * 128], SC[:, 6 + j, c * 128:(c + 1) * 128])
                    last.then_inc(sem("swa_pT"), 1)
                    fill(16 // (2 * nb))
                    if j > 0:
                        attend(j - 1, t, before, blocks)
                attend(2 * nb - 1, t, before, blocks)
                fill.rest()

            def attend(j, t, before, blocks):
                nb = len(blocks)
                a, b = j // nb, blocks[j % nb]
                n = TOK if b >= 2 else CTX
                pe.wait_ge(sem("swa_pTc"), before + (j + 1))
                if j == 0:
                    pe.wait_ge(sem("swa_vtc"), t + 1)
                bank = (4, 7)[a]
                for c in range(n // 128):
                    last = mm(ps[bank][:, b * 128:(b + 1) * 128], SC[:, 5, c * 128:(c + 1) * 128],
                              SC[:, 14 + j, c * 128:(c + 1) * 128],
                              start=(c == 0 and j % nb == 0), stop=True)
                if j % nb == nb - 1:
                    last.then_inc(sem("swa_o"), 1)

            channel_sum(0, 0)
            ada_rows(0, *ADA_GATE)
            for l in range(DEPTH):
                lo = 0 if l == 0 else CTX
                pe.wait_ge(sem("norm_ready"), l + 1)
                Fill(l, "gdn", 4, 0, lo).rest()
                with pe.Fori(0, 2) as i:
                    Fill(l, "gdn", 4, i, 0, off=4).rest()
                wt, n = segs[(l, "small")]
                pe.wait_ge(sem("small_split"), l + 1)
                bank_wait(pe, n, 0, 2, 0)
                for k in range(KT):
                    x = pair(N[:, k, :])
                    last = pairs(ps[n % 2][0:NLR, :], wlr16[:, 0, k, :], wlr16[:, 1, k, :], x[:, 0, :], x[:, 1, :],
                                 k == 0, k == KT - 1)
                last.then_inc(sem(f"bank{n % 2}_full"), 1)
                bank_wait(pe, n, 0, 2, 1)
                for b in range(NC):
                    for k in range(KT):
                        x = pair(N[:, k, :])[:, :, b * 128:(b + 1) * 128]
                        last = pairs(ps[1][:, b * NAB:(b + 1) * NAB], x[:, 0, :], x[:, 1, :],
                                     wab16[:, 0, k, :], wab16[:, 1, k, :], k == 0, k == KT - 1)
                last.then_inc(sem("bank1_full"), 1)
                gate_tiles = Fill(l, "gdng", 4, 0, lo)
                gate_tiles(2 * KT)
                pe.wait_ge(sem("gdn_g"), l + 1)
                for d in range(2):
                    for kind, lhs in enumerate((cm(CUM[d]), cm(TAIL[d]), ones)):
                        last = mm(ps[3][:, (3 * d + kind) * 16:(3 * d + kind + 1) * 16], lhs, g[:, 0:4, d, :])
                last.then_inc(sem("gdn_cums"), 1)
                gate_tiles.rest()
                for rounds, first in GDN_LOOPS[l]:
                    with pe.Fori(0, rounds) as i:
                        gdn(i + first, i + (4 * l + first), l,
                            Fill(l, "p2", 4, i, lo if first else 0, off=4 * first))
                with pe.Fori(0, 2) as i:
                    gla(i, i + 2 * l, l, Fill(l, "p3", 4, i, 0))
                blocks = list(range(4)) if l == 0 else [2, 3]
                with pe.Fori(0, 2) as i:
                    swa(i, i + 2 * l, l, Fill(l, "p4", 6, i, lo), blocks)
                Fill(l, "p4", 4, 0, lo, off=12).rest()
                pe.wait_ge(sem("bank1_full"), segs[(l, "out")][1] // 2)
                pe.sem_inc(sem("norm_used"), 1)
                mixed = lambda k: pair(act[:, Y_ORDER[K_ORDER[k]], :])[:, :, lo:]
                pe.wait_ge(sem("swa_y"), 2 * l + 2)
                first, second = (Fill(l, "out", 4, 0, lo, mixed, off=j, korder=K_ORDER) for j in range(2))
                first(KT - 4)
                second(KT - 4)
                pe.wait_ge(sem("sc_y"), 4 * l + 4)
                first(4)
                second(4)
                for j in (2, 3):
                    Fill(l, "out", 4, 0, lo, mixed, off=j, korder=K_ORDER)(KT)
                with pe.Fori(0, 3) as i:
                    Fill(l, "out", 4, i, lo, mixed, off=4, korder=K_ORDER).rest()
                pe.wait_ge(sem("bank1_full"), (segs[(l, "out")][1] + 16) // 2)
                pe.sem_inc(sem("layer_multiplied"), 1)
                channel_sum(2 * l + 1, lo)
                if l == 0:
                    pe.wait_ge(sem("cs_ready"), 2)
                    ada_rows(1, *ADA_NORM)
                    channel_sum(2, 0)
                    ada_rows(1, *ADA_GATE)
            wt, n = segs["end"]
            for q in range(4):
                pe.wait_ge(sem("h_add"), KT * (DEPTH - 1) + 4 * q + 4)
                for b in range(2):
                    j = 2 * q + b
                    bank_wait(pe, n, 0, 8, j)
                    for c in range(4):
                        last = tp(ps[(n + j) % 2][:, c * 128:(c + 1) * 128],
                                  N[:, 4 * q + c, CTX + b * 128:CTX + (b + 1) * 128])
                    last.then_inc(sem(f"bank{(n + j) % 2}_full"), 1)

        @block.scalar
        def _(sc_eng):
            A = sc_eng
            oa = Order(A, sem("act_order"))

            def act_(out, in_, f, **kw):
                return nc.scalar.activation(out, in_, f, **kw)

            def evac(l, name, tb, i, tt, dst, off=0):
                n = segs[(l, name)][1] + off
                b = (n + tt) % 2
                out_wait(A, n, i, tb, tt)
                act_(dst, ps[b][:, 0:dst.shape[-1]], ACT.Copy, scale=1.0 / WSCALE)\
                    .then_inc(sem(f"bank{b}_free"), 1)

            def ada_evac(l, rounds, first):
                n = segs[(0, f"ada{l}")][1] + 2 * first
                with A.Fori(0, rounds) as i:
                    out_wait(A, n, i, 2, 0)
                    act_(SC[:, 6, :], ps[0][:, :], ACT.Copy).then_inc(sem("bank0_free"), 1)
                    out_wait(A, n, i, 2, 1)
                    act_(ada[:, l, bass.ds(i * 4 + 4 * first, 4), :], ps[1][:, 0:8].rearrange("p (k s) -> p k s", s=2), ACT.Copy)\
                        .then_inc(sem("bank1_free"), 1)
                A.wait_ge(sem("bank1_free"), n // 2 + rounds)
                A.sem_inc(sem("ada_out"), 1)

            def link(ins):
                oa.done(ins)
                oa.wait()

            def sigmoid(a):
                link(act_(a, a, ACT.Exp, scale=-1.0))
                link(act_(a, a, ACT.Ln, bias=one1))
                return act_(a, a, ACT.Exp, scale=-1.0)

            nc.scalar.preload_act_table_set("natural_log_exp_and_others")

            A.wait_ge(sem("con_in"), 16)
            A.wait_ge(sem("par_in"), 16)
            act_(cst[:, :, :], par[:, P_C:P_C + 2 * KT].rearrange("p (k s) -> p k s", s=2), ACT.Exp, scale=-1.0)\
                .then_inc(sem("c_exp"), 1)
            for k in range(KT):
                out_wait(A, 0, 0, KT, k)
                act_(N[:, k, :], ps[k % 2][:, :], ACT.Copy).then_inc(sem(f"bank{k % 2}_free"), 1)
            ada_evac(0, *ADA_NORM)

            def rstd(t, bank, n, lo):
                A.wait_ge(sem("chansum_done"), t + 1)
                link(act_(SC[:, 2, lo:], ps[bank][:, lo:], ACT.Ln, scale=1.0 / n, bias=eps))
                act_(SC[:, 3, lo:], SC[:, 2, lo:], ACT.Exp, scale=-0.5).then_inc(sem("rstd_ready"), 1)

            def gdn(i, t, l, lo, take):
                A.wait_ge(sem("gdn_D"), t + 1)
                for d in range(2):
                    last = act_(SC[:, 20 + d, :], ps[5 + d][:, :], ACT.Exp)
                last.then_inc(sem("gdn_E"), 1)
                A.wait_ge(sem("gdn_tok"), t + 1)
                for j in range(3):
                    last = act_(SC[:, 3 + j, :], ps[2 + j][:, :], ACT.Copy)
                last.then_inc(sem("gdn_tokc"), 1)
                for a in range(2):
                    for c in range(NC):
                        s = slice(c * 128, (c + 1) * 128)
                        last = act_(SC[:, 8 + a, s], ps[2 + a][:, s], ACT.Square, accum_out=rn[:, a, c:c + 1])
                link(last)
                link(act_(rn[:, :, :], rn[:, :, :], ACT.Ln, bias=eps))
                act_(rn[:, :, :], rn[:, :, :], ACT.Exp, scale=-0.5).then_inc(sem("gdn_rn"), 1)
                for j, (b, dst) in enumerate(((5, 14), (2, 16), (3, 17), (6, 15))):
                    A.wait_ge(sem("gdn_T1"), 4 * t + j + 1)
                    act_(SC[:, dst, :], ps[b][:, :], ACT.Copy).then_inc(sem("gdn_T1c"), 1)
                take(0)
                for d, b in ((0, 6), (1, 2)):
                    A.wait_ge(sem("gdn_T2"), 2 * t + d + 1)
                    act_(SC[:, 18 + d, :], ps[b][:, :], ACT.Copy).then_inc(sem("gdn_T2c"), 1)
                A.wait_ge(sem("gdn_gc"), t + 1)
                sigmoid(SC[:, 2, lo:]).then_inc(sem("gdn_gs"), 1)
                A.wait_ge(sem("gdn_P"), 14 * t + 2 + 6)
                take(1)
                for s in range(NC):
                    A.wait_ge(sem("gdn_vn"), 4 * t + s + 1)
                    if s:
                        A.wait_ge(sem("gdn_dS"), 3 * t + s)
                    act_(vn[:, :, :], ps[3][:, 0:256].rearrange("p (d v) -> p d v", d=2), ACT.Copy,
                         scale=1.0 if s == 0 else -1.0).then_inc(sem("gdn_vnc"), 1)
                    if s == 2:
                        take(2)
                A.wait_ge(sem("gdn_o"), t + 1)
                act_(SC[:, 0, lo:], ps[5][:, lo:], ACT.Copy)
                act_(SC[:, 1, :], ps[5][:, :], ACT.Square).then_inc(sem("gdn_osq"), 1)
                A.wait_ge(sem("gdn_oss"), t + 1)
                link(act_(SC[:, 3, lo:], ps[6][:, lo:], ACT.Ln, scale=1.0 / HD, bias=eps))
                act_(SC[:, 3, lo:], SC[:, 3, lo:], ACT.Exp, scale=-0.5).then_inc(sem("gdn_orn"), 1)
                take(3)

            def gla(i, t, l, lo, take):
                A.wait_ge(sem("gla_z"), t + 1)
                for d in range(2):
                    last = act_(SC[:, d, :], ps[2 + d][:, :], ACT.Identity,
                                bias=par[:, bass.ds(i + (l * PL + P_GLAB + 2 * d), 1)])
                last.then_inc(sem("gla_zc"), 1)
                A.wait_ge(sem("gla_vt"), t + 1)
                for a in range(2):
                    last = act_(SC[:, 18 + a, :], ps[4 + a][:, :], ACT.Copy)
                last.then_inc(sem("gla_vtc"), 1)
                A.wait_ge(sem("gla_abs"), t + 1)
                link(act_(SC[:, 2:4, :], SC[:, 2:4, :], ACT.Exp, scale=-1.0))
                act_(SC[:, 2:4, :], SC[:, 2:4, :], ACT.Ln, bias=one1).then_inc(sem("gla_l"), 1)
                A.wait_ge(sem("gla_cen"), t + 1)
                act_(SC[:, 8:10, :], SC[:, 2:4, :], ACT.Exp, scale=-1.0 / 16).then_inc(sem("gla_ek"), 1)
                act_(SC[:, 6:8, :], SC[:, 2:4, :], ACT.Exp, scale=1.0 / 16).then_inc(sem("gla_eq"), 1)
                for d in range(2):
                    mid, last_ = (CH // 2 - 1, CH - 1) if d == 0 else (CH // 2, 0)
                    act_(gs[:, 0, d, :], SC[:, 4 + d, mid::CH], ACT.Exp, scale=1.0 / 16)
                    act_(gs[:, 1, d, :], SC[:, 4 + d, last_::CH], ACT.Exp, scale=1.0 / 16)
                act_(gs[:, 2, :, :], gd[:, :, :], ACT.Exp, scale=1.0 / 16).then_inc(sem("gla_gs"), 1)
                A.wait_ge(sem("gla_gc"), t + 1)
                sigmoid(SC[:, 16:18, lo:]).then_inc(sem("gla_gsig"), 1)
                take(0)
                take(1)
                A.wait_ge(sem("gla_kt"), t + 1)
                for d in range(2):
                    last = act_(SC[:, 14 + d, :], ps[2 + d][:, :], ACT.Copy)
                last.then_inc(sem("gla_ktc"), 1)
                take(2)
                A.wait_ge(sem("gla_AT"), t + 1)
                for a in range(2):
                    A.wait_ge(sem("gla_o"), 2 * t + a + 1)
                    act_(SC[:, 6 + a, lo:], ps[6 + a][:, lo:], ACT.Copy)
                    act_(SC[:, 4 + a, :], ps[6 + a][:, :], ACT.Square).then_inc(sem("gla_osq"), 1)
                for a in range(2):
                    A.wait_ge(sem("gla_oss"), 2 * t + a + 1)
                    link(act_(SC[:, 8 + a, lo:], ps[2 + a][:, lo:], ACT.Ln, scale=1.0 / HD, bias=eps))
                    act_(SC[:, 8 + a, lo:], SC[:, 8 + a, lo:], ACT.Exp, scale=-0.5).then_inc(sem("gla_orn"), 1)
                take(3)
                A.wait_ge(sem("gla_y"), t + 1)

            def swa(i, t, l, lo, take, blocks):
                nb = len(blocks)
                before = i * 2 * nb + swa_blocks(l)
                A.wait_ge(sem("swa_vt"), t + 1)
                act_(SC[:, 5, :], ps[4][:, :], ACT.Copy).then_inc(sem("swa_vtc"), 1)
                A.wait_ge(sem("swa_gc"), t + 1)
                sigmoid(SC[:, 22:24, lo:]).then_inc(sem("swa_gs"), 1)
                take(0)
                A.wait_ge(sem("swa_m"), t + 1)
                for j in range(2 * nb):
                    n = TOK if blocks[j % nb] >= 2 else CTX
                    act_(SC[:, 6 + j, 0:n], SC[:, 6 + j, 0:n], ACT.Exp, scale=HD ** -0.5,
                         bias=sm[:, 1, j:j + 1], accum_out=sm[:, 2, j:j + 1])
                for a in range(2):
                    last = act_(sm[:, 3, a * nb:(a + 1) * nb], sm[:, 1, a * nb:(a + 1) * nb], ACT.Exp,
                                bias=par[:, bass.ds(i * 2 + (l * PL + P_SINK + a), 1)])
                last.then_inc(sem("swa_e"), 1)
                take(1)
                take(2)
                for j in range(2 * nb):
                    n = TOK if blocks[j % nb] >= 2 else CTX
                    A.wait_ge(sem("swa_pT"), before + (j + 1))
                    act_(SC[:, 14 + j, 0:n], ps[2 + j % 2][:, 0:n], ACT.Copy).then_inc(sem("swa_pTc"), 1)
                for tt in range(3, 6):
                    take(tt)
                A.wait_ge(sem("swa_y"), t + 1)

            def take_(l, name, tb, i, dst, off=0):
                return lambda tt: evac(l, name, tb, i, tt, dst(tt), off)

            rstd(0, 2, D, 0)
            ada_evac(0, *ADA_GATE)
            for l in range(DEPTH):
                lo = 0 if l == 0 else CTX
                if l:
                    A.wait_ge(sem("yo_used"), l)
                oa.straight()
                for tt in range(4):
                    evac(l, "gdn", 4, 0, tt, act[:, tt, lo:])
                    A.wait_ge(sem("conv_done"), 12 * l + tt + 1)
                    sigmoid(SC[:, 10 + tt % 2, lo:]).then_inc(sem("conv_gs"), 1)
                oa.straight()
                with A.Fori(0, 2) as i:
                    oa.round(i, CONV_ACT)
                    for tt in range(4):
                        evac(l, "gdn", 4, i, tt, act[:, i * 4 + (4 + tt), :], off=4)
                        t = i * 4 + (12 * l + 4 + tt + 1)
                        A.wait_ge(sem("conv_done"), t)
                        sigmoid(SC[:, 10 + tt % 2, :]).then_inc(sem("conv_gs"), 1)
                oa.close(2)
                wt, n = segs[(l, "small")]
                assert n % 2 == 0
                out_wait(A, n, 0, 2, 0)
                act_(lrT, ps[0][0:NLR, :], ACT.Copy, scale=1.0 / WSCALE).then_inc(sem("bank0_free"), 1)
                A.wait_ge(sem("bank0_free"), n // 2 + 1)
                A.sem_inc(sem("lr_copied"), 1)
                out_wait(A, n, 0, 2, 1)
                act_(ab, ps[1][:, 0:NC * NAB].rearrange("p (c k) -> p c k", k=NAB), ACT.Copy, scale=1.0 / WSCALE)\
                    .then_inc(sem("bank1_free"), 1)
                A.wait_ge(sem("bank1_free"), n // 2 + 1)
                A.sem_inc(sem("ab_copied"), 1)
                if l:
                    A.wait_ge(sem("gdn_g"), l)
                act_(expA[:, :, :], P(l, P_ALOG, 8).rearrange("p (d h) -> p d h", d=2), ACT.Exp)\
                    .then_inc(sem("expA"), 1)
                A.wait_ge(sem("gate_abs"), l + 1)
                link(act_(gt[:, :, :, :], gt[:, :, :, :], ACT.Exp, scale=-1.0))
                act_(gt[:, :, :, :], gt[:, :, :, :], ACT.Ln, bias=one1).then_inc(sem("gate_l"), 1)
                A.wait_ge(sem("gate_bc"), l + 1)
                sigmoid(beta[:, :, :, :]).then_inc(sem("beta_ready"), 1)
                for tt in range(4):
                    evac(l, "gdng", 4, 0, tt, act[:, Y_GDN + tt, lo:])
                A.wait_ge(sem("gdn_cums"), l + 1)
                act_(eg[:, :, :, :, :].rearrange("p a b c d -> p (a b c d)"), ps[3][:, 0:96], ACT.Exp)\
                    .then_inc(sem("gdn_eg"), 1)
                oa.straight()
                for rounds, first in GDN_LOOPS[l]:
                    with A.Fori(0, rounds) as i:
                        oa.round(i, GDN_ACT)
                        pl = lo if first else 0
                        gdn(i + first, i + (4 * l + first), l, lo, take_(
                            l, "p2", 4, i, lambda tt: act[:, i * 4 + (T_B + 4 * first + tt), pl:], 4 * first))
                    oa.close(rounds)
                A.wait_ge(sem("gdn_y"), 4 * l + 5)
                with A.Fori(0, 2) as i:
                    oa.round(i, GLA_ACT)
                    gla(i, i + 2 * l, l, lo, take_(l, "p3", 4, i, lambda tt: act[:, i * 4 + (T_A + tt), :]))
                oa.close(2)
                blocks = list(range(4)) if l == 0 else [2, 3]
                with A.Fori(0, 2) as i:
                    oa.round(i, SWA_ACT)
                    swa(i, i + 2 * l, l, lo, take_(l, "p4", 6, i, lambda tt: act[:, i * 6 + (8 + tt), lo:]), blocks)
                oa.close(2)
                for j in range(4):
                    evac(l, "p4", 4, 0, j, act[:, Y_SC + j, lo:], off=12)
                    A.wait_ge(sem("sc_gc"), 4 * l + j + 1)
                    sigmoid(SC[:, 8 + j, lo:]).then_inc(sem("sc_gs"), 1)
                oa.straight()
                A.wait_ge(sem("sc_y"), 4 * l + 4)
                n = segs[(l, "out")][1]
                with A.Fori(0, 4) as i:
                    for tt in range(4):
                        b = (n + tt) % 2
                        out_wait(A, n, i, 4, tt)
                        act_(act[:, i * 4 + tt, lo:], ps[b][:, 0:TOK - lo], ACT.Copy, scale=1.0 / WSCALE)
                        if tt >= 2:
                            A.wait_ge(sem("yo_add"), i * 4 + (16 * l + tt - 1))
                        else:
                            A.wait_ge(sem("yo_round"), i + (4 * l + 1))
                        act_(SC[:, 4 + tt % 2, lo:], ps[b][:, 0:TOK - lo], ACT.Square, scale=1.0 / WSCALE)\
                            .then_inc(sem(f"bank{b}_free"), 1)
                rstd(2 * l + 1, 2, D, lo)
                if l == 0:
                    ada_evac(1, *ADA_NORM)
                    A.wait_ge(sem("rstd_used"), 1)
                    rstd(2, 2, D, 0)
                    ada_evac(1, *ADA_GATE)
            wt, n = segs["end"]
            for j in range(8):
                out_wait(A, n, 0, 8, j)
                act_(SC[:, 8 + j, :], ps[(n + j) % 2][:, :], ACT.Copy).then_inc(sem(f"bank{(n + j) % 2}_free"), 1)
                A.wait_ge(sem(f"bank{(n + j) % 2}_free"), (n + j) // 2 + 1)
                A.sem_inc(sem("out_staged"), 1)

        @block.vector
        def _(dve):
            V = nc.vector
            o = Order(dve, sem("dve_order"))

            def link(ins):
                o.done(ins)
                o.wait()

            dve.wait_ge(sem("con_in"), 16)
            dve.wait_ge(sem("par_in"), 16)
            dve.wait_ge(sem("c_exp"), 1)
            link(V.tensor_scalar(cst[:, :, :], cst[:, :, :], 1.0, None, ALU.add))
            link(V.reciprocal(cst[:, :, :], cst[:, :, :]))
            link(V.tensor_tensor(cs[:, :, :], cst[:, :, :], par[:, P_C:P_C + 2 * KT].rearrange(
                "p (k s) -> p k s", s=2), ALU.mult))

            def pad_cs():
                link(V.memset(csp, 0.0))
                V.tensor_copy(csp[:, :, 0:2], cs[:, :, :]).then_inc(sem("cs_ready"), 1)

            for s in range(2):
                dve.sem_inc(sem(f"stage{s}_split"), 1)
            pad_cs()

            def split_tile(s, full):
                dve.wait_ge(sem(f"stage{s}_full"), full)
                h = halves(s)
                link(V.tensor_scalar(h[:, :, 0, :], ring[:, s, :, :], WSCALE, None, ALU.mult))
                V.scalar_tensor_tensor(h[:, :, 1, :], ring[:, s, :, :], WSCALE, h[:, :, 0, :],
                                       ALU.mult, ALU.subtract).then_inc(sem(f"stage{s}_split"), 1)

            def splitter(l, name, tb, i, off=0):
                wt, n = segs[(l, name)]

                def split(j):
                    out_wait(dve, n + off, i, tb, j)
                    split_tile(j % 2, i * (8 * tb) + 16 * ((wt + off + j + 2) // 2 + 1))
                return split

            def split_y(dst, src, lo):
                d = pair(dst)
                link(V.tensor_copy(d[:, 0, lo:], src))
                return V.tensor_tensor(d[:, 1, lo:], src, d[:, 0, lo:], ALU.subtract)

            def modulation(l):
                dve.wait_ge(sem("ada_out"), 2 * l + 1)
                link(V.tensor_tensor(ada[:, l, 0:32, :], ada[:, l, 0:32, :], along(P(l, P_ADAB, 32), 2), ALU.add))
                link(V.scalar_tensor_tensor(modA[:, l, :, :], ada[:, l, 16:32, :], 1.0, along(P(l, P_NPRE, 16), 2),
                                            ALU.add, ALU.mult))

            def gate_modulation(l):
                dve.wait_ge(sem("ada_out"), 2 * l + 2)
                link(V.tensor_tensor(ada[:, l, 32:48, :], ada[:, l, 32:48, :], along(P(l, P_ADAB + 32, 16), 2),
                                     ALU.add))
                link(V.tensor_tensor(modG[:, l, :, :], ada[:, l, 32:48, :], along(P(l, P_NPOST, 16), 2), ALU.mult))

            def prenorm(l, t):
                dve.wait_ge(sem("rstd_ready"), t + 1)
                dve.wait_ge(sem("h_saved"), 16 * (l + 1))
                at = {}
                for k in range(KT + 3):
                    if k < KT:
                        if k >= 4:
                            o.wait(at[k - 4, 3])
                        at[k, 0] = o.done(V.tensor_tensor(SC[:, 8 + k % 4, :], N[:, k, :], SC[:, 3, :], ALU.mult))
                    q = k - 1
                    if 0 <= q < KT:
                        o.wait(at[q, 0])
                        for hf in range(2):
                            s = slice(hf * 256, hf * 256 + 256)
                            last = V.tensor_scalar(SC[:, 8 + q % 4, s], SC[:, 8 + q % 4, s],
                                                   modA[:, l, q, hf:hf + 1], ada[:, l, q, hf:hf + 1],
                                                   ALU.mult, ALU.add)
                        at[q, 1] = o.done(last)
                    q = k - 2
                    if 0 <= q < KT:
                        o.wait(at[q, 1])
                        at[q, 2] = o.done(V.tensor_copy(pair(N[:, q, :])[:, 0, :], SC[:, 8 + q % 4, :]))
                    q = k - 3
                    if 0 <= q < KT:
                        o.wait(at[q, 2])
                        at[q, 3] = o.done(V.tensor_tensor(pair(N[:, q, :])[:, 1, :], SC[:, 8 + q % 4, :],
                                                          pair(N[:, q, :])[:, 0, :], ALU.subtract))
                o.wait()
                dve.sem_inc(sem("norm_ready"), 1)

            def two(a):
                return a.rearrange("p (s t) -> p s t", s=2)

            def conv_tap(dst, src, wcol, sh):
                d, s = two(dst), two(src)
                a, b = max(0, -sh), SEQ - max(0, sh)
                return V.scalar_tensor_tensor(d[:, :, a:b], s[:, :, a + sh:b + sh], wcol, d[:, :, a:b],
                                              ALU.mult, ALU.add)

            def gates(l):
                dve.wait_ge(sem("ab_copied"), l + 1)
                z = o.done(V.tensor_tensor(gz[:, :, :, :].rearrange("p c d h -> p c (d h)"), ab[:, :, 0:8],
                                           over(P(l, P_DT, 8)), ALU.add))
                V.tensor_copy(beta[:, :, :, :].rearrange("p h d c -> p c d h"),
                              ab[:, :, 8:16].rearrange("p c (d h) -> p c d h", d=2)).then_inc(sem("gate_bc"), 1)
                o.wait(z)
                V.scalar_tensor_tensor(gt[:, :, :, :], gz[:, :, :, :], -1.0, gz[:, :, :, :], ALU.mult, ALU.max)\
                    .then_inc(sem("gate_abs"), 1)
                dve.wait_ge(sem("gate_l"), l + 1)
                link(V.scalar_tensor_tensor(gz[:, :, :, :], gz[:, :, :, :], 0.0, gt[:, :, :, :], ALU.max, ALU.add))
                dve.wait_ge(sem("expA"), l + 1)
                for d in range(2):
                    last = V.scalar_tensor_tensor(g[:, 0:4, d, :].rearrange("p h c -> p c h"), gz[:, :, d, :], -1.0,
                                                  over(expA[:, d, :]), ALU.mult, ALU.mult)
                last.then_inc(sem("gdn_g"), 1)

            def conv_tile(j, tile, l, l0, t, wcol):
                s0, acc, sg = l0 // SEQ, SC[:, 8 + j % 2, :], SC[:, 10 + j % 2, :]

                def tap(tp, sh):
                    d, s = two(acc)[:, s0:, :], two(tile)[:, s0:, :]
                    a, b = max(0, -sh), SEQ - max(0, sh)
                    return V.scalar_tensor_tensor(d[:, :, a:b], s[:, :, a + sh:b + sh], wcol(tp), d[:, :, a:b],
                                                  ALU.mult, ALU.add)
                link(V.tensor_scalar(acc[:, l0:], tile[:, l0:], wcol(2), None, ALU.mult))
                for tp in (0, 1, 3, 4):
                    link(tap(tp, tp - 2))
                V.tensor_scalar(sg[:, l0:], acc[:, l0:], CLAMP, None, ALU.max).then_inc(sem("conv_done"), 1)

            def conv_end(j, tile, l0, t):
                dve.wait_ge(sem("conv_gs"), t)
                return V.tensor_tensor(tile[:, l0:], SC[:, 8 + j % 2, l0:], SC[:, 10 + j % 2, l0:], ALU.mult)

            def gdn_projection(l, lo):
                n = segs[(l, "gdn")][1]
                for rounds, first in ((1, 0), (2, 4)):
                    l0 = lo if first == 0 else 0
                    if first:
                        dve.wait_ge(sem("small_in"), 32 * (l + 1))
                        for w16, w in ((wlr16, wlr), (wab16, wab)):
                            link(V.tensor_scalar(w16[:, 0], w, WSCALE, None, ALU.mult))
                            last = V.scalar_tensor_tensor(w16[:, 1], w, WSCALE, w16[:, 0], ALU.mult, ALU.subtract)
                        last.then_inc(sem("small_split"), 1)
                        o.straight()
                    with dve.Fori(0, rounds) as i:
                        o.round(i, CONV_DVE)
                        split = splitter(l, "gdn", 4, i, first)
                        for j in range(4):
                            tile = act[:, i * 4 + (T_A + first + j), :]
                            t = i * 4 + (12 * l + first + j + 1)
                            split(j)
                            dve.wait_ge(sem(f"bank{(n + j) % 2}_free"), i * 2 + ((n + first + j) // 2 + 1))
                            conv_tile(j, tile, l, l0, t, lambda tp: par[
                                :, bass.ds(i * 20 + (l * PL + P_CONV + 5 * (first + j) + tp), 1)])
                            link(conv_end(j, tile, l0, t))
                    o.close(rounds)
                gates(l)
                split = splitter(l, "gdng", 4, 0)
                for j in range(3):
                    split(j)

            def gdn(i, t, l, lo, split):
                qkv = act[:, T_A:T_A + 12, :].rearrange("p (j h) t -> p j h t", j=3)
                V.tensor_copy(SC[:, 0:3, :], qkv[:, :, i, :]).then_inc(sem("gdn_x"), 1)
                split(-1)
                dve.wait_ge(sem("gdn_tokc"), t + 1)
                dve.wait_ge(sem("gdn_ks"), t + 1)
                V.tensor_tensor(chunks(SC[:, 7, :]), chunks(SC[:, 4, :]), along(rn[:, 1, :]), ALU.mult)
                for d in range(2):
                    V.tensor_tensor(chunks(SC[:, 8 + d, :]), chunks(SC[:, 4, :]), along(ks[:, 0, d, :]), ALU.mult)
                V.tensor_tensor(chunks(SC[:, 6, :]), chunks(SC[:, 3, :]), along(rq[:, :]), ALU.mult)\
                    .then_inc(sem("gdn_kn"), 1)
                V.tensor_scalar(SC[:, 2, lo:], act[:, i + Y_GDN, lo:], CLAMP, None, ALU.max)\
                    .then_inc(sem("gdn_gc"), 1)
                split(0)
                dve.wait_ge(sem("gdn_Em"), t + 1)
                dve.wait_ge(sem("gdn_G"), 3 * t + 1)
                for d in range(2):
                    last = V.tensor_tensor(SC[:, 20 + d, :], ps[5][:, :], SC[:, 20 + d, :], ALU.mult)
                last.then_inc(sem("gdn_AT"), 1)
                for d, bank in ((0, 4), (1, 7)):
                    dve.wait_ge(sem("gdn_G"), 3 * t + 2 + d)
                    V.tensor_tensor(SC[:, 22 + d, :], ps[bank][:, :], SC[:, 22 + d, :], ALU.mult)\
                        .then_inc(sem("gdn_U"), 1)
                MK = (C_LO, C_UP)
                for d, bank in ((0, 3), (1, 4)):
                    dve.wait_ge(sem("gdn_P"), 14 * t + d + 1)
                    o.done(V.tensor_tensor(chunks(SC[:, 16 + d, :]), chunks(ps[bank][:, :]), over(cm(MK[d])),
                                           ALU.mult))
                    o.wait()
                    V.tensor_tensor(chunks(SC[:, 6 + d, :]), over(ident), chunks(SC[:, 16 + d, :]), ALU.subtract)\
                        .then_inc(sem("gdn_T"), 1)
                for lv in range(1, 7):
                    for d in range(2):
                        dve.wait_ge(sem("gdn_P"), 14 * t + 2 * lv + d + 1)
                        V.tensor_tensor(chunks(SC[:, 16 + d, :]), chunks(ps[2 + d][:, :]),
                                        over(cm(MK[d] + 128 * lv)), ALU.mult).then_inc(sem("gdn_Pm"), 1)
                    for d in range(2):
                        if lv < 6:
                            dve.wait_ge(sem("gdn_Y"), 10 * t + 2 * (lv - 1) + d + 1)
                            dve.wait_ge(sem("gdn_T"), 12 * t + 2 * (lv - 1) + d + 1)
                            V.tensor_tensor(SC[:, 6 + d, :], SC[:, 6 + d, :], ps[4 + d][:, :], ALU.subtract)\
                                .then_inc(sem("gdn_T"), 1)
                        dve.wait_ge(sem("gdn_YT"), 12 * t + 2 * (lv - 1) + d + 1)
                        if lv == 1:
                            dve.wait_ge(sem("gdn_M0"), 2 * t + d + 1)
                        else:
                            dve.wait_ge(sem("gdn_M"), 10 * t + 2 * (lv - 2) + d + 1)
                        last = V.tensor_tensor(SC[:, 8 + d, :], SC[:, 8 + d, :], ps[6 + d][:, :], ALU.subtract)
                        if lv < 6:
                            last.then_inc(sem("gdn_M"), 1)
                    if lv == 5:
                        split(1)
                last.then_inc(sem("gdn_Mlast"), 1)
                for s in range(NC):
                    cc = (s, (1, 0, 3, 2)[s])
                    if s:
                        dve.wait_ge(sem("gdn_KS"), 3 * t + s)
                        for d in range(2):
                            last = V.scalar_tensor_tensor(rr[:, d, :], ps[2][:, d * 128:d * 128 + 128],
                                                          ks[:, 3, d, cc[d]:cc[d] + 1],
                                                          SC[:, 12 + d, cc[d] * 128:cc[d] * 128 + 128],
                                                          ALU.mult, ALU.subtract)
                        last.then_inc(sem("gdn_r"), 1)
                    if s < NC - 1:
                        dve.wait_ge(sem("gdn_dS"), 3 * t + s + 1)
                        if s == 0:
                            V.tensor_copy(st[:, :, :], ps[4][:, 0:256].rearrange("p (d v) -> p d v", d=2))\
                                .then_inc(sem("gdn_S"), 1)
                        else:
                            dve.wait_ge(sem("gdn_S"), 3 * t + s)
                            for d in range(2):
                                last = V.scalar_tensor_tensor(st[:, d, :], st[:, d, :],
                                                              tot[:, d, cc[d]:cc[d] + 1],
                                                              ps[4][:, d * 128:d * 128 + 128], ALU.mult, ALU.add)
                            last.then_inc(sem("gdn_S"), 1)
                split(2)
                dve.wait_ge(sem("gdn_orn"), t + 1)
                link(V.scalar_tensor_tensor(SC[:, 0, lo:], SC[:, 0, lo:], P(l, P_GDNN), SC[:, 3, lo:],
                                            ALU.mult, ALU.mult))
                dve.wait_ge(sem("gdn_silu"), t + 1)
                link(V.tensor_tensor(SC[:, 1, lo:], SC[:, 0, lo:], SC[:, 2, lo:], ALU.mult))
                split_y(act[:, i + Y_GDN, :], SC[:, 1, lo:], lo).then_inc(sem("gdn_y"), 1)
                dve.wait_ge(sem("gdn_y"), t + 2)

            def gla(i, t, l, lo, split):
                dve.wait_ge(sem("gla_zc"), t + 1)
                V.scalar_tensor_tensor(SC[:, 2:4, :], SC[:, 0:2, :], -1.0, SC[:, 0:2, :], ALU.mult, ALU.max)\
                    .then_inc(sem("gla_abs"), 1)
                split(-1)
                dve.wait_ge(sem("gla_l"), t + 1)
                link(V.scalar_tensor_tensor(SC[:, 0:2, :], SC[:, 0:2, :], 0.0, SC[:, 2:4, :], ALU.min, ALU.subtract))
                V.tensor_tensor_scan(SC[:, 4, :], con[:, C_SEG:C_SEG + TOK], SC[:, 0, :], 0.0, ALU.mult, ALU.add)
                link(V.tensor_tensor_scan(SC[:, 5, ::-1], con[:, C_SEG:C_SEG + TOK], SC[:, 1, ::-1], 0.0,
                                          ALU.mult, ALU.add))
                for d in range(2):
                    mid, last_ = (CH // 2 - 1, CH - 1) if d == 0 else (CH // 2, 0)
                    V.tensor_tensor(gd[:, d, :], SC[:, 4 + d, last_::CH], SC[:, 4 + d, mid::CH], ALU.subtract)
                    last = V.tensor_tensor(chunks(SC[:, 2 + d, :]), chunks(SC[:, 4 + d, :]),
                                           along(SC[:, 4 + d, mid::CH]), ALU.subtract)
                link(last)
                V.tensor_scalar(SC[:, 2:4, :], SC[:, 2:4, :], 640.0, -640.0, ALU.min, ALU.max)\
                    .then_inc(sem("gla_cen"), 1)
                dve.wait_ge(sem("gla_vtc"), t + 1)
                V.tensor_scalar(SC[:, 16:18, lo:], act[:, bass.ds(i * 2 + Y_GLA, 2), lo:], CLAMP, None, ALU.max)\
                    .then_inc(sem("gla_gc"), 1)
                split(0)
                dve.wait_ge(sem("gla_eq"), t + 1)
                for d in range(2):
                    last = V.scalar_tensor_tensor(SC[:, 10 + d, :], act[:, i + T_B, :], 64 ** -0.5, SC[:, 6 + d, :],
                                                  ALU.mult, ALU.mult)
                last.then_inc(sem("gla_qd"), 1)
                split(1)
                for a in range(2):
                    for d in range(2):
                        bank = (6, 7, 2, 3)[2 * a + d]
                        dve.wait_ge(sem("gla_att"), 4 * t + 2 * a + d + 1)
                        last = V.tensor_tensor(chunks(SC[:, 20 + 2 * a + d, :]), chunks(ps[bank][:, :]),
                                               over(cm(CUM[d])), ALU.mult)
                last.then_inc(sem("gla_AT"), 1)
                dve.wait_ge(sem("gla_dS"), t + 1)
                dve.wait_ge(sem("gla_gs"), t + 1)
                dve.wait_ge(sem("gla_kd"), t + 1)
                for d in range(2):
                    last = V.tensor_tensor(chunks(SC[:, 2 + d, :]), chunks(ps[4 + d][:, :]),
                                           along(gs[:, 2, d, :]), ALU.mult)
                link(last)
                for s in range(1, NC):
                    for d in range(2):
                        prev = (s - 1, (1, 0, 3, 2)[s - 1])[d]
                        own = SC[:, 2 + d, prev * 128:prev * 128 + 128]
                        to = SC[:, 8 + d, (s - 1) * 128:s * 128]
                        if s == 1:
                            last = V.tensor_copy(to, own)
                        else:
                            last = V.scalar_tensor_tensor(to, SC[:, 8 + d, (s - 2) * 128:(s - 1) * 128],
                                                          gs[:, 1, d, prev:prev + 1], own, ALU.mult, ALU.add)
                    link(last)
                for s in range(1, NC):
                    for d in range(2):
                        c = (s, (1, 0, 3, 2)[s])[d]
                        last = V.tensor_scalar(SC[:, d, (s - 1) * 128:s * 128], SC[:, 8 + d, (s - 1) * 128:s * 128],
                                               gs[:, 0, d, c:c + 1], None, ALU.mult)
                last.then_inc(sem("gla_S"), 1)
                split(2)
                dve.wait_ge(sem("gla_silu"), t + 1)
                for a in range(2):
                    dve.wait_ge(sem("gla_orn"), 2 * t + a + 1)
                    link(V.scalar_tensor_tensor(SC[:, 6 + a, lo:], SC[:, 6 + a, lo:], P(l, P_GLAN),
                                                SC[:, 8 + a, lo:], ALU.mult, ALU.mult))
                link(V.tensor_tensor(SC[:, 4:6, lo:], SC[:, 6:8, lo:], SC[:, 16:18, lo:], ALU.mult))
                for a in range(2):
                    last = split_y(act[:, i * 2 + (Y_GLA + a), :], SC[:, 4 + a, lo:], lo)
                last.then_inc(sem("gla_y"), 1)
                dve.wait_ge(sem("gla_y"), t + 1)

            def swa(i, t, l, lo, blocks, split):
                nb = len(blocks)
                before = i * 2 * nb + swa_blocks(l)
                split(-1)
                dve.wait_ge(sem("swa_stat"), t + 1)
                dve.wait_ge(sem("swa_rot"), t + 1)
                V.tensor_scalar(SC[:, 22:24, lo:], act[:, bass.ds(i * 2 + Y_SWA, 2), lo:], CLAMP, None, ALU.max)\
                    .then_inc(sem("swa_gc"), 1)
                sin2 = con[:, C_SIN:C_SIN + SEQ]
                V.tensor_tensor(SC[:, 20:22, 0:SEQ], ps[2][:, :].rearrange("p (a t) -> p a t", a=2),
                                over(sin2, 2), ALU.mult)
                V.tensor_tensor(SC[:, 4, 0:SEQ], ps[3][:, 0:SEQ], sin2, ALU.mult)
                link(V.tensor_tensor(SC[:, 0:3, CTX:], SC[:, 0:3, CTX:], over(con[:, C_COS:C_COS + SEQ], 3), ALU.mult))
                V.tensor_tensor(SC[:, 0:2, CTX:], SC[:, 0:2, CTX:], SC[:, 20:22, 0:SEQ], ALU.add)
                V.tensor_tensor(SC[:, 2, CTX:], SC[:, 2, CTX:], SC[:, 4, 0:SEQ], ALU.add)\
                    .then_inc(sem("swa_rope"), 1)
                for j in range(2 * nb):
                    b = blocks[j % nb]
                    n = TOK if b >= 2 else CTX
                    dve.wait_ge(sem("swa_s"), before + (j + 1))
                    last = V.tensor_copy(SC[:, 6 + j, 0:CTX], ps[5 + j % 2][:, 0:CTX])
                    if b >= 2:
                        mk = C_MASK + (b - 2) * SEQ
                        last = V.tensor_tensor(SC[:, 6 + j, CTX:], ps[5 + j % 2][:, CTX:], con[:, mk:mk + SEQ],
                                               ALU.add)
                    last.then_inc(sem("swa_sc"), 1)
                dve.wait_ge(sem("swa_sc"), before + 2 * nb)
                split(0)
                for j in range(2 * nb):
                    n = TOK if blocks[j % nb] >= 2 else CTX
                    last = V.tensor_reduce(sm[:, 0, j:j + 1], SC[:, 6 + j, 0:n], AX, ALU.max)
                link(last)
                for a in range(2):
                    last = V.tensor_scalar(sm[:, 1, a * nb:(a + 1) * nb], sm[:, 0, a * nb:(a + 1) * nb], HD ** -0.5,
                                           par[:, bass.ds(i * 2 + (l * PL + P_SINK + a), 1)], ALU.mult, ALU.max)
                link(last)
                V.tensor_scalar(sm[:, 1, 0:2 * nb], sm[:, 1, 0:2 * nb], -1.0, None, ALU.mult)\
                    .then_inc(sem("swa_m"), 1)
                split(1)
                dve.wait_ge(sem("swa_e"), t + 1)
                link(V.tensor_tensor(sm[:, 4, 0:2 * nb], sm[:, 2, 0:2 * nb], sm[:, 3, 0:2 * nb], ALU.add))
                link(V.reciprocal(sm[:, 5, 0:2 * nb], sm[:, 4, 0:2 * nb]))
                for j in range(2 * nb):
                    n = TOK if blocks[j % nb] >= 2 else CTX
                    V.tensor_scalar(SC[:, 6 + j, 0:n], SC[:, 6 + j, 0:n], sm[:, 5, j:j + 1], None, ALU.mult)\
                        .then_inc(sem("swa_p"), 1)
                split(2)
                split(3)
                dve.wait_ge(sem("swa_silu"), t + 1)
                for a in range(2):
                    dve.wait_ge(sem("swa_o"), 2 * t + a + 1)
                    link(V.tensor_tensor(SC[:, a, lo:], ps[(4, 7)[a]][:, lo:], SC[:, 22 + a, lo:], ALU.mult))
                    last = split_y(act[:, i * 2 + (Y_SWA + a), :], SC[:, a, lo:], lo)
                last.then_inc(sem("swa_y"), 1)
                dve.wait_ge(sem("swa_y"), t + 1)
                split(4)

            def shortconv(l, lo, split):
                s0 = lo // 256

                def wcol(j, tap):
                    return P(l, P_SCW + 3 * j + tap)

                def tap(dst, src, wc, sh):
                    d, s = two(dst)[:, s0:, :], two(src)[:, s0:, :]
                    a, b = max(0, -sh), SEQ - max(0, sh)
                    return V.scalar_tensor_tensor(d[:, :, a:b], s[:, :, a + sh:b + sh], wc, d[:, :, a:b],
                                                  ALU.mult, ALU.add)

                def finish(j):
                    dve.wait_ge(sem("sc_gs"), 4 * l + j + 1)
                    link(V.tensor_tensor(SC[:, 4 + j, lo:], SC[:, 4 + j, lo:], SC[:, 8 + j, lo:], ALU.mult))
                    split_y(act[:, Y_SC + j, :], SC[:, 4 + j, lo:], lo).then_inc(sem("sc_y"), 1)
                link(V.tensor_tensor(SC[:, 0:4, lo:], act[:, 12:16, lo:], act[:, 16:20, lo:], ALU.mult))
                split(0)
                for j in range(4):
                    last = V.tensor_scalar(SC[:, 4 + j, lo:], SC[:, j, lo:], wcol(j, 1), None, ALU.mult)
                link(last)
                for k, sh in ((0, -1), (2, 1)):
                    for j in range(4):
                        last = tap(SC[:, 4 + j, :], SC[:, j, :], wcol(j, k), sh)
                    link(last)
                link(V.tensor_tensor(SC[:, 4:8, lo:], SC[:, 4:8, lo:], act[:, 8:12, lo:], ALU.mult))
                for j in range(4):
                    if j:
                        split(j)
                    n = segs[(l, "p4")][1] + 12 + j
                    dve.wait_ge(sem(f"bank{n % 2}_free"), n // 2 + 1)
                    V.tensor_scalar(SC[:, 8 + j, lo:], act[:, Y_SC + j, lo:], CLAMP, None, ALU.max)\
                        .then_inc(sem("sc_gc"), 1)
                    link(V.tensor_tensor(SC[:, 4 + j, lo:], SC[:, 4 + j, lo:], act[:, Y_SC + j, lo:], ALU.mult))
                    if j:
                        finish(j - 1)
                finish(3)
                dve.wait_ge(sem("sc_y"), 4 * l + 4)

            dve.sem_inc(sem("gdn_y"), 1)
            modulation(0)
            prenorm(0, 0)
            for l in range(DEPTH):
                lo = 0 if l == 0 else CTX
                wt = segs[(l, "gdn")][0]
                for s in range(2):
                    dve.wait_ge(sem(f"slot{2 + s}_free"), 12 * (l + 1) + 1)
                    split_tile(s, 16 * (wt // 2 + 1))
                o.straight()
                gdn_projection(l, lo)
                gate_modulation(l)
                o.straight()
                full = segs[(l, "p2")][1] // 2
                dve.wait_ge(sem("bank0_free"), full)
                dve.wait_ge(sem("bank1_free"), full)
                dve.wait_ge(sem("gdn_eg"), l + 1)
                for rounds, first in GDN_LOOPS[l]:
                    with dve.Fori(0, rounds) as i:
                        o.round(i, GDN_DVE)
                        gdn(i + first, i + (4 * l + first), l, lo, splitter(l, "p2", 4, i, 4 * first))
                    o.close(rounds)
                full = (segs[(l, "p3")][1]) // 2
                dve.wait_ge(sem("bank0_free"), full)
                dve.wait_ge(sem("bank1_free"), full)
                with dve.Fori(0, 2) as i:
                    o.round(i, GLA_DVE)
                    gla(i, i + 2 * l, l, lo, splitter(l, "p3", 4, i))
                o.close(2)
                blocks = list(range(4)) if l == 0 else [2, 3]
                with dve.Fori(0, 2) as i:
                    o.round(i, SWA_DVE)
                    swa(i, i + 2 * l, l, lo, blocks, splitter(l, "p4", 6, i))
                o.close(2)
                full = (segs[(l, "p4")][1] + 12) // 2
                dve.wait_ge(sem("bank0_free"), full)
                dve.wait_ge(sem("bank1_free"), full)
                split = splitter(l, "p4", 4, 0, 12)
                split(-1)
                shortconv(l, lo, split)
                if l == 0:
                    pad_cs()
                o.straight()
                with dve.Fori(0, 3) as i:
                    o.round(i, 4)
                    split = splitter(l, "out", 4, i)
                    for j in range(4):
                        split(j)
                o.close(3)
                split = splitter(l, "out", 4, 0, 12)
                for j in range(2):
                    split(j)
                o.straight()
                dve.wait_ge(sem("rstd_ready"), 2 * l + 2)
                n = segs[(l, "out")][1] + 16
                dve.wait_ge(sem("bank0_free"), n // 2)
                dve.wait_ge(sem("bank1_free"), n // 2)
                with dve.Fori(0, KT) as k:
                    for hf in range(l, 2):
                        s = slice(hf * 256, hf * 256 + 256)
                        last = V.scalar_tensor_tensor(act[:, k, s], act[:, k, s],
                                                      modG[:, l, k, hf:hf + 1], SC[:, 3, s], ALU.mult, ALU.mult)
                    last.then_inc(sem("yo_scaled"), 1)
                dve.wait_ge(sem("yo_scaled"), KT * (l + 1))
                dve.sem_inc(sem("rstd_used"), 1)
                if l == 0:
                    modulation(1)
                    prenorm(1, 2)

        @block.gpsimd
        def _(pool):
            G = nc.gpsimd
            o = Order(pool, sem("pool_order"))

            def link(ins):
                o.done(ins)
                o.wait()
            G.memset(wdec[:, :, :], 0.0).then_inc(sem("wdec_zero"), 1)
            link(G.memset(g[:, 4, :, :], 0.0))
            pool.wait_ge(sem("con_in"), 16)

            def square_sum(lo):
                for k in range(KT):
                    if k == 0:
                        link(G.tensor_tensor(SC[:, 0, lo:], N[:, 0, lo:], N[:, 0, lo:], ALU.mult))
                    else:
                        link(G.tensor_tensor(SC[:, 1, lo:], N[:, k, lo:], N[:, k, lo:], ALU.mult))
                        link(G.tensor_tensor(SC[:, 0, lo:], SC[:, 0, lo:], SC[:, 1, lo:], ALU.add))
                pool.sem_inc(sem("sumsq_ready"), 1)

            pool.wait_ge(sem("bank0_free"), 8)
            pool.wait_ge(sem("bank1_free"), 8)
            pool.sem_inc(sem("h_ready"), 1)
            square_sum(0)

            def decays(i):
                rg = SC[:, 16:18, :].rearrange("p d (c t) -> p d c t", t=128)
                for d in range(2):
                    last = G.tensor_tensor(rg[:, d], over(cm(CUM[d])), along(g[:, i, d, :]), ALU.mult)
                last.then_inc(sem("gdn_rg"), 1)

            def gdn(i, t, l, lo):
                pool.wait_ge(sem("gdn_y"), t + 1)
                pool.wait_ge(sem("gdn_E"), t + 1)
                strict = (C_TAILB, C_TAILF)
                for d in range(2):
                    G.tensor_tensor(chunks(SC[:, 22 + d, :]), chunks(SC[:, 20 + d, :]), over(cm(strict[d])), ALU.mult)
                for d in range(2):
                    last = G.tensor_tensor(chunks(SC[:, 20 + d, :]), chunks(SC[:, 20 + d, :]), over(cm(CUM[d])),
                                           ALU.mult)
                last.then_inc(sem("gdn_Em"), 1)
                pool.wait_ge(sem("gdn_rn"), t + 1)
                G.tensor_tensor(ks[:, 0, :, :], beta[:, i, :, :], over(rn[:, 1, :], 2), ALU.mult)
                G.tensor_copy(tot[:, :, :], eg[:, :, 2, i, :])
                link(G.tensor_scalar(rq[:, :], rn[:, 0, :], HD ** -0.5, None, ALU.mult))
                G.tensor_tensor(ks[:, 1, :, :], eg[:, :, 0, i, :], over(rq[:, :], 2), ALU.mult)
                G.tensor_tensor(ks[:, 2, :, :], eg[:, :, 1, i, :], over(rn[:, 1, :], 2), ALU.mult)
                G.tensor_tensor(ks[:, 3, :, :], beta[:, i, :, :], eg[:, :, 0, i, :], ALU.mult)\
                    .then_inc(sem("gdn_ks"), 1)
                pool.wait_ge(sem("gdn_ks"), t + 1)
                pool.wait_ge(sem("gdn_tokc"), t + 1)
                for d in range(2):
                    last = G.tensor_tensor(chunks(SC[:, d, :]), chunks(SC[:, 3, :]), along(ks[:, 1, d, :]), ALU.mult)
                last.then_inc(sem("gdn_sc"), 1)
                level0 = (C_UP, C_LO)
                pool.wait_ge(sem("gdn_T1"), 4 * t + 4)
                for d in range(2):
                    pool.wait_ge(sem("gdn_U"), 2 * t + d + 1)
                    link(G.tensor_tensor(chunks(SC[:, 8 + d, :]), chunks(SC[:, 22 + d, :]), over(cm(level0[d])),
                                         ALU.mult))
                    G.tensor_tensor(chunks(SC[:, 8 + d, :]), over(ident), chunks(SC[:, 8 + d, :]), ALU.subtract)\
                        .then_inc(sem("gdn_M0"), 1)
                pool.wait_ge(sem("gdn_gs"), t + 1)
                G.tensor_tensor(SC[:, 2, lo:], SC[:, 2, lo:], act[:, i + Y_GDN, lo:], ALU.mult)\
                    .then_inc(sem("gdn_silu"), 1)
                for d in range(2):
                    G.tensor_tensor(chunks(SC[:, 12 + d, :]), chunks(SC[:, 5, :]), along(beta[:, i, d, :]), ALU.mult)
                    last = G.tensor_tensor(chunks(SC[:, 10 + d, :]), chunks(SC[:, 4, :]), along(ks[:, 2, d, :]),
                                           ALU.mult)
                last.then_inc(sem("gdn_vk"), 1)
                pool.wait_ge(sem("gdn_YT"), 12 * t + 12)
                decays(i + 1)

            for l in range(DEPTH):
                lo = 0 if l == 0 else CTX
                pool.wait_ge(sem("gdn_g"), l + 1)
                decays(0)
                pool.wait_ge(sem("beta_ready"), l + 1)
                pool.wait_ge(sem("gdn_eg"), l + 1)
                o.straight()
                for rounds, first in GDN_LOOPS[l]:
                    with pool.Fori(0, rounds) as i:
                        o.round(i, GDN_POOL)
                        gdn(i + first, i + (4 * l + first), l, lo)
                    o.close(rounds)
                pool.wait_ge(sem("gdn_y"), 4 * l + 5)
                pool.wait_ge(sem("gdn_rg"), 5 * l + 5)
                n = segs[(l, "p3")][1]
                pool.wait_ge(sem("bank0_free"), n // 2)
                pool.wait_ge(sem("bank1_free"), n // 2)
                pool.wait_ge(sem("wdec_in"), 32 * (l + 1))
                with pool.Fori(0, 2) as i:
                    t = i + 2 * l
                    G.tensor_copy(wdp, wdec[:, :, bass.ds(i * 128, 128)]).then_inc(sem("gla_wd"), 1)
                    G.tensor_copy(SC[:, 16:18, :], act[:, bass.ds(i * 2 + (T_B + 4), 2), :]).then_inc(sem("gla_stat"), 1)
                    pool.wait_ge(sem("gla_ek"), t + 1)
                    for d in range(2):
                        last = G.tensor_tensor(SC[:, 12 + d, :], act[:, i + (T_B + 2), :], SC[:, 8 + d, :], ALU.mult)
                    last.then_inc(sem("gla_kd"), 1)
                    pool.wait_ge(sem("gla_gsig"), t + 1)
                    G.tensor_tensor(SC[:, 16:18, lo:], SC[:, 16:18, lo:], act[:, bass.ds(i * 2 + Y_GLA, 2), lo:],
                                    ALU.mult).then_inc(sem("gla_silu"), 1)
                    pool.wait_ge(sem("gla_y"), t + 1)
                n = segs[(l, "p4")][1]
                pool.wait_ge(sem("bank0_free"), n // 2)
                pool.wait_ge(sem("bank1_free"), n // 2)
                with pool.Fori(0, 2) as i:
                    t = i + 2 * l
                    G.tensor_copy(SC[:, 0:2, :], act[:, bass.ds(i * 2, 2), :])
                    G.tensor_copy(SC[:, 2, :], act[:, i + 4, :])
                    G.tensor_copy(SC[:, 3, :], act[:, i + 6, :]).then_inc(sem("swa_stat"), 1)
                    pool.wait_ge(sem("swa_gs"), t + 1)
                    G.tensor_tensor(SC[:, 22:24, lo:], SC[:, 22:24, lo:], act[:, bass.ds(i * 2 + Y_SWA, 2), lo:],
                                    ALU.mult).then_inc(sem("swa_silu"), 1)
                    pool.wait_ge(sem("swa_y"), t + 1)
                pool.wait_ge(sem("sc_y"), 4 * l + 4)
                link(G.memset(SC[:, 0, lo:], 0.0))
                if l == 0:
                    pool.sem_inc(sem("yo_round"), 1)
                n = segs[(l, "out")][1]
                o.straight()
                with pool.Fori(0, 4) as i:
                    for tt in range(4):
                        b = (n + tt) % 2
                        pool.wait_ge(sem(f"bank{b}_free"), i * 2 + ((n + tt) // 2 + 1))
                        G.tensor_tensor(SC[:, 0, lo:], SC[:, 0, lo:], SC[:, 4 + tt % 2, lo:], ALU.add)\
                            .then_inc(sem("yo_add"), 1)
                        pool.wait_ge(sem("yo_add"), i * 4 + (16 * l + tt + 1))
                    pool.sem_inc(sem("yo_round"), 1)
                pool.sem_inc(sem("sumsq_ready"), 1)
                pool.wait_ge(sem("h_back"), 16 * (l + 1))
                with pool.Fori(0, KT) as k:
                    pool.wait_ge(sem("yo_scaled"), k + (KT * l + 1))
                    G.tensor_tensor(N[:, k, lo:], N[:, k, lo:], act[:, k, lo:], ALU.add).then_inc(sem("h_add"), 1)
                pool.wait_ge(sem("h_add"), KT * (l + 1))
                pool.sem_inc(sem("yo_used"), 1)
                pool.sem_inc(sem("h_ready"), 1)
                if l == 0:
                    pool.wait_ge(sem("chansum_done"), 2)
                    square_sum(0)


GDN_LOOPS = (((4, 0),), ((2, 0), (2, 2)))
ADA_NORM, ADA_GATE = (8, 0), (4, 8)
K_ORDER = list(range(8)) + list(range(12, 16)) + list(range(8, 12))


def swa_blocks(l):
    return l * 2 * 2 * 4


CONV_ACT, GDN_ACT, GLA_ACT, SWA_ACT = 8, 5, 5, 2
CONV_DVE = 28
GDN_DVE = 9
GLA_DVE = 16
SWA_DVE = 15
GDN_POOL = 3


def kernel(**inputs):
    import concourse.bacc as bacc
    from concourse.bass_utils import run_bass_kernel_spmd

    nc = bacc.Bacc("TRN2", target_bir_lowering=False, num_devices=1)
    f32 = mybir.dt.float32
    arrays = {
        "x": np.asarray(inputs["x"]).reshape(SEQ, D),
        "ctx": np.asarray(inputs["ctx"]).reshape(CTX, D),
        "ada_w": np.asarray(inputs["ada_w"]),
        "w_in": np.asarray(inputs["w_in"]),
        "w_out": np.asarray(inputs["w_out"]),
        "w_decay": np.asarray(inputs["gla_w_decay"]),
        "params": parameters(inputs),
        "consts": constants(),
    }
    args = [nc.dram_tensor(n, a.shape, f32, kind="ExternalInput").ap() for n, a in arrays.items()]
    out = nc.dram_tensor("out", (SEQ, D), f32, kind="ExternalOutput").ap()
    build(nc, *args, out)
    r = run_bass_kernel_spmd(nc, [arrays], core_ids=[0])
    return r.results[0]["out"].reshape(1, SEQ, D)
```
